# Optimizing a Trainium2 kernel written in Bass

```python
import math
import jax
import jax.numpy as jnp
from jax import lax
import numpy as np

D_MODEL = 1024
BATCH = 1
SEQ = 512
DEPTH = 2

GRID_W = 64
CTX_LEN = 256
EPS = 1e-6
N_MOD = 6
F32 = jnp.float32

SSD_HEADS = 8
SSD_HEAD_DIM = 64
SSD_INNER = SSD_HEADS * SSD_HEAD_DIM
SSD_GROUPS = 2
SSD_STATE = 64
SSD_CONV_W = 3
SSD_CHUNK = 128
SSD_CONV_DIM = SSD_INNER + 2 * SSD_GROUPS * SSD_STATE

DIFF_HEADS = 4
DIFF_QK_DIM = 32
DIFF_V_DIM = 2 * DIFF_QK_DIM
DIFF_INNER = DIFF_HEADS * DIFF_V_DIM

MLA_HEADS = 4
MLA_Q_LORA = 192
MLA_KV_LORA = 128
MLA_NOPE = 64
MLA_ROPE = 32
MLA_V = 64
MLA_INNER = MLA_HEADS * MLA_V

MIX_WIDTH = SSD_INNER + DIFF_INNER + MLA_INNER

SSD_COLS = 2 * SSD_INNER + 2 * SSD_GROUPS * SSD_STATE + 2 * SSD_HEADS
DIFF_COLS = 3 * DIFF_HEADS * DIFF_V_DIM
MLA_COLS = MLA_Q_LORA + MLA_KV_LORA + MLA_ROPE
IN_COLS = SSD_COLS + DIFF_COLS + MLA_COLS

N_EXPERTS = 16
EC_CAPACITY = 2
EXPERT_FF = 1024

ROPE_BASE = 10000.0
Q_BLOCK = 128

kernel_name = 'hybrid_ssd_diffattn_mla_ecmoe_dit'

def rmsnorm(x, w):
    xf = x.astype(F32)
    y = xf * lax.rsqrt(jnp.mean(xf * xf, axis=-1, keepdims=True) + EPS)
    return (y * w.astype(F32)).astype(x.dtype)

def modulate(x, shift, scale):
    return x * (1 + scale) + shift

def rope_2d(x, rows, cols):
    half = x.shape[-1] // 2
    quarter = half // 2
    inv = ROPE_BASE ** (-jnp.arange(quarter, dtype=F32) / quarter)

    def rot(xh, pos):
        ang = pos[:, None] * inv[None, :]
        cos = jnp.cos(ang)[None, :, None, :].astype(x.dtype)
        sin = jnp.sin(ang)[None, :, None, :].astype(x.dtype)
        x1, x2 = xh[..., :quarter], xh[..., quarter:]
        return jnp.concatenate([x1 * cos - x2 * sin, x1 * sin + x2 * cos], axis=-1)

    return jnp.concatenate([rot(x[..., :half], rows), rot(x[..., half:], cols)], axis=-1)

def over_query_blocks(fn, *qs):
    b, s = qs[0].shape[:2]
    nb = s // Q_BLOCK
    blocks = tuple(jnp.moveaxis(q.reshape((b, nb, Q_BLOCK) + q.shape[2:]), 1, 0) for q in qs)
    out = lax.map(lambda blk: fn(*blk), blocks)
    out = jnp.moveaxis(out, 0, 1)
    return out.reshape((b, s) + out.shape[3:])

def softmax_attend(q, k, v, scale):
    s = jnp.einsum('bqhd,bkhd->bhqk', q, k).astype(F32) * scale
    p = jax.nn.softmax(s, axis=-1)
    return jnp.einsum('bhqk,bkhd->bqhd', p.astype(v.dtype), v)

def centred_dwconv(u, w, b):
    k = w.shape[0]
    out = lax.conv_general_dilated(u, w[:, None, :].astype(u.dtype), window_strides=(1,),
                                   padding=[((k - 1) // 2, (k - 1) // 2)],
                                   dimension_numbers=('NWC', 'WIO', 'NWC'),
                                   feature_group_count=u.shape[-1])
    return out + b

def ssd_scan(xs, dt, a, bm, cm, h0, with_output):
    b, L, H, P = xs.shape
    G, N = bm.shape[2], bm.shape[3]
    rep = H // G
    Q = SSD_CHUNK
    nc = L // Q
    bh = jnp.repeat(bm, rep, axis=2).reshape(b, nc, Q, H, N)
    ch = jnp.repeat(cm, rep, axis=2).reshape(b, nc, Q, H, N)
    xdt = (xs * dt[..., None]).reshape(b, nc, Q, H, P)
    acum = jnp.cumsum((dt * a).reshape(b, nc, Q, H), axis=2)
    a_last = acum[:, :, -1]
    states = jnp.einsum('bcqhn,bcqh,bcqhp->bchpn', bh, jnp.exp(a_last[:, :, None] - acum), xdt)

    def step(h, inp):
        s, al = inp
        return jnp.exp(al)[..., None, None] * h + s, h

    h_final, h_prev = lax.scan(step, h0, (jnp.moveaxis(states, 1, 0), jnp.moveaxis(a_last, 1, 0)))
    if not with_output:
        return None, h_final
    h_prev = jnp.moveaxis(h_prev, 0, 1)
    seg = acum[:, :, :, None, :] - acum[:, :, None, :, :]
    lower = jnp.tril(jnp.ones((Q, Q), bool))[None, None, :, :, None]
    decay = jnp.exp(jnp.where(lower, seg, -jnp.inf))
    cb = jnp.einsum('bcihn,bcjhn->bcijh', ch, bh)
    y_diag = jnp.einsum('bcijh,bcjhp->bcihp', cb * decay, xdt)
    y_off = jnp.einsum('bcihn,bchpn->bcihp', ch * jnp.exp(acum)[..., None], h_prev)
    return (y_diag + y_off).reshape(b, L, H, P), h_final

def ssd_mixer(p_ctx, p_lat, conv_w, conv_b, a_log, dt_bias, d_skip, norm_w, ctx_out):
    def prep(p):
        b, L, _ = p.shape
        z, xbc, dt = jnp.split(p, [SSD_INNER, SSD_INNER + SSD_CONV_DIM], axis=-1)
        xbc = jax.nn.silu(centred_dwconv(xbc, conv_w, conv_b))
        xs, bm, cm = jnp.split(xbc, [SSD_INNER, SSD_INNER + SSD_GROUPS * SSD_STATE], axis=-1)
        xs = xs.reshape(b, L, SSD_HEADS, SSD_HEAD_DIM).astype(F32)
        bm = bm.reshape(b, L, SSD_GROUPS, SSD_STATE).astype(F32)
        cm = cm.reshape(b, L, SSD_GROUPS, SSD_STATE).astype(F32)
        dt = dt.reshape(b, L, 2, SSD_HEADS).astype(F32)
        return z, xs, bm, cm, dt

    zc, xc, bc, cc, dtc = prep(p_ctx)
    zl, xl, bl, cl, dtl = prep(p_lat)
    b = p_lat.shape[0]
    dsk = d_skip.astype(F32)[:, None]
    y_lat = dsk * xl
    y_ctx = dsk * xc if ctx_out else None
    for direction in range(2):
        a = -jnp.exp(a_log[direction].astype(F32))
        bias = dt_bias[direction].astype(F32)
        flip = (lambda t: jnp.flip(t, axis=1)) if direction == 1 else (lambda t: t)
        h0 = jnp.zeros((b, SSD_HEADS, SSD_HEAD_DIM, SSD_STATE), F32)
        yc, hc = ssd_scan(flip(xc), jax.nn.softplus(flip(dtc[:, :, direction]) + bias), a,
                          flip(bc), flip(cc), h0, ctx_out)
        yl, _ = ssd_scan(flip(xl), jax.nn.softplus(flip(dtl[:, :, direction]) + bias), a,
                         flip(bl), flip(cl), hc, True)
        y_lat = y_lat + flip(yl)
        if ctx_out:
            y_ctx = y_ctx + flip(yc)

    def gate_norm(y, z):
        bb, L = y.shape[:2]
        g = y.reshape(bb, L, SSD_INNER).astype(z.dtype) * jax.nn.silu(z)
        g = g.reshape(bb, L, SSD_GROUPS, SSD_INNER // SSD_GROUPS)
        return rmsnorm(g, norm_w.reshape(SSD_GROUPS, SSD_INNER // SSD_GROUPS)).reshape(bb, L, SSD_INNER)

    out_l = gate_norm(y_lat, zl)
    out_c = gate_norm(y_ctx, zc) if ctx_out else None
    return out_l, out_c

def diff_attn_mixer(p_ctx, p_lat, lam_q1, lam_k1, lam_q2, lam_k2, subln_w, lambda_init, rows, cols, ctx_out):
    lam = (jnp.exp(jnp.sum(lam_q1.astype(F32) * lam_k1.astype(F32)))
           - jnp.exp(jnp.sum(lam_q2.astype(F32) * lam_k2.astype(F32))) + lambda_init)
    scale = DIFF_QK_DIM ** -0.5

    def split(p):
        b, L, _ = p.shape
        q, k, v = jnp.split(p, 3, axis=-1)
        q = q.reshape(b, L, DIFF_HEADS, 2, DIFF_QK_DIM)
        k = k.reshape(b, L, DIFF_HEADS, 2, DIFF_QK_DIM)
        v = v.reshape(b, L, DIFF_HEADS, DIFF_V_DIM)
        return q[..., 0, :], q[..., 1, :], k[..., 0, :], k[..., 1, :], v

    def diff_attend(q1, q2, k1, k2, v):
        s1 = jnp.einsum('bqhd,bkhd->bhqk', q1, k1).astype(F32) * scale
        s2 = jnp.einsum('bqhd,bkhd->bhqk', q2, k2).astype(F32) * scale
        amap = jax.nn.softmax(s1, axis=-1) - lam * jax.nn.softmax(s2, axis=-1)
        o = jnp.einsum('bhqk,bkhd->bqhd', amap.astype(v.dtype), v)
        return rmsnorm(o, subln_w) * (1.0 - lambda_init)

    q1c, q2c, k1c, k2c, vc = split(p_ctx)
    q1l, q2l, k1l, k2l, vl = split(p_lat)
    rp = lambda t: rope_2d(t, rows, cols)
    k1 = jnp.concatenate([k1c, rp(k1l)], axis=1)
    k2 = jnp.concatenate([k2c, rp(k2l)], axis=1)
    v = jnp.concatenate([vc, vl], axis=1)
    b, L = p_lat.shape[:2]
    out_l = over_query_blocks(lambda a1, a2: diff_attend(a1, a2, k1, k2, v), rp(q1l), rp(q2l))
    out_l = out_l.reshape(b, L, DIFF_INNER)
    out_c = None
    if ctx_out:
        out_c = diff_attend(q1c, q2c, k1c, k2c, vc).reshape(b, p_ctx.shape[1], DIFF_INNER)
    return out_l, out_c

def mla_mixer(p_ctx, p_lat, q_norm_w, w_q_up, kv_norm_w, w_kv_up, rows, cols, ctx_out):
    scale = (MLA_NOPE + MLA_ROPE) ** -0.5

    def project(p):
        b, L, _ = p.shape
        cq, ckv, k_rope = jnp.split(p, [MLA_Q_LORA, MLA_Q_LORA + MLA_KV_LORA], axis=-1)
        q = (rmsnorm(cq, q_norm_w) @ w_q_up).reshape(b, L, MLA_HEADS, MLA_NOPE + MLA_ROPE)
        kv = (rmsnorm(ckv, kv_norm_w) @ w_kv_up).reshape(b, L, MLA_HEADS, MLA_NOPE + MLA_V)
        return q[..., :MLA_NOPE], q[..., MLA_NOPE:], kv[..., :MLA_NOPE], k_rope[:, :, None, :], kv[..., MLA_NOPE:]

    def join_keys(k_nope, k_rope):
        return jnp.concatenate([k_nope, jnp.broadcast_to(k_rope, k_nope.shape[:-1] + (MLA_ROPE,))], axis=-1)

    qn_c, qr_c, kn_c, kr_c, v_c = project(p_ctx)
    qn_l, qr_l, kn_l, kr_l, v_l = project(p_lat)
    k_c = join_keys(kn_c, kr_c)
    k_all = jnp.concatenate([k_c, join_keys(kn_l, rope_2d(kr_l, rows, cols))], axis=1)
    v_all = jnp.concatenate([v_c, v_l], axis=1)
    q_l = jnp.concatenate([qn_l, rope_2d(qr_l, rows, cols)], axis=-1)
    b, L = p_lat.shape[:2]
    out_l = over_query_blocks(lambda qb: softmax_attend(qb, k_all, v_all, scale), q_l).reshape(b, L, MLA_INNER)
    out_c = None
    if ctx_out:
        q_c = jnp.concatenate([qn_c, qr_c], axis=-1)
        out_c = softmax_attend(q_c, k_c, v_c, scale).reshape(b, p_ctx.shape[1], MLA_INNER)
    return out_l, out_c

def mix_heads(h_ctx, h_lat, w_in, w_out, conv_w, conv_b, a_log, dt_bias, d_skip, ssd_norm_w,
              lam_q1, lam_k1, lam_q2, lam_k2, subln_w, q_norm_w, w_q_up, kv_norm_w, w_kv_up,
              rows, cols, lambda_init, ctx_out):
    cuts = [SSD_COLS, SSD_COLS + DIFF_COLS]
    ssd_c, diff_c, mla_c = jnp.split(h_ctx @ w_in, cuts, axis=-1)
    ssd_l, diff_l, mla_l = jnp.split(h_lat @ w_in, cuts, axis=-1)
    s_l, s_c = ssd_mixer(ssd_c, ssd_l, conv_w, conv_b, a_log, dt_bias, d_skip, ssd_norm_w, ctx_out)
    d_l, d_c = diff_attn_mixer(diff_c, diff_l, lam_q1, lam_k1, lam_q2, lam_k2, subln_w, lambda_init, rows, cols, ctx_out)
    a_l, a_c = mla_mixer(mla_c, mla_l, q_norm_w, w_q_up, kv_norm_w, w_kv_up, rows, cols, ctx_out)
    out_l = jnp.concatenate([s_l, d_l, a_l], axis=-1) @ w_out
    out_c = jnp.concatenate([s_c, d_c, a_c], axis=-1) @ w_out if ctx_out else None
    return out_l, out_c

def expert_choice_ffn(h, router_w, router_b, w_gate, w_up, w_down):
    b, n, d = h.shape
    cap = EC_CAPACITY * n // N_EXPERTS
    affinity = jax.nn.softmax((h @ router_w + router_b).astype(F32), axis=-1)
    gates, idx = lax.top_k(jnp.swapaxes(affinity, 1, 2), cap)
    xg = jax.vmap(lambda hb, ib: hb[ib])(h, idx)
    hid = jax.nn.silu(jnp.einsum('becd,edf->becf', xg, w_gate)) * jnp.einsum('becd,edf->becf', xg, w_up)
    y = jnp.einsum('becf,efd->becd', hid, w_down) * gates[..., None].astype(h.dtype)
    scatter = lambda yb, ib: jnp.zeros((n, d), h.dtype).at[ib.reshape(-1)].add(yb.reshape(-1, d))
    return jax.vmap(scatter)(y, idx)

def setup_inputs(seed: int = 0) -> dict:
    key = jax.random.key(seed)
    ks = iter(jax.random.split(key, 48))
    D = D_MODEL

    def nrm(shape, s):
        return jax.random.normal(next(ks), shape, F32) * s

    def gain(shape):
        return 1.0 + nrm(shape, 0.02)

    dt0 = jnp.exp(jax.random.uniform(next(ks), (DEPTH, 2, SSD_HEADS), F32,
                                     minval=math.log(1e-3), maxval=math.log(1e-1)))
    dt_bias = dt0 + jnp.log(-jnp.expm1(-dt0))
    a_log = jnp.log(jax.random.uniform(next(ks), (DEPTH, 2, SSD_HEADS), F32, minval=1.0, maxval=16.0))
    return {
        'x': nrm((BATCH, SEQ, D), 1.0),
        'c': nrm((BATCH, D), 1.0),
        'ctx': nrm((BATCH, CTX_LEN, D), 1.0),
        'c_ctx': nrm((D,), 1.0),
        'ada_w': nrm((DEPTH, D, N_MOD * D), 0.5 * D ** -0.5),
        'ada_b': nrm((DEPTH, N_MOD * D), 0.02),
        'norm_mix_pre': gain((DEPTH, D)),
        'norm_mix_post': gain((DEPTH, D)),
        'norm_ffn_pre': gain((DEPTH, D)),
        'norm_ffn_post': gain((DEPTH, D)),
        'w_in': nrm((DEPTH, D, IN_COLS), D ** -0.5),
        'ssd_conv_w': nrm((DEPTH, SSD_CONV_W, SSD_CONV_DIM), SSD_CONV_W ** -0.5),
        'ssd_conv_b': nrm((DEPTH, SSD_CONV_DIM), 0.02),
        'ssd_a_log': a_log,
        'ssd_dt_bias': dt_bias,
        'ssd_d': gain((DEPTH, SSD_HEADS)),
        'ssd_norm': gain((DEPTH, SSD_INNER)),
        'diff_lam_q1': nrm((DEPTH, DIFF_QK_DIM), 0.1),
        'diff_lam_k1': nrm((DEPTH, DIFF_QK_DIM), 0.1),
        'diff_lam_q2': nrm((DEPTH, DIFF_QK_DIM), 0.1),
        'diff_lam_k2': nrm((DEPTH, DIFF_QK_DIM), 0.1),
        'diff_subln': gain((DEPTH, DIFF_V_DIM)),
        'mla_q_norm': gain((DEPTH, MLA_Q_LORA)),
        'mla_w_q_up': nrm((DEPTH, MLA_Q_LORA, MLA_HEADS * (MLA_NOPE + MLA_ROPE)), MLA_Q_LORA ** -0.5),
        'mla_kv_norm': gain((DEPTH, MLA_KV_LORA)),
        'mla_w_kv_up': nrm((DEPTH, MLA_KV_LORA, MLA_HEADS * (MLA_NOPE + MLA_V)), MLA_KV_LORA ** -0.5),
        'w_out': nrm((DEPTH, MIX_WIDTH, D), MIX_WIDTH ** -0.5),
        'router_w': nrm((DEPTH, D, N_EXPERTS), D ** -0.5),
        'router_b': nrm((DEPTH, N_EXPERTS), 0.01),
        'w_gate': nrm((DEPTH, N_EXPERTS, D, EXPERT_FF), D ** -0.5),
        'w_up': nrm((DEPTH, N_EXPERTS, D, EXPERT_FF), D ** -0.5),
        'w_down': nrm((DEPTH, N_EXPERTS, EXPERT_FF, D), EXPERT_FF ** -0.5),
    }

def reference(x, c, ctx, c_ctx, ada_w, ada_b, norm_mix_pre, norm_mix_post, norm_ffn_pre, norm_ffn_post,
              w_in, ssd_conv_w, ssd_conv_b, ssd_a_log, ssd_dt_bias, ssd_d, ssd_norm,
              diff_lam_q1, diff_lam_k1, diff_lam_q2, diff_lam_k2, diff_subln,
              mla_q_norm, mla_w_q_up, mla_kv_norm, mla_w_kv_up, w_out,
              router_w, router_b, w_gate, w_up, w_down):
    n_rows = x.shape[1] // GRID_W
    rows = jnp.repeat(jnp.arange(n_rows, dtype=F32), GRID_W)
    cols = jnp.tile(jnp.arange(GRID_W, dtype=F32), n_rows)
    silu_c = jax.nn.silu(c)
    silu_cc = jax.nn.silu(c_ctx)
    for l in range(DEPTH):
        ctx_out = l < DEPTH - 1
        lambda_init = 0.8 - 0.6 * math.exp(-0.3 * l)
        mod_l = jnp.split((silu_c @ ada_w[l] + ada_b[l])[:, None, :], N_MOD, axis=-1)
        mod_c = jnp.split(silu_cc @ ada_w[l] + ada_b[l], N_MOD, axis=-1)
        h_l = modulate(rmsnorm(x, norm_mix_pre[l]), mod_l[0], mod_l[1])
        h_c = modulate(rmsnorm(ctx, norm_mix_pre[l]), mod_c[0], mod_c[1])
        m_l, m_c = mix_heads(h_c, h_l, w_in[l], w_out[l], ssd_conv_w[l], ssd_conv_b[l], ssd_a_log[l],
                             ssd_dt_bias[l], ssd_d[l], ssd_norm[l], diff_lam_q1[l], diff_lam_k1[l],
                             diff_lam_q2[l], diff_lam_k2[l], diff_subln[l], mla_q_norm[l], mla_w_q_up[l],
                             mla_kv_norm[l], mla_w_kv_up[l], rows, cols, lambda_init, ctx_out)
        x = x + mod_l[2] * rmsnorm(m_l, norm_mix_post[l])
        if ctx_out:
            ctx = ctx + mod_c[2] * rmsnorm(m_c, norm_mix_post[l])
        f_l = expert_choice_ffn(modulate(rmsnorm(x, norm_ffn_pre[l]), mod_l[3], mod_l[4]),
                                router_w[l], router_b[l], w_gate[l], w_up[l], w_down[l])
        x = x + mod_l[5] * rmsnorm(f_l, norm_ffn_post[l])
        if ctx_out:
            f_c = expert_choice_ffn(modulate(rmsnorm(ctx, norm_ffn_pre[l]), mod_c[3], mod_c[4]),
                                    router_w[l], router_b[l], w_gate[l], w_up[l], w_down[l])
            ctx = ctx + mod_c[5] * rmsnorm(f_c, norm_ffn_post[l])
    return x


_drawn_inputs = setup_inputs


def setup_inputs(seed=0):
    import zlib

    import numpy as np

    out = dict(_drawn_inputs(seed))
    spreads = {}
    factors = {'norm_ffn_post': 4.275,
     'ssd_d': 5.217,
     'diff_lam_q1': 4.338,
     'diff_lam_q2': 8.0,
     'diff_lam_k2': 4.036,
     'diff_subln': 3.971,
     'mla_q_norm': 8.0,
     'mla_kv_norm': 6.078,
     'router_b': 2.67}
    for name, (base, spread) in spreads.items():
        noise = np.random.default_rng([zlib.crc32(name.encode()), seed]).standard_normal(out[name].shape)
        drawn = base * np.exp(spread * noise) if base else spread * noise
        out[name] = jnp.asarray(drawn.astype(out[name].dtype))
    for name, factor in factors.items():
        out[name] = (out[name] * factor).astype(out[name].dtype)
    return out
```

```python
import math
from contextlib import ExitStack

import numpy as np
import concourse.bass as bass
from concourse import mybir

ALU = mybir.AluOpType
ACT = mybir.ActivationFunctionType
F32 = mybir.dt.float32
U32 = mybir.dt.uint32
AX_X = mybir.AxisListType.X

P = 128
D = 1024
KD = D // P
DEPTH = 2
CTX, SEQ, GRID_W = 256, 512, 64
TOK = CTX + SEQ
NT = TOK // P
CT = CTX // P
EPS = 1e-6
SH, SP, SG, SN = 8, 64, 2, 64
HPG = SH // SG
SI = SH * SP
CONV_T = (SI + 2 * SG * SN) // P
DH, DQ, DV = 4, 32, 64
MH, MQL, MKL, MN, MR, MV = 4, 192, 128, 64, 32, 64
MQK = MN + MR
COL_Z, COL_X, COL_B = 0, SI, 2 * SI
COL_DT = COL_B + 2 * SG * SN
COL_QK = COL_DT + 2 * SH
COL_V = COL_QK + 2 * DH * DV
COL_MLA = COL_V + DH * DV
MLA_COLS = MQL + MKL + MR
NE, FF = 16, 1024
CAP_L, CAP_C = 2 * SEQ // NE, 2 * CTX // NE
BLK = 512
RING = 4
NSLOT = 4
LAYER_BLOCKS = 12 + 2 + 1 + 3 + 2 + 6 * NE
NEG = -30000.0

K_ID, K_TRU, K_TRL, K_MF, K_MB, K_ROT, K_ONE = (i * P for i in range(7))
K_COS = 7 * P
K_SIN = K_COS + SEQ
K_IOTA = K_SIN + SEQ
K_TID = K_IOTA + TOK
K_EPS = K_TID + NT
K_END = K_EPS + 1

R_ADAB, R_MPRE, R_FPRE, R_MPOST, R_FPOST = 0, 48, 56, 64, 72
R_CW, R_CB, R_QN, R_KVN, R_SN, R_SUB, R_C = 80, 98, 104, 106, 107, 111, 112
B_ALOG, B_DTB, B_DSK, B_RB, B_LAM, B_END = 0, 16, 32, 40, 56, 184


def constants():
    t = np.zeros((P, K_END), np.float32)
    j = np.arange(P)
    t[:, K_ID:K_ID + P] = np.eye(P)
    t[:, K_TRU:K_TRU + P] = j[:, None] <= j[None, :]
    t[:, K_TRL:K_TRL + P] = j[:, None] >= j[None, :]
    t[:, K_MF:K_MF + P] = np.where(j[:, None] <= j[None, :], 0.0, NEG)
    t[:, K_MB:K_MB + P] = np.where(j[:, None] >= j[None, :], 0.0, NEG)
    t[:, K_ONE:K_ONE + P] = 1.0
    q = DQ // 4
    inv = np.float32(10000.0) ** (-np.arange(q, dtype=np.float32) / np.float32(q))
    pos = np.arange(SEQ)
    for p in range(P):
        d = p % DQ
        where = (pos // GRID_W if d < DQ // 2 else pos % GRID_W).astype(np.float32)
        ang = where * inv[d % q]
        t[p, K_COS:K_COS + SEQ] = np.cos(ang)
        t[p, K_SIN:K_SIN + SEQ] = np.sin(ang)
        if (d // q) % 2 == 0:
            t[p + q, K_ROT + p] = -1.0
        else:
            t[p - q, K_ROT + p] = 1.0
    t[:, K_IOTA:K_IOTA + TOK] = np.arange(TOK)[None, :]
    t[:, K_TID:K_TID + NT] = j[:, None] + P * np.arange(NT)[None, :]
    t[:, K_EPS] = EPS
    return t


def query_tiles(l):
    return list(range(NT)) if l < DEPTH - 1 else list(range(CT, NT))


def spans(t):
    return ((0, CTX),) if t < CT else ((0, 512), (512, TOK))


def n_keys(t):
    return (CT if t < CT else NT) * P


def chunks():
    fwd = list(range(NT))
    bwd = list(range(CT - 1, -1, -1)) + list(range(NT - 1, CT - 1, -1))
    return [(d, c, (fwd, bwd)[d][c]) for c in range(NT) for d in range(2)]


def job_plan():
    at, n = {}, 0
    for l in range(DEPTH):
        q = len(query_tiles(l))
        for name, c in [("par", 1), ("ada", 1), ("h", NT),
                        ("qk", 4), ("v", 2), ("rot", 4), ("datt", 4 * DH * q),
                        ("mla", 3), ("mlaT", 3), ("mq", MH), ("mk", MH), ("mv", 2), ("mrot", MH + 1),
                        ("matt", 3 * MH * q),
                        ("xbc", CONV_T), ("dt", 1), ("z", 3), ("xT", NT), ("cum", 1), ("ssd", 4 * q),
                        ("rec", 2 * NT), ("gm", 2), ("out", 2 * q), ("f", 2 * q), ("aT", 1), ("idx", 3),
                        ("moe", NE * (4 + q)), ("gf", 2)]:
            at[l, name] = n
            n += c
    return at


def att_job(base, maps, n, u, kind, m=0):
    def start(i):
        return base + maps + i * (maps + 1) + max(0, i - 1)
    if kind == "score":
        return base + m if u == 0 else start(u - 1) + m
    if kind == "turn":
        return start(u) + (maps if u + 1 < n else 0)
    return base + n * (maps + 2) - 1 if u == n - 1 else att_job(base, maps, n, u + 1, "turn") + 1


def two_job(base, n, i, second):
    if not second:
        return base if i == 0 else base + 2 * i - 1
    return base + (2 * n - 1 if i == n - 1 else 2 * i + 2)


def ssd_job(base, n, i, k):
    if k < 3:
        return base + k if i == 0 else base + 4 * i - 1 + k
    return base + (4 * n - 1 if i == n - 1 else 4 * i + 6)


def pair_jobs(jm, nq, i, last=False):
    first = isinstance(i, int) and i == 0
    b = jm + 1 if first else jm + 9 + nq
    turn = 0 if first else (i - 1) * ((8 + 2 * nq) // NSLOT)
    out = []
    for p in range(2):
        o = {"gate": b, "up": b + 1, "scatter": b + 2}
        b += 2 + (0 if first and p == 0 else nq)
        o["gather"] = b
        b += 0 if last and p == 1 else 1
        o["down"] = b
        b += 1
        out.append(o)
    return out, turn, b


class Slots:

    def __init__(self, ps, s_full, s_free, first):
        self.ps, self.s_full, self.s_free, self.first = ps, s_full, s_free, first

    def tile(self, j):
        return self.ps[j % NSLOT]

    def fill(self, j):
        return self.s_full[j % NSLOT], 1

    def free(self, j):
        return self.s_free[j % NSLOT], 1

    def filled(self, j, turn=0):
        return self.s_full[j % NSLOT], turn + (j // NSLOT + 1)

    def freed(self, j, turn=0):
        return self.s_free[j % NSLOT], turn + (j // NSLOT + 1)

    def empty(self, j, turn=0):
        return (self.s_free[j % NSLOT], turn + j // NSLOT) if j >= NSLOT else self.first


class Tally:

    def __init__(self):
        self.n = {}

    def next(self, sem, k=1):
        self.n[sem.name] = self.n.get(sem.name, 0) + k
        return sem, self.n[sem.name]


N_SMALL = 1 + NT + DEPTH * (1 + 4 + 3 + 1 + 2 + 1 + 1 + 2 + 2 + 4 + 4 + 2 + 1 + 1)


def build(nc, T, out):
    JOB = job_plan()
    with ExitStack() as ctx:
        def sb(name, cols, dt=F32):
            return ctx.enter_context(nc.sbuf_tensor(name, [P, cols], dt))

        def sem(name):
            return ctx.enter_context(nc.semaphore(name))

        ring = [sb(f"ring{i}", KD * BLK) for i in range(RING)]
        X = sb("resid", NT * D)
        K = sb("const", K_END)
        wqu = sb("w_q_up", DEPTH * 2 * MH * MQK)
        wkv = sb("w_kv_up", DEPTH * MH * (MN + MV))
        wrt = sb("w_router", DEPTH * KD * NE)
        pack = sb("pack", DEPTH * P)
        par = sb("par", DEPTH * P)
        rowp = sb("rowp", DEPTH * B_END)
        sc = sb("silu_c", 2 * KD)
        mod = sb("mod", 96)
        coef = sb("coef", 64)
        fac = sb("fac", 8)
        small = sb("small", 512)
        dummy = sb("mark", 8)
        ssum, rstd = sb("ssum", 64), sb("rstd", 64)
        nmax, esum, rcol = sb("nmax", 8), sb("esum", 8), sb("rcol", 16)
        acol = sb("acol", 16)
        lam = sb("lam", 136)
        arena_cols = 22464
        A = sb("arena", arena_cols)
        ps = [ctx.enter_context(nc.psum_tensor(f"ps{i}", [P, 1024], F32)) for i in range(NSLOT)]

        ring_full = [sem(f"ring_full{i}") for i in range(RING)]
        half_used = sem("half_used")
        s_load, s_out, s_zero = sem("small_loads"), sem("out_stored"), sem("pack_zeroed")
        J = Slots(ps, [sem(f"ps_full{i}") for i in range(NSLOT)], [sem(f"ps_free{i}") for i in range(NSLOT)],
                  (s_load, 16 * N_SMALL))
        dve_step, act_step = sem("dve_step"), sem("act_step")
        dve_ph, act_ph, pool_ph = sem("dve_phase"), sem("act_phase"), sem("pool_phase")
        S = {n: sem(n) for n in [
            "silu_ready", "xn_ready", "h_ready", "lam_dots", "lam_exps", "qk_roped", "negmax", "prob_ready",
            "o_ss", "o_rstd", "lat_ss", "lat_rstd", "lat_scaled", "kr_ready", "kr_all", "q_roped",
            "conv_mid", "conv_out", "xbc_ready", "dt_neg", "dt_exp", "dt_w", "dt_ln", "neg_a", "la_ready",
            "ac_ready", "dec_exp", "w_ready", "seg_ready", "seg_exp", "mask_ready", "xw_ready", "g_ss", "g_rstd",
            "diag_ready", "m_rstd", "router_max", "router_exp", "aff_ready", "topk_ready", "bd_ready",
            "sel_ready", "scat_ready", "xg_ready", "out_ready"]}

        def kc(c, n=P):
            return K[:, c:c + n]

        ident, ones, eps = kc(K_ID), kc(K_ONE), K[:, K_EPS:K_EPS + 1]

        def Xt(t):
            return X[:, t * D:(t + 1) * D]

        def ar(at, n):
            assert at + n <= arena_cols, (at, n)
            return A[:, at:at + n]

        def view(ap, **kw):
            (k, n), = kw.items()
            return ap.rearrange(f"p ({k} n) -> p {k} n", **{k: n})

        def spread(ap, n, axis, shape):
            return ap.unsqueeze(axis).to_broadcast(shape)

        hT = view(ar(0, KD * TOK), k=KD)
        a0 = KD * TOK
        matt = view(ar(a0, NT * 512), t=NT)
        a1 = a0 + NT * 512
        xn = [ar(a1 + i * D, D) for i in range(2)]
        junk = ar(a1 + 2 * D, D)
        QK = view(ar(a1, 4 * TOK), m=4)
        V = view(ar(a1 + 4 * TOK, NT * 256), t=NT)
        a2 = a1 + 4 * TOK + NT * 256
        rope_t = [ar(a2 + i * SEQ, SEQ) for i in range(2)]
        PD = [[ar(a2 + (2 * i + m) * TOK, TOK) for m in range(2)] for i in range(2)]
        PT_d = [ar(a2 + (4 + i) * TOK, TOK) for i in range(2)]
        osq = ar(a1, NT * 256)
        QT, KT = view(ar(a1, MH * TOK), h=MH), view(ar(a1 + MH * TOK, MH * TOK), h=MH)
        VM = view(ar(a1 + 2 * MH * TOK, NT * 256), t=NT)
        a3 = a1 + 2 * MH * TOK + NT * 256
        MT = view(ar(a3, NT * MLA_COLS), t=NT)
        msq = view(ar(a1, NT * (MQL + MKL)), t=NT)
        cq0, cq1, ckv = (ar(a3 + NT * MLA_COLS + i * TOK, TOK) for i in range(3))
        PM = [[ar(a3 + i * TOK, TOK)] for i in range(2)]
        PT_m = [ar(a3 + (2 + i) * TOK, TOK) for i in range(2)]
        mrope_t = ar(a3, SEQ)
        XB = view(ar(a1, CONV_T * TOK), m=CONV_T)
        XT = view(ar(a1 + CONV_T * TOK, NT * 640), t=NT)
        a4 = a1 + CONV_T * TOK + NT * 640
        ZS = view(ar(a4, NT * SI), t=NT)
        a5 = a4 + NT * SI
        HS = [ar(a5 + i * HPG * SP, HPG * SP) for i in range(2)]
        EA, ET = ar(a5 + 2 * HPG * SP, 96), ar(a5 + 2 * HPG * SP + 96, 96)
        Y = view(ar(0, NT * SI), t=NT)
        seg = [view(ar(NT * SI + i * 1024, 1024), h=SH) for i in range(3)]
        dts = [ar(NT * SI + 96 * i, 96) for i in range(6)]
        cbs = view(ar(a1, 256), g=SG)
        xdk = ytmp = ar(a1 + 256, SI)
        XW = [ar(a1 + 256 + SI + i * SI, SI) for i in range(2)]
        ysq = ar(a1, NT * SI)
        LA, DTV, AC, TOT, WJ = (small[:, i * 96:(i + 1) * 96] for i in range(5))
        mixT = [view(ar(a1 + i * D, D), k=KD) for i in range(2)]
        GB = [ar(a1 + (2 + i) * D, D) for i in range(2)]
        diag = [view(ar(a1 + (4 + i) * D, D), k=KD) for i in range(2)]
        rn, rn2 = ar(a1 + 6 * D, D), ar(a1 + 7 * D, D)
        htok = view(ar(0, NT * D), t=NT)
        Fa = view(ar(NT * D, NT * D), t=NT)
        fhT = [view(ar(NT * D + i * D, D), k=KD) for i in range(2)]
        fj = ar(NT * D + 2 * D, D)
        b0 = 2 * NT * D
        idxB = ar(b0, NE * 96)
        b1 = b0 + NE * 96
        xg = [ar(b1 + i * 768, 768) for i in range(2)]
        hid = [ar(b1 + (2 + i) * 768, 768) for i in range(2)]
        sg = ar(b1 + 4 * 768, 768)
        yb = [ar(b1 + 5 * 768 + i * D, D) for i in range(2)]
        b2 = b1 + 5 * 768 + 2 * D
        Sel = [ar(b2 + i * 576, 576) for i in range(2)]
        Sc = [ar(b2 + 2 * 576 + i * TOK, TOK) for i in range(2)]
        aT = [ar(b1 + i * TOK, TOK) for i in range(2)]
        bd = ar(b1, NE * 96)
        aff, ex, idu, idf, gv = (ar(b1 + 2 * TOK + i * 96, 96) for i in range(5))
        slotc = small[:, 480:512]
        GBf = [ar(b1 + i * D, D) for i in range(2)]
        diagf = [view(ar(b1 + (2 + i) * D, D), k=KD) for i in range(2)]
        rnf = ar(b1 + 4 * D, D)

        par_l = [par[:, l * P:(l + 1) * P] for l in range(DEPTH)]
        row_l = [rowp[:, l * B_END:(l + 1) * B_END] for l in range(DEPTH)]
        mod3 = mod[:, :].rearrange("p (m s) -> p m s", s=2)
        cA, cF, cGm, cGf = (coef[:, 16 * i:16 * i + 16].rearrange("p (k s) -> p k s", s=2) for i in range(4))
        LINIT = [0.8 - 0.6 * math.exp(-0.3 * l) for l in range(DEPTH)]

        def ringv(j):
            return ring[j % RING][:, :].rearrange("p (k n) -> p k n", k=KD)

        def grid(tile, ns):
            return tile[:, :].rearrange("p (b c) -> p b c", b=2)[:, :, 0:4 * ns].rearrange("p b (k n) -> p b k n", n=ns)

        def grid_sb(ap, ns):
            return ap[:, 0:8 * ns].rearrange("p (b k n) -> p b k n", b=2, k=4)

        def slots_of(l):
            return CAP_L + (CAP_C if l < DEPTH - 1 else 0)

        block = ctx.enter_context(nc.Block())

        @block.sync
        def _(sp):
            n_small = [0]

            def load(dst, src):
                sp.dma_start(dst, src).then_inc(s_load, 16)
                n_small[0] += 1

            def block_used(l, b):
                if b < 11:
                    sp.wait_ge(half_used, l * (11 + 3 * NE) + b + 1)
                    return
                n = len(query_tiles(l))
                name, k = {11: ("ada", 0), 12: ("qk", 3), 13: ("v", 1), 14: ("mla", 2), 15: ("xbc", 3),
                           16: ("dt", 0), 17: ("z", 2), 18: ("out", 2 * n - 1), 19: ("out", 2 * n - 1)}[b]
                sp.wait_ge(*J.filled(JOB[l, name] + k))

            def expert_used(l, i, k, last=False):
                p, w, hf = k // 6, k % 6 // 2, k % 2
                o, turn, _ = pair_jobs(JOB[l, "moe"], len(query_tiles(l)), i, last)
                if hf == 0:
                    sp.wait_ge(half_used, i * 6 + (l * (11 + 3 * NE) + 11 + 3 * p + w + 1))
                else:
                    sp.wait_ge(*J.filled(o[p][("gate", "up", "down")[w]], turn))

            load(K[:, :], T["const"])
            for t in range(CT):
                load(Xt(t), T["ctx"][0, t * P:(t + 1) * P, :])
            for t in range(CT, NT):
                load(Xt(t), T["x"][0, (t - CT) * P:(t - CT + 1) * P, :])
            sp.wait_ge(s_zero, 1)
            for l in range(DEPTH):
                pk = pack[:, l * P:(l + 1) * P]

                def rows(at, src, n):
                    load(pk[at:at + n, :], src.rearrange("(r c) -> r c", c=P))
                rows(R_ADAB, T["ada_b"][l], 48)
                for at, nm in ((R_MPRE, "norm_mix_pre"), (R_FPRE, "norm_ffn_pre"), (R_MPOST, "norm_mix_post"),
                               (R_FPOST, "norm_ffn_post")):
                    rows(at, T[nm][l], KD)
                for w in range(3):
                    rows(R_CW + CONV_T * w, T["ssd_conv_w"][l, w], CONV_T)
                rows(R_CB, T["ssd_conv_b"][l], CONV_T)
                rows(R_QN, T["mla_q_norm"][l, 0:P], 1)
                load(pk[R_QN + 1:R_QN + 2, 0:MQL - P], T["mla_q_norm"][l:l + 1, P:MQL])
                rows(R_KVN, T["mla_kv_norm"][l], 1)
                rows(R_SN, T["ssd_norm"][l], 4)
                for i in range(2):
                    load(pk[R_SUB:R_SUB + 1, i * DV:(i + 1) * DV], T["diff_subln"][l:l + 1, :])
                rows(R_C, T["c"][0], KD)
                rows(R_C + KD, T["c_ctx"], KD)
                rw = row_l[l]
                load(rw[:, B_ALOG:B_ALOG + 16], T["ssd_a_log"][l].rearrange("a b -> (a b)").partition_broadcast(P))
                load(rw[:, B_DTB:B_DTB + 16], T["ssd_dt_bias"][l].rearrange("a b -> (a b)").partition_broadcast(P))
                load(rw[:, B_DSK:B_DSK + 8], T["ssd_d"][l].partition_broadcast(P))
                load(rw[:, B_RB:B_RB + 16], T["router_b"][l].partition_broadcast(P))
                for i, nm in enumerate(("diff_lam_q1", "diff_lam_k1", "diff_lam_q2", "diff_lam_k2")):
                    load(rw[:, B_LAM + 32 * i:B_LAM + 32 * i + 32], T[nm][l].partition_broadcast(P))
                wq = wqu[:, l * 2 * MH * MQK:(l + 1) * 2 * MH * MQK]
                load(wq[:, 0:MH * MQK], T["mla_w_q_up"][l, 0:P, :])
                load(wq[0:MQL - P, MH * MQK:2 * MH * MQK], T["mla_w_q_up"][l, P:MQL, :])
                load(wkv[:, l * 512:(l + 1) * 512], T["mla_w_kv_up"][l])
                load(view(wrt[:, l * KD * NE:(l + 1) * KD * NE], k=KD),
                     T["router_w"][l].rearrange("(k p) n -> p k n", p=P))
            assert n_small[0] == N_SMALL, n_small[0]

            for l in range(DEPTH):
                jl = l * LAYER_BLOCKS
                aw, wi, wo = (T[n][l].rearrange("(k p) n -> p k n", p=P) for n in ("ada_w", "w_in", "w_out"))
                srcs = [aw[:, :, b * BLK:(b + 1) * BLK] for b in range(12)]
                srcs += [wi[:, :, c:c + n] for c, n in ((COL_QK, 512), (COL_V, 256), (COL_MLA, MLA_COLS), (COL_X, 512),
                                                        (COL_B, 272), (COL_Z, 512))]
                srcs += [wo[:, :, b * BLK:(b + 1) * BLK] for b in range(2)]
                for b, src in enumerate(srcs):
                    if b >= RING:
                        block_used(l, b - RING)
                    elif l:
                        expert_used(l - 1, NE // 2 - 1, 8 + b, last=True)
                    sp.dma_start(ringv(jl + b)[:, :, 0:src.shape[2]], src).then_inc(ring_full[(jl + b) % RING], 16)
                gud = [T[n].rearrange("l e (k p) n -> (l e) p k n", p=P) for n in ("w_gate", "w_up", "w_down")]

                def pair_loads(i, before):
                    for k in range(12):
                        p, w, hf = k // 6, k % 6 // 2, k % 2
                        before(k)
                        e = i * 2 + (l * NE + p)
                        src = gud[w][e] if isinstance(i, int) else gud[w][bass.ds(e, 1)][0]
                        sp.dma_start(ringv(k), src[:, :, hf * BLK:(hf + 1) * BLK]).then_inc(ring_full[k % RING], 16)

                pair_loads(0, lambda k: block_used(l, 16 + k) if k < RING else expert_used(l, 0, k - RING))
                pair_loads(1, lambda k: expert_used(l, 0, 8 + k) if k < RING else expert_used(l, 1, k - RING))
                with sp.Fori(2, NE // 2) as i:
                    pair_loads(i, lambda k: expert_used(l, i - 1, 8 + k) if k < RING else expert_used(l, i, k - RING))
            for t in range(CT, NT):
                sp.wait_ge(S["out_ready"], t - CT + 1)
                sp.dma_start(out[0, (t - CT) * P:(t - CT + 1) * P, :], Xt(t)).then_inc(s_out, 16)
            sp.wait_ge(s_out, 16 * (NT - CT))

        @block.gpsimd
        def _(pool):
            g = Tally()
            pool.memset(pack[:, :], 0.0).then_inc(s_zero, 1)

            def phase():
                pool.memset(dummy[0:1, 0:1], 0.0).then_inc(pool_ph, 1)
                for s in (pool_ph, dve_ph, act_ph):
                    pool.wait_ge(*g.next(s))

            for l in range(DEPTH):
                phase()
                phase()
                pool.wait_ge(*g.next(S["kr_ready"]))
                for h in range(1, MH):
                    pool.tensor_copy(KT[MN:MQK, h, :], KT[MN:MQK, 0, :]).then_inc(S["kr_all"], 1)
                phase()
                pool.wait_ge(*g.next(S["w_ready"]))
                pool.wait_ge(*J.freed(JOB[l, "xT"] + NT - 1))
                for n, (d, c, t) in enumerate(chunks()):
                    if n >= 2:
                        pool.wait_ge(*J.filled(JOB[l, "rec"] + n - 2))
                    w = WJ[:, t * 16 + d * 8:t * 16 + d * 8 + 8]
                    pool.tensor_tensor(view(XW[n % 2], h=SH), view(XT[:, t, 0:SI], h=SH),
                                       w.unsqueeze(2).to_broadcast([P, SH, SP]), ALU.mult).then_inc(S["xw_ready"], 1)
                for _ in range(5):
                    phase()

        @block.scalar
        def _(act):
            a = Tally()
            act.wait_ge(s_load, 16 * N_SMALL)

            def phase():
                act.activation(dummy[0:1, 1:2], K[0:1, 0:1], ACT.Copy).then_inc(act_ph, 1)
                for s in (act_ph, dve_ph, pool_ph):
                    act.wait_ge(*a.next(s))

            def rsqrt(dst, src, n_feat, signal):
                act.activation(dst, src, ACT.Ln, bias=eps, scale=1.0 / n_feat).then_inc(act_step, 1)
                act.wait_ge(*a.next(act_step))
                act.activation(dst, dst, ACT.Exp, scale=-0.5).then_inc(signal, 1)

            def copy_out(dst, src, j, func=ACT.Copy, scale=1.0):
                act.wait_ge(*J.filled(j))
                act.activation(dst, src, func, scale=scale).then_inc(*J.free(j))

            def norm_tiles(tiles, out_of, junk_, turned):
                for t in tiles:
                    act.activation(junk_, Xt(t), ACT.Square, accum_out=ssum[:, t:t + 1]).then_inc(act_step, 1)
                    act.wait_ge(*a.next(act_step))
                r = slice(tiles[0], NT)
                act.activation(rstd[:, r], ssum[:, r], ACT.Ln, bias=eps, scale=1.0 / D).then_inc(act_step, 1)
                act.wait_ge(*a.next(act_step))
                act.activation(rstd[:, r], rstd[:, r], ACT.Exp, scale=-0.5).then_inc(act_step, 1)
                act.wait_ge(*a.next(act_step))
                for i, t in enumerate(tiles):
                    if turned is not None and i >= 2:
                        act.wait_ge(*J.filled(turned + i - 2))
                    act.activation(out_of(i, t), Xt(t), ACT.Copy, scale=rstd[:, t:t + 1]).then_inc(S["xn_ready"], 1)

            def softmax(l, heads, base, maps, P_of, PT_of):
                units = [(h, t) for h in range(heads) for t in query_tiles(l)]
                n = len(units)
                for i in range(n + 1):
                    if i < n:
                        nk = n_keys(units[i][1])
                        if i >= 2:
                            act.wait_ge(*J.filled(att_job(base, maps, n, i - 2, "turn")))
                        for m in range(maps):
                            j = att_job(base, maps, n, i, "score", m)
                            act.wait_ge(*a.next(S["negmax"]))
                            c = 2 * (i % 2) + m
                            act.activation(P_of[i % 2][m][:, 0:nk], J.tile(j)[:, 0:nk], ACT.Exp,
                                           bias=nmax[:, c:c + 1], accum_out=esum[:, c:c + 1]).then_inc(*J.free(j))
                    if i >= 1:
                        u = i - 1
                        nk = n_keys(units[u][1])
                        if u >= 2:
                            act.wait_ge(*J.filled(att_job(base, maps, n, u - 2, "value")))
                        j = att_job(base, maps, n, u, "turn")
                        copy_out(PT_of[u % 2][:, 0:nk], J.tile(j)[:, 0:nk], j)

            for l in range(DEPTH):
                def jb(n):
                    return JOB[l, n]
                rw, pc, q = row_l[l], par_l[l], query_tiles(l)
                nq, ns = len(q), slots_of(l)
                act.wait_ge(*J.freed(jb("par")))
                act.activation(sc[:, :], pc[:, R_C:R_C + 16], ACT.Silu).then_inc(S["silu_ready"], 1)
                norm_tiles(range(NT), lambda i, t: xn[i % 2], junk, jb("h"))
                phase()

                act.wait_ge(*a.next(S["lam_dots"]))
                act.activation(lam[:, 132:134], lam[:, 128:130], ACT.Exp).then_inc(S["lam_exps"], 1)
                for m in range(4):
                    copy_out(QK[:, m, :], J.tile(jb("qk") + m)[:, 0:TOK], jb("qk") + m, scale=DQ ** -0.5 if m < 2 else 1.0)
                for i, (t0, n) in enumerate(((0, 4), (4, 2))):
                    copy_out(V[:, t0:t0 + n, :].rearrange("p t n -> p (t n)"), J.tile(jb("v") + i)[:, 0:256 * n], jb("v") + i)
                softmax(l, DH, jb("datt"), 2, PD, PT_d)
                act.wait_ge(*a.next(S["o_ss"]))
                rsqrt(rstd[:, 4 * q[0]:4 * NT], ssum[:, 4 * q[0]:4 * NT], DV, S["o_rstd"])
                phase()

                for i in range(3):
                    j = jb("mla") + i
                    copy_out(MT[:, 2 * i:2 * i + 2, :],
                             J.tile(j)[:, :].rearrange("p (b n) -> p b n", b=2)[:, :, 0:MLA_COLS], j)
                act.wait_ge(*a.next(S["lat_ss"]))
                act.activation(rstd[:, 0:NT], ssum[:, 0:NT], ACT.Ln, bias=eps, scale=1.0 / MQL)
                act.activation(rstd[:, 8:8 + NT], ssum[:, 8:8 + NT], ACT.Ln, bias=eps, scale=1.0 / MKL).then_inc(act_step, 1)
                act.wait_ge(*a.next(act_step))
                act.activation(rstd[:, 0:NT], rstd[:, 0:NT], ACT.Exp, scale=-0.5)
                act.activation(rstd[:, 8:8 + NT], rstd[:, 8:8 + NT], ACT.Exp, scale=-0.5).then_inc(S["lat_rstd"], 1)
                for i in range(3):
                    j = jb("mlaT") + i
                    act.wait_ge(*J.filled(j))
                    v4 = J.tile(j)[:, :].rearrange("p (b q n) -> p b q n", b=2, q=4)
                    for s, (dst, r0, r1, col) in enumerate(((cq0, 0, P, R_QN), (cq1, 0, MQL - P, R_QN + 1),
                                                            (ckv, 0, P, R_KVN), (KT[:, 0, :], MN, MQK, None))):
                        ins = act.activation(dst[r0:r1, i * 256:i * 256 + 256].rearrange("p (b n) -> p b n", b=2),
                                             v4[r0:r1, :, s, :], ACT.Copy,
                                             scale=1.0 if col is None else pc[r0:r1, col:col + 1])
                    ins.then_inc(*J.free(j))
                for h in range(MH):
                    copy_out(QT[0:MQK, h, :], J.tile(jb("mq") + h)[0:MQK, 0:TOK], jb("mq") + h, scale=MQK ** -0.5)
                for h in range(MH):
                    copy_out(KT[0:MN, h, :], J.tile(jb("mk") + h)[0:MN, 0:TOK], jb("mk") + h)
                for i, (t0, n) in enumerate(((0, 4), (4, 2))):
                    copy_out(VM[:, t0:t0 + n, :].rearrange("p t n -> p (t n)"), J.tile(jb("mv") + i)[:, 0:256 * n],
                             jb("mv") + i)
                softmax(l, MH, jb("matt"), 1, PM, PT_m)
                phase()

                for m in range(CONV_T + 1):
                    if m < CONV_T:
                        j = jb("xbc") + m
                        act.wait_ge(*J.filled(j))
                        act.activation(XB[:, m, :], J.tile(j)[:, 0:TOK], ACT.Identity, bias=pc[:, R_CB + m:R_CB + m + 1],
                                       scale=pc[:, R_CW + CONV_T + m:R_CW + CONV_T + m + 1]).then_inc(S["conv_mid"], 1)
                    if m >= 1:
                        act.wait_ge(*J.freed(jb("xbc") + m - 1))
                        act.activation(XB[:, m - 1, :], XB[:, m - 1, :], ACT.Silu).then_inc(S["xbc_ready"], 1)
                for i in range(3):
                    copy_out(ZS[:, 2 * i:2 * i + 2, :].rearrange("p t n -> p (t n)"), J.tile(jb("z") + i)[:, :],
                             jb("z") + i, func=ACT.Silu)
                for t in range(NT):
                    copy_out(XT[:, t, :], J.tile(jb("xT") + t)[:, 0:640], jb("xT") + t)
                act.wait_ge(*a.next(S["dt_neg"]))
                act.activation(dts[1], dts[1], ACT.Exp).then_inc(S["dt_exp"], 1)
                act.activation(acol[:, 0:16], rw[:, B_ALOG:B_ALOG + 16], ACT.Exp).then_inc(S["neg_a"], 1)
                act.wait_ge(*a.next(S["dt_w"]))
                act.activation(dts[3], dts[2], ACT.Ln).then_inc(S["dt_ln"], 1)
                act.wait_ge(*a.next(S["ac_ready"]))
                act.activation(WJ, WJ, ACT.Exp)
                act.activation(EA, AC, ACT.Exp)
                act.activation(ET, TOT, ACT.Exp).then_inc(S["dec_exp"], 1)
                for i in range(nq):
                    for d in range(2):
                        act.wait_ge(*a.next(S["seg_ready"]))
                        act.activation(seg[d], seg[d], ACT.Exp).then_inc(S["seg_exp"], 1)
                act.wait_ge(*a.next(S["g_ss"]))
                rsqrt(rstd[:, 2 * q[0]:2 * NT], ssum[:, 2 * q[0]:2 * NT], SI // SG, S["g_rstd"])
                phase()

                for s in range(2):
                    copy_out(GB[s], J.tile(jb("gm") + s)[:, :], jb("gm") + s)
                for i, t in enumerate(q):
                    j = two_job(jb("out"), nq, i, True)
                    act.wait_ge(*J.filled(j))
                    act.activation(rn, J.tile(j)[:, :], ACT.Square, accum_out=ssum[:, t:t + 1]).then_inc(act_step, 1)
                    act.wait_ge(*a.next(act_step))
                    rsqrt(rstd[:, t:t + 1], ssum[:, t:t + 1], D, S["m_rstd"])
                phase()

                norm_tiles(q, lambda i, t: htok[:, t, :], fj, None)
                act.wait_ge(*a.next(S["router_max"]))
                act.activation(ex, ex, ACT.Exp).then_inc(S["router_exp"], 1)
                w = NE * ns // 2
                for i in range(2):
                    copy_out(idxB[:, i * w:(i + 1) * w], J.tile(jb("idx") + i)[:, 0:w], jb("idx") + i)
                phase()

                def pair(i, last=False):
                    o, turn, _ = pair_jobs(jb("moe"), nq, i, last)
                    before, b_turn, _ = pair_jobs(jb("moe"), nq, i - 1) if not (isinstance(i, int) and i == 0) \
                        else (None, 0, 0)
                    for p in range(2):
                        act.wait_ge(*J.filled(o[p]["gate"], turn))
                        if p:
                            act.wait_ge(*J.freed(o[0]["up"], turn))
                        elif before:
                            act.wait_ge(*J.freed(before[1]["up"], b_turn))
                        act.activation(grid_sb(sg, ns), grid(J.tile(o[p]["gate"]), ns), ACT.Silu).then_inc(*J.free(o[p]["gate"]))
                        act.wait_ge(*J.filled(o[p]["down"], turn))
                        act.activation(yb[p][0:ns, :], J.tile(o[p]["down"])[0:ns, :], ACT.Copy).then_inc(*J.free(o[p]["down"]))

                pair(0)
                pair(1)
                with act.Fori(2, NE // 2 - 1) as i:
                    pair(i)
                pair(NE // 2 - 1, last=True)
                phase()

                for s in range(2):
                    copy_out(GBf[s], J.tile(jb("gf") + s)[:, :], jb("gf") + s)
                for t in q:
                    act.activation(rnf, Fa[:, t, :], ACT.Square, accum_out=ssum[:, t:t + 1]).then_inc(act_step, 1)
                    act.wait_ge(*a.next(act_step))
                    rsqrt(rstd[:, t:t + 1], ssum[:, t:t + 1], D, S["m_rstd"])
                phase()

        @block.vector
        def _(dve):
            v = Tally()
            dve.wait_ge(s_load, 16 * N_SMALL)
            TT = dve.tensor_tensor

            def phase():
                dve.memset(dummy[0:1, 4:5], 0.0).then_inc(dve_ph, 1)
                for s in (dve_ph, act_ph, pool_ph):
                    dve.wait_ge(*v.next(s))

            def modulate(dst, j, c_scale, c_shift, s):
                dve.wait_ge(*J.filled(j))
                TT(dst, view(J.tile(j)[:, :], k=KD), c_scale[:, :, s].unsqueeze(2).to_broadcast([P, KD, P]),
                   ALU.mult).then_inc(*J.free(j))
                dve.wait_ge(*J.freed(j))
                return TT(dst, dst, c_shift[:, :, s].unsqueeze(2).to_broadcast([P, KD, P]), ALU.add)

            def attend(l, base, maps, heads, weigh, finish):
                units = [(h, t) for h in range(heads) for t in query_tiles(l)]
                n = len(units)
                for i in range(n + 2):
                    if i < n:
                        nk = n_keys(units[i][1])
                        for m in range(maps):
                            j = att_job(base, maps, n, i, "score", m)
                            dve.wait_ge(*J.filled(j))
                            if i >= 2:
                                dve.wait_ge(*J.freed(att_job(base, maps, n, i - 2, "score", m)))
                            c = 2 * (i % 2) + m
                            dve.tensor_reduce(nmax[:, c:c + 1], J.tile(j)[:, 0:nk], AX_X, ALU.max,
                                              negate=True).then_inc(S["negmax"], 1)
                    if 1 <= i <= n:
                        for m in range(maps):
                            dve.wait_ge(*J.freed(att_job(base, maps, n, i - 1, "score", m)))
                        if i >= 3:
                            dve.wait_ge(*J.freed(att_job(base, maps, n, i - 3, "value")))
                        weigh(i - 1, n_keys(units[i - 1][1]))
                    if i >= 2:
                        h, t = units[i - 2]
                        j = att_job(base, maps, n, i - 2, "value")
                        dve.wait_ge(*J.filled(j))
                        finish(i - 2, h, t, j)

            for l in range(DEPTH):
                def jb(n):
                    return JOB[l, n]
                rw, pc, q = row_l[l], par_l[l], query_tiles(l)
                nq, ns, t0 = len(q), slots_of(l), q[0]
                j = jb("par")
                dve.wait_ge(*J.filled(j))
                dve.tensor_copy(pc, J.tile(j)[:, 0:P]).then_inc(*J.free(j))
                dve.wait_ge(*J.freed(j))
                dve.tensor_copy(fac[:, 0:4], pc[:, R_SN:R_SN + 4])
                for i in range(2):
                    dve.tensor_scalar(fac[:, 4 + i:5 + i], pc[:, R_SUB:R_SUB + 1], 1.0 - LINIT[l], None, ALU.mult)
                dve.memset(fac[:, 6:8], 1.0)
                j = jb("ada")
                dve.wait_ge(*J.filled(j))
                TT(mod3, J.tile(j)[:, 0:96].rearrange("p (m s) -> p m s", s=2),
                   pc[:, R_ADAB:R_ADAB + 48].unsqueeze(2).to_broadcast([P, 48, 2]), ALU.add).then_inc(*J.free(j))
                dve.wait_ge(*J.freed(j))
                for dst, m0, col, one in ((cF, 32, R_FPRE, 1.0), (cGm, 16, R_MPOST, 0.0), (cGf, 40, R_FPOST, 0.0),
                                          (cA, 8, R_MPRE, 1.0)):
                    ins = dve.scalar_tensor_tensor(dst, mod3[:, m0:m0 + 8, :], one,
                                                   pc[:, col:col + 8].unsqueeze(2).to_broadcast([P, KD, 2]),
                                                   ALU.add, ALU.mult)
                ins.then_inc(dve_step, 1)
                dve.wait_ge(*v.next(dve_step))
                for t in range(NT):
                    modulate(hT[:, :, t * P:(t + 1) * P], jb("h") + t, cA, mod3[:, 0:8, :],
                             1 if t < CT else 0).then_inc(S["h_ready"], 1)
                phase()

                for i in range(2):
                    c = B_LAM + 64 * i
                    ins = TT(lam[:, 32 * i:32 * i + 32], rw[:, c:c + 32], rw[:, c + 32:c + 64], ALU.mult)
                ins.then_inc(dve_step, 1)
                dve.wait_ge(*v.next(dve_step))
                dve.tensor_reduce(lam[:, 128:130], view(lam[:, 0:64], a=2), AX_X, ALU.add).then_inc(S["lam_dots"], 1)
                dve.wait_ge(*v.next(S["lam_exps"]))
                TT(lam[:, 134:135], lam[:, 133:134], lam[:, 132:133], ALU.subtract).then_inc(dve_step, 1)
                dve.wait_ge(*v.next(dve_step))
                dve.tensor_scalar(lam[:, 135:136], lam[:, 134:135], -LINIT[l], None, ALU.add).then_inc(dve_step, 1)
                dve.wait_ge(*v.next(dve_step))
                for m in range(4):
                    dve.wait_ge(*J.freed(jb("qk") + m))
                    lat = QK[:, m, CTX:TOK]
                    TT(rope_t[0], lat, kc(K_COS, SEQ), ALU.mult)
                    j = jb("rot") + m
                    dve.wait_ge(*J.filled(j))
                    TT(rope_t[1], J.tile(j)[:, 0:SEQ], kc(K_SIN, SEQ), ALU.mult).then_inc(*J.free(j))
                    dve.wait_ge(*J.freed(j))
                    TT(lat, rope_t[0], rope_t[1], ALU.add).then_inc(S["qk_roped"], 1)
                    dve.wait_ge(*v.next(S["qk_roped"]))

                def diff_weigh(u, nk):
                    c = 2 * (u % 2)
                    dve.reciprocal(rcol[:, c:c + 2], esum[:, c:c + 2]).then_inc(dve_step, 1)
                    dve.wait_ge(*v.next(dve_step))
                    dve.scalar_tensor_tensor(rcol[:, 8 + c:9 + c], esum[:, c:c + 1], lam[:, 135:136],
                                             rcol[:, c + 1:c + 2], ALU.mult, ALU.mult).then_inc(dve_step, 1)
                    dve.wait_ge(*v.next(dve_step))
                    p1, p2 = PD[u % 2]
                    dve.scalar_tensor_tensor(p1[:, 0:nk], p2[:, 0:nk], rcol[:, 8 + c:9 + c], p1[:, 0:nk],
                                             ALU.mult, ALU.add).then_inc(S["prob_ready"], 1)

                def diff_finish(u, h, t, j):
                    dve.tensor_scalar(matt[:, t, h * DV:(h + 1) * DV], J.tile(j)[:, 0:DV],
                                      rcol[:, 2 * (u % 2):2 * (u % 2) + 1], None, ALU.mult).then_inc(*J.free(j))

                attend(l, jb("datt"), 2, DH, diff_weigh, diff_finish)
                dve.wait_ge(*J.freed(att_job(jb("datt"), 2, DH * nq, DH * nq - 1, "value")))
                TT(view(osq[:, 0:nq * 256], t=nq), matt[:, t0:NT, 0:256], matt[:, t0:NT, 0:256], ALU.mult).then_inc(dve_step, 1)
                dve.wait_ge(*v.next(dve_step))
                dve.tensor_reduce(ssum[:, 4 * t0:4 * NT], osq[:, 0:nq * 256].rearrange("p (a n) -> p a n", n=DV),
                                  AX_X, ALU.add).then_inc(S["o_ss"], 1)
                dve.wait_ge(*v.next(S["o_rstd"]))
                for t in q:
                    o = matt[:, t, 0:256].rearrange("p (h n) -> p h n", h=DH)
                    TT(o, o, rstd[:, 4 * t:4 * t + 4].unsqueeze(2).to_broadcast([P, DH, DV]), ALU.mult)
                phase()

                for i in range(3):
                    dve.wait_ge(*J.freed(jb("mla") + i))
                TT(msq, MT[:, :, 0:MQL + MKL], MT[:, :, 0:MQL + MKL], ALU.mult).then_inc(dve_step, 1)
                dve.wait_ge(*v.next(dve_step))
                dve.tensor_reduce(ssum[:, 0:NT], msq[:, :, 0:MQL], AX_X, ALU.add)
                dve.tensor_reduce(ssum[:, 8:8 + NT], msq[:, :, MQL:MQL + MKL], AX_X, ALU.add).then_inc(S["lat_ss"], 1)
                dve.wait_ge(*v.next(S["lat_rstd"]))
                TT(MT[:, :, 0:MQL], MT[:, :, 0:MQL], rstd[:, 0:NT].unsqueeze(2).to_broadcast([P, NT, MQL]), ALU.mult)
                TT(MT[:, :, MQL:MQL + MKL], MT[:, :, MQL:MQL + MKL],
                   rstd[:, 8:8 + NT].unsqueeze(2).to_broadcast([P, NT, MKL]), ALU.mult).then_inc(S["lat_scaled"], 1)
                R = slice(MN, MQK)
                for h in range(MH + 1):
                    if h == 0:
                        dve.wait_ge(*J.freed(jb("mlaT") + 2))
                    else:
                        dve.wait_ge(*J.freed(jb("mq") + h - 1))
                    lat = KT[R, 0, CTX:TOK] if h == 0 else QT[R, h - 1, CTX:TOK]
                    j = jb("mrot") + h
                    dve.wait_ge(*J.filled(j))
                    TT(mrope_t[R, :], lat, K[R, K_COS:K_COS + SEQ], ALU.mult).then_inc(dve_step, 1)
                    dve.wait_ge(*v.next(dve_step))
                    TT(lat, J.tile(j)[R, 0:SEQ], K[R, K_SIN:K_SIN + SEQ], ALU.mult).then_inc(*J.free(j))
                    dve.wait_ge(*J.freed(j))
                    ins = TT(lat, lat, mrope_t[R, :], ALU.add)
                    ins.then_inc(S["kr_ready"] if h == 0 else S["q_roped"], 1)
                    dve.wait_ge(*v.next(S["kr_ready"] if h == 0 else S["q_roped"]))

                def mla_weigh(u, nk):
                    c = 2 * (u % 2)
                    dve.reciprocal(rcol[:, c:c + 1], esum[:, c:c + 1]).then_inc(S["prob_ready"], 1)

                def mla_finish(u, h, t, j):
                    dve.tensor_scalar(matt[:, t, 256 + h * MV:256 + (h + 1) * MV], J.tile(j)[:, 0:MV],
                                      rcol[:, 2 * (u % 2):2 * (u % 2) + 1], None, ALU.mult).then_inc(*J.free(j))

                attend(l, jb("matt"), 1, MH, mla_weigh, mla_finish)
                phase()

                for m in range(CONV_T):
                    j = jb("xbc") + m
                    dve.wait_ge(*v.next(S["conv_mid"]))
                    src, dst = J.tile(j), XB[:, m, :]
                    for tap, sh in ((0, -1), (2, 1)):
                        w = pc[:, R_CW + tap * CONV_T + m:R_CW + tap * CONV_T + m + 1]
                        for s0, s1 in ((0, CTX), (CTX, TOK)):
                            lo, hi = (s0 + 1, s1) if sh < 0 else (s0, s1 - 1)
                            ins = dve.scalar_tensor_tensor(dst[:, lo:hi], src[:, lo + sh:hi + sh], w, dst[:, lo:hi],
                                                           ALU.mult, ALU.add)
                        if sh < 0:
                            ins.then_inc(dve_step, 1)
                            dve.wait_ge(*v.next(dve_step))
                    ins.then_inc(*J.free(j))
                j = jb("dt")
                dve.wait_ge(*J.filled(j))
                dve.wait_ge(*J.filled(jb("z") + 2))
                TT(view(dts[0], t=NT), view(J.tile(j)[:, 0:96], t=NT),
                   rw[:, B_DTB:B_DTB + 16].unsqueeze(1).to_broadcast([P, NT, 16]), ALU.add).then_inc(*J.free(j))
                dve.wait_ge(*J.freed(j))
                dve.scalar_tensor_tensor(dts[1], dts[0], -1.0, dts[0], ALU.mult, ALU.min).then_inc(S["dt_neg"], 1)
                dve.wait_ge(*v.next(S["dt_exp"]))
                dve.tensor_scalar(dts[2], dts[1], 1.0, None, ALU.add).then_inc(S["dt_w"], 1)
                dve.wait_ge(*v.next(S["dt_ln"]))
                dve.tensor_scalar(dts[4], dts[2], 1.0, 1e-30, ALU.subtract, ALU.max).then_inc(dve_step, 1)
                dve.wait_ge(*v.next(dve_step))
                dve.reciprocal(dts[5], dts[4]).then_inc(dve_step, 1)
                dve.wait_ge(*v.next(dve_step))
                TT(dts[5], dts[5], dts[1], ALU.mult).then_inc(dve_step, 1)
                dve.wait_ge(*v.next(dve_step))
                TT(dts[3], dts[3], dts[5], ALU.mult).then_inc(dve_step, 1)
                dve.wait_ge(*v.next(dve_step))
                dve.tensor_scalar(dts[4], dts[2], 1.0, None, ALU.is_equal).then_inc(dve_step, 1)
                dve.wait_ge(*v.next(dve_step))
                TT(dts[4], dts[4], dts[1], ALU.mult).then_inc(dve_step, 1)
                dve.wait_ge(*v.next(dve_step))
                TT(dts[3], dts[3], dts[4], ALU.add).then_inc(dve_step, 1)
                dve.wait_ge(*v.next(dve_step))
                dve.scalar_tensor_tensor(DTV, dts[0], 0.0, dts[3], ALU.max, ALU.add).then_inc(dve_step, 1)
                dve.wait_ge(*v.next(dve_step))
                dve.wait_ge(*v.next(S["neg_a"]))
                dve.scalar_tensor_tensor(view(LA, t=NT), view(DTV, t=NT), -1.0,
                                         acol[:, 0:16].unsqueeze(1).to_broadcast([P, NT, 16]),
                                         ALU.mult, ALU.mult).then_inc(S["la_ready"], 1)
                j = jb("cum")
                dve.wait_ge(*J.filled(j))
                ac4 = AC.rearrange("p (t d n) -> p t d n", t=NT, d=2)
                for d in range(2):
                    dve.tensor_copy(ac4[:, :, d, :], view(J.tile(j)[:, 48 * d:48 * d + 48], t=NT))
                dve.tensor_copy(TOT, J.tile(j)[:, 96:192]).then_inc(*J.free(j))
                dve.wait_ge(*J.freed(j))
                TT(WJ, TOT, AC, ALU.subtract).then_inc(S["ac_ready"], 1)
                dve.wait_ge(*v.next(S["dec_exp"]))
                TT(WJ, WJ, DTV, ALU.mult).then_inc(S["w_ready"], 1)
                for t in range(NT):
                    dve.wait_ge(*J.freed(jb("xT") + t))
                for i, t in enumerate(q):
                    sj = [ssd_job(jb("ssd"), nq, i, k) for k in range(4)]
                    dve.wait_ge(*J.filled(sj[0]))
                    dve.tensor_copy(cbs, view(J.tile(sj[0])[:, :], g=SG)[:, :, 0:P]).then_inc(*J.free(sj[0]))
                    dve.wait_ge(*J.freed(sj[0]))
                    for d in range(2):
                        dve.wait_ge(*J.filled(sj[1 + d]))
                        ac = AC[:, t * 16 + 8 * d:t * 16 + 8 * d + 8].unsqueeze(2).to_broadcast([P, SH, P])
                        TT(seg[d], view(J.tile(sj[1 + d])[:, :], h=SH), ac, ALU.subtract).then_inc(*J.free(sj[1 + d]))
                        dve.wait_ge(*J.freed(sj[1 + d]))
                        mk = kc(K_MF if d == 0 else K_MB).unsqueeze(1).to_broadcast([P, SH, P])
                        TT(seg[d], seg[d], mk, ALU.min).then_inc(S["seg_ready"], 1)
                    for d in range(2):
                        dve.wait_ge(*v.next(S["seg_exp"]))
                        dt_ = DTV[:, t * 16 + 8 * d:t * 16 + 8 * d + 8].unsqueeze(2).to_broadcast([P, SH, P])
                        TT(seg[d], seg[d], dt_, ALU.mult).then_inc(dve_step, 1)
                        dve.wait_ge(*v.next(dve_step))
                    TT(seg[2], seg[0], seg[1], ALU.add).then_inc(dve_step, 1)
                    dve.wait_ge(*v.next(dve_step))
                    for g in range(SG):
                        hs = slice(g * HPG, (g + 1) * HPG)
                        ins = TT(seg[2][:, hs, :], seg[2][:, hs, :], cbs[:, g, :].unsqueeze(1).to_broadcast([P, HPG, P]),
                                 ALU.mult)
                    ins.then_inc(S["mask_ready"], 1)
                    TT(view(xdk, h=SH), view(XT[:, t, 0:SI], h=SH),
                       rw[:, B_DSK:B_DSK + 8].unsqueeze(2).to_broadcast([P, SH, SP]), ALU.mult).then_inc(dve_step, 1)
                    dve.wait_ge(*v.next(dve_step))
                    dve.wait_ge(*J.filled(sj[3]))
                    TT(Y[:, t, :], J.tile(sj[3])[:, 0:SI], xdk, ALU.add).then_inc(*J.free(sj[3]))
                dve.wait_ge(*J.freed(ssd_job(jb("ssd"), nq, nq - 1, 3)))
                for n, (d, c, t) in enumerate(chunks()):
                    j = jb("rec") + n
                    dve.wait_ge(*J.filled(j))
                    if c and t in q:
                        ea = EA[:, t * 16 + 8 * d:t * 16 + 8 * d + 8].rearrange("p (g h) -> p g h", g=SG)
                        TT(ytmp.rearrange("p (g h n) -> p g h n", g=SG, h=HPG),
                           view(J.tile(j)[:, :], g=SG)[:, :, 0:256].rearrange("p g (h n) -> p g h n", h=HPG),
                           ea.unsqueeze(3).to_broadcast([P, SG, HPG, SP]), ALU.mult).then_inc(dve_step, 1)
                        dve.wait_ge(*v.next(dve_step))
                        TT(Y[:, t, :], Y[:, t, :], ytmp, ALU.add).then_inc(dve_step, 1)
                        dve.wait_ge(*v.next(dve_step))
                    if c:
                        for g in range(SG):
                            et = ET[g * SN:(g + 1) * SN, t * 16 + 8 * d + g * HPG:t * 16 + 8 * d + (g + 1) * HPG]
                            hv = view(HS[d][g * SN:(g + 1) * SN, :], h=HPG)
                            ins = TT(hv, hv, et.unsqueeze(2).to_broadcast([SN, HPG, SP]), ALU.mult)
                        ins.then_inc(dve_step, 1)
                        dve.wait_ge(*v.next(dve_step))
                        TT(HS[d], HS[d], J.tile(j)[:, 768:1024], ALU.add).then_inc(*J.free(j))
                        dve.wait_ge(*J.freed(j))
                    else:
                        dve.tensor_copy(HS[d], J.tile(j)[:, 768:1024]).then_inc(*J.free(j))
                        dve.wait_ge(*J.freed(j))
                TT(Y[:, t0:NT, :], Y[:, t0:NT, :], ZS[:, t0:NT, :], ALU.mult).then_inc(dve_step, 1)
                dve.wait_ge(*v.next(dve_step))
                TT(view(ysq[:, 0:nq * SI], t=nq), Y[:, t0:NT, :], Y[:, t0:NT, :], ALU.mult).then_inc(dve_step, 1)
                dve.wait_ge(*v.next(dve_step))
                dve.tensor_reduce(ssum[:, 2 * t0:2 * NT], ysq[:, 0:nq * SI].rearrange("p (a n) -> p a n", n=SI // SG),
                                  AX_X, ALU.add).then_inc(S["g_ss"], 1)
                dve.wait_ge(*v.next(S["g_rstd"]))
                for t in q:
                    y3 = view(Y[:, t, :], g=SG)
                    TT(y3, y3, rstd[:, 2 * t:2 * t + 2].unsqueeze(2).to_broadcast([P, SG, SI // SG]), ALU.mult)
                phase()

                for s in range(2):
                    TT(diag[s], ident.unsqueeze(1).to_broadcast([P, KD, P]),
                       cGm[:, :, s].unsqueeze(2).to_broadcast([P, KD, P]), ALU.mult).then_inc(S["diag_ready"], 1)
                for i in range(nq + 1):
                    if i < nq:
                        j = two_job(jb("out"), nq, i, False)
                        dve.wait_ge(*J.filled(j))
                        if i >= 2:
                            dve.wait_ge(*J.filled(two_job(jb("out"), nq, i - 2, True)))
                        TT(mixT[i % 2], view(J.tile(j)[:, :], k=KD),
                           fac[:, 0:8].unsqueeze(2).to_broadcast([P, KD, P]), ALU.mult).then_inc(*J.free(j))
                    if i >= 1:
                        t = q[i - 1]
                        j = two_job(jb("out"), nq, i - 1, True)
                        dve.wait_ge(*J.filled(j))
                        dve.wait_ge(*v.next(S["m_rstd"]))
                        dve.wait_ge(*J.freed(jb("gm") + (1 if t < CT else 0)))
                        dve.scalar_tensor_tensor(rn2, J.tile(j)[:, :], rstd[:, t:t + 1], GB[1 if t < CT else 0],
                                                 ALU.mult, ALU.mult).then_inc(*J.free(j))
                        dve.wait_ge(*J.freed(j))
                        TT(Xt(t), Xt(t), rn2, ALU.add).then_inc(dve_step, 1)
                        dve.wait_ge(*v.next(dve_step))
                phase()

                def logits(i):
                    j = two_job(jb("f"), nq, i, True)
                    dve.wait_ge(*J.filled(j))
                    TT(aff[:, q[i] * NE:(q[i] + 1) * NE], J.tile(j)[:, 0:NE], rw[:, B_RB:B_RB + NE], ALU.add).then_inc(*J.free(j))

                for i, t in enumerate(q):
                    if i >= 2:
                        dve.wait_ge(*J.filled(two_job(jb("f"), nq, i - 2, True)))
                    modulate(fhT[i % 2], two_job(jb("f"), nq, i, False), cF, mod3[:, 24:32, :],
                             1 if t < CT else 0).then_inc(S["h_ready"], 1)
                    if i:
                        logits(i - 1)
                logits(nq - 1)
                for i in range(nq):
                    dve.wait_ge(*J.freed(two_job(jb("f"), nq, i, True)))
                lg, e3 = (x[:, t0 * NE:NT * NE].rearrange("p (t n) -> p t n", n=NE) for x in (aff, ex))
                if t0:
                    dve.memset(ex[:, 0:t0 * NE], 0.0)
                dve.tensor_reduce(ssum[:, 32:32 + nq], lg, AX_X, ALU.max).then_inc(dve_step, 1)
                dve.wait_ge(*v.next(dve_step))
                TT(e3, lg, ssum[:, 32:32 + nq].unsqueeze(2).to_broadcast([P, nq, NE]), ALU.subtract)\
                    .then_inc(S["router_max"], 1)
                dve.wait_ge(*v.next(S["router_exp"]))
                dve.tensor_reduce(ssum[:, 40:40 + nq], e3, AX_X, ALU.add).then_inc(dve_step, 1)
                dve.wait_ge(*v.next(dve_step))
                dve.reciprocal(ssum[:, 48:48 + nq], ssum[:, 40:40 + nq]).then_inc(dve_step, 1)
                dve.wait_ge(*v.next(dve_step))
                TT(e3, e3, ssum[:, 48:48 + nq].unsqueeze(2).to_broadcast([P, nq, NE]), ALU.mult)\
                    .then_inc(S["aff_ready"], 1)
                j = jb("aT")
                dve.wait_ge(*J.filled(j))
                dve.tensor_copy(aT[0][0:NE, t0 * P:TOK], J.tile(j)[0:NE, t0 * P:TOK]).then_inc(*J.free(j))
                dve.wait_ge(*J.freed(j))
                idi = idu.bitcast(U32)
                for s0, s1, c0, cap in ((CTX, TOK, 0, CAP_L), (0, CTX, CAP_L, CAP_C)):
                    if s0 < t0 * P:
                        continue
                    for r in range(cap // 8):
                        c = c0 + 8 * r
                        src = aT[r % 2][0:NE, s0:s1]
                        dve.max(gv[0:NE, c:c + 8], src).then_inc(dve_step, 1)
                        dve.wait_ge(*v.next(dve_step))
                        dve.max_index(idi[0:NE, c:c + 8], gv[0:NE, c:c + 8], src)
                        dve.match_replace(aT[1 - r % 2][0:NE, s0:s1], gv[0:NE, c:c + 8], src, -1.0).then_inc(dve_step, 1)
                        dve.wait_ge(*v.next(dve_step))
                    dve.tensor_copy(idf[0:NE, c0:c0 + cap], idi[0:NE, c0:c0 + cap]).then_inc(dve_step, 1)
                    dve.wait_ge(*v.next(dve_step))
                    if s0:
                        dve.tensor_scalar(idf[0:NE, c0:c0 + cap], idf[0:NE, c0:c0 + cap], float(s0), None, ALU.add).then_inc(dve_step, 1)
                        dve.wait_ge(*v.next(dve_step))
                dve.memset(dummy[0:1, 5:6], 0.0).then_inc(S["topk_ready"], 1)
                TT(bd[0:NE, 0:NE * ns].rearrange("p (e n) -> p e n", e=NE),
                   idf[0:NE, 0:ns].unsqueeze(1).to_broadcast([NE, NE, ns]),
                   K[0:NE, K_ID:K_ID + NE].unsqueeze(2).to_broadcast([NE, NE, ns]), ALU.mult).then_inc(S["bd_ready"], 1)
                j = jb("idx") + 2
                dve.wait_ge(*J.filled(j))
                dve.tensor_copy(slotc[0:ns, 0:32], J.tile(j)[0:ns, 0:32]).then_inc(*J.free(j))
                phase()

                parts = ((0, 0, CAP_L), (1, CAP_L, CAP_C))[:2 if ns > CAP_L else 1]
                dve.memset(Fa[:, t0:NT, :], 0.0).then_inc(dve_step, 1)
                dve.wait_ge(*v.next(dve_step))

                def select(e, p):
                    src = idxB[:, e * ns:(e + 1) * ns] if isinstance(e, int) else idxB[:, bass.ds(e * ns, ns)]
                    TT(view(Sel[p][:, 0:nq * ns], t=nq), src.unsqueeze(1).to_broadcast([P, nq, ns]),
                       K[:, K_TID + t0:K_TID + NT].unsqueeze(2).to_broadcast([P, nq, ns]),
                       ALU.is_equal).then_inc(S["sel_ready"], 1)

                def scatter_mask(e, p):
                    def col(c):
                        return slotc[0:ns, c + e:c + e + 1] if isinstance(e, int) else slotc[0:ns, bass.ds(e + c, 1)]
                    dve.tensor_scalar(Sc[p][0:ns, 0:nq * P], K[0:ns, K_IOTA + t0 * P:K_IOTA + TOK], col(0), col(NE),
                                      ALU.is_equal, ALU.mult).then_inc(S["scat_ready"], 1)

                def gathered(j, turn, p):
                    dve.wait_ge(*J.filled(j, turn))
                    for s, c, n in parts:
                        ins = TT(grid_sb(xg[p], ns)[:, :, :, c:c + n], grid(J.tile(j), ns)[:, :, :, c:c + n],
                                 cF[:, :, s].rearrange("p (b k) -> p b k", b=2).unsqueeze(3).to_broadcast([P, 2, 4, n]),
                                 ALU.mult)
                    ins.then_inc(*J.free(j))
                    dve.wait_ge(*J.freed(j, turn))
                    for s, c, n in parts:
                        x4 = grid_sb(xg[p], ns)[:, :, :, c:c + n]
                        ins = TT(x4, x4, mod3[:, 24:32, s].rearrange("p (b k) -> p b k", b=2).unsqueeze(3)
                                 .to_broadcast([P, 2, 4, n]), ALU.add)
                    ins.then_inc(S["xg_ready"], 1)

                def scattered(j, turn):
                    for k, t in enumerate(q):
                        dve.wait_ge(*J.filled(j + k, turn))
                        TT(Fa[:, t, :], Fa[:, t, :], J.tile(j + k)[:, :], ALU.add).then_inc(*J.free(j + k))

                def pair(i, last=False):
                    first = isinstance(i, int) and i == 0
                    o, turn, end = pair_jobs(jb("moe"), nq, i, last)
                    for p in range(2):
                        e = i * 2 + p
                        scatter_mask(e, p)
                        if not (last and p):
                            select(e + 1, 1 - p)
                        dve.wait_ge(*J.filled(o[p]["up"], turn))
                        dve.wait_ge(*J.freed(o[p]["gate"], turn))
                        TT(grid_sb(hid[p], ns), grid_sb(sg, ns), grid(J.tile(o[p]["up"]), ns), ALU.mult).then_inc(*J.free(o[p]["up"]))
                        if not (first and p == 0):
                            scattered(o[p]["scatter"], turn)
                        if not (last and p):
                            gathered(o[p]["gather"], turn, 1 - p)
                    return end, turn

                select(0, 0)
                gathered(jb("moe"), 0, 0)
                pair(0)
                with dve.Fori(1, NE // 2 - 1) as i:
                    pair(i)
                end, turn = pair(NE // 2 - 1, last=True)
                scattered(end, turn)
                phase()

                for s in range(2):
                    TT(diagf[s], ident.unsqueeze(1).to_broadcast([P, KD, P]),
                       cGf[:, :, s].unsqueeze(2).to_broadcast([P, KD, P]), ALU.mult).then_inc(S["diag_ready"], 1)
                for s in range(2):
                    dve.wait_ge(*J.freed(jb("gf") + s))
                for t in q:
                    dve.wait_ge(*v.next(S["m_rstd"]))
                    dve.scalar_tensor_tensor(Fa[:, t, :], Fa[:, t, :], rstd[:, t:t + 1], GBf[1 if t < CT else 0],
                                             ALU.mult, ALU.mult).then_inc(dve_step, 1)
                    dve.wait_ge(*v.next(dve_step))
                    ins = TT(Xt(t), Xt(t), Fa[:, t, :], ALU.add)
                    if l == DEPTH - 1:
                        ins.then_inc(S["out_ready"], 1)
                phase()

        @block.tensor
        def _(pe):
            w_ = Tally()
            pe.wait_ge(s_load, 16 * N_SMALL)
            mm = pe.matmul

            def phase():
                for s in (dve_ph, act_ph, pool_ph):
                    pe.wait_ge(*w_.next(s))

            def arrived(j, turn=0):
                pe.wait_ge(ring_full[j % RING], turn + (j // RING + 1) * 16)
                return ringv(j)

            def feature_major(j, w, col, n):
                pe.wait_ge(*J.empty(j))
                o = J.tile(j)
                for c0, c1 in spans(NT):
                    for k in range(KD):
                        ins = mm(o[0:n, c0:c1], w[:, k, col:col + n], hT[:, k, c0:c1], start=k == 0, stop=k == KD - 1)
                ins.then_inc(*J.fill(j))

            def token_major(j, w, tiles, n, stride):
                pe.wait_ge(*J.empty(j))
                o = J.tile(j)
                for i, t in enumerate(tiles):
                    for k in range(KD):
                        ins = mm(o[:, i * stride:i * stride + n], hT[:, k, t * P:(t + 1) * P], w[:, k, :],
                                 start=k == 0, stop=k == KD - 1)
                ins.then_inc(*J.fill(j))

            def turn_tile(j, src, n=KD):
                pe.wait_ge(*J.empty(j))
                o = J.tile(j)
                for k in range(n):
                    ins = pe.transpose(o[:, k * P:(k + 1) * P], src(k), ident)
                ins.then_inc(*J.fill(j))

            def attention(l, heads, base, maps, score, P_of, PT_of, v_of):
                units = [(h, t) for h in range(heads) for t in query_tiles(l)]
                n = len(units)

                def scores(u):
                    h, t = units[u]
                    for m in range(maps):
                        j = att_job(base, maps, n, u, "score", m)
                        pe.wait_ge(*J.empty(j))
                        o = J.tile(j)
                        for c0, c1 in spans(t):
                            lhs, rhs = score(h, m, t, c0, c1)
                            ins = mm(o[:, c0:c1], lhs, rhs, start=True, stop=True)
                        ins.then_inc(*J.fill(j))

                def values(u):
                    h, t = units[u]
                    pe.wait_ge(*J.freed(att_job(base, maps, n, u, "turn")))
                    j = att_job(base, maps, n, u, "value")
                    pe.wait_ge(*J.empty(j))
                    o = J.tile(j)
                    nk = n_keys(t) // P
                    for k in range(nk):
                        ins = mm(o[:, 0:64], PT_of[u % 2][:, k * P:(k + 1) * P], v_of(h, k), start=k == 0, stop=k == nk - 1)
                    ins.then_inc(*J.fill(j))

                scores(0)
                for u in range(n):
                    if u + 1 < n:
                        scores(u + 1)
                    pe.wait_ge(*w_.next(S["prob_ready"]))
                    turn_tile(att_job(base, maps, n, u, "turn"), lambda k: P_of[u % 2][0][:, k * P:(k + 1) * P],
                              n_keys(units[u][1]) // P)
                    if u:
                        values(u - 1)
                values(n - 1)

            def gate_rows(j, dg):
                pe.wait_ge(*w_.next(S["diag_ready"]))
                pe.wait_ge(*J.empty(j))
                o = J.tile(j)
                for hf in range(2):
                    ins = mm(o[:, hf * 512:(hf + 1) * 512], ones, dg[:, 4 * hf:4 * hf + 4, :].rearrange("p k n -> p (k n)"),
                             start=True, stop=True)
                ins.then_inc(*J.fill(j))

            for l in range(DEPTH):
                def jb(n):
                    return JOB[l, n]
                wb, q = l * LAYER_BLOCKS, query_tiles(l)
                nq, ns, t0 = len(q), slots_of(l), q[0]
                j = jb("par")
                pe.wait_ge(*J.empty(j))
                o = J.tile(j)
                pe.transpose(o[:, 0:P], pack[:, l * P:(l + 1) * P], ident).then_inc(*J.fill(j))
                pe.wait_ge(*w_.next(S["silu_ready"]))
                j = jb("ada")
                pe.wait_ge(*J.empty(j))
                o = J.tile(j)
                sc3 = sc[:, :].rearrange("p (s k) -> p s k", s=2)
                for b in range(12):
                    w = arrived(wb + b)
                    for m in range(4):
                        c = 2 * (4 * b + m)
                        for k in range(KD):
                            ins = mm(o[:, c:c + 2], w[:, k, m * P:(m + 1) * P], sc3[:, :, k], start=k == 0, stop=k == KD - 1)
                    if b < 11:
                        ins.then_inc(half_used, 1)
                ins.then_inc(*J.fill(j))
                for t in range(NT):
                    pe.wait_ge(*w_.next(S["xn_ready"]))
                    turn_tile(jb("h") + t, lambda k: xn[t % 2][:, k * P:(k + 1) * P])
                pe.wait_ge(*w_.next(S["h_ready"], NT))
                phase()

                w = arrived(wb + 12)
                for m in range(4):
                    feature_major(jb("qk") + m, w, m * P, P)
                w = arrived(wb + 13)
                token_major(jb("v"), w[:, :, 0:256], range(0, 4), 256, 256)
                token_major(jb("v") + 1, w[:, :, 0:256], range(4, 6), 256, 256)
                for m in range(4):
                    j = jb("rot") + m
                    pe.wait_ge(*J.freed(jb("qk") + m))
                    pe.wait_ge(*J.empty(j))
                    o = J.tile(j)
                    mm(o[:, 0:SEQ], kc(K_ROT), QK[:, m, CTX:TOK], start=True, stop=True).then_inc(*J.fill(j))
                pe.wait_ge(*w_.next(S["qk_roped"], 4))
                pe.wait_ge(*J.freed(jb("v")))
                pe.wait_ge(*J.freed(jb("v") + 1))

                def diff_score(h, m, t, c0, c1):
                    r = slice(64 * (h % 2) + 32 * m, 64 * (h % 2) + 32 * m + 32)
                    return QK[r, h // 2, t * P:(t + 1) * P], QK[r, 2 + h // 2, c0:c1]

                attention(l, DH, jb("datt"), 2, diff_score, PD, PT_d, lambda h, k: V[:, k, h * DV:(h + 1) * DV])
                phase()

                w = arrived(wb + 14)
                for i in range(3):
                    token_major(jb("mla") + i, w[:, :, 0:MLA_COLS], (2 * i, 2 * i + 1), MLA_COLS, 512)
                pe.wait_ge(*w_.next(S["lat_scaled"]))
                for i in range(3):
                    j = jb("mlaT") + i
                    pe.wait_ge(*J.empty(j))
                    o = J.tile(j)
                    for b in range(2):
                        m_ = MT[:, 2 * i + b, :]
                        for s, (c0, n) in enumerate(((0, P), (P, MQL - P), (MQL, P), (MLA_COLS - MQK, MQK))):
                            c = 512 * b + P * s
                            ins = pe.transpose(o[0:n, c:c + P], m_[:, c0:c0 + n], ident)
                    ins.then_inc(*J.fill(j))
                for i in range(3):
                    pe.wait_ge(*J.freed(jb("mlaT") + i))
                wq = wqu[:, l * 2 * MH * MQK:(l + 1) * 2 * MH * MQK]
                wk = wkv[:, l * 512:(l + 1) * 512]
                for h in range(MH):
                    j = jb("mq") + h
                    pe.wait_ge(*J.empty(j))
                    o = J.tile(j)
                    for c0, c1 in spans(NT):
                        mm(o[0:MQK, c0:c1], wq[:, h * MQK:(h + 1) * MQK], cq0[:, c0:c1], start=True, stop=False)
                        ins = mm(o[0:MQK, c0:c1], wq[0:MQL - P, (MH + h) * MQK:(MH + h + 1) * MQK], cq1[0:MQL - P, c0:c1],
                                 start=False, stop=True)
                    ins.then_inc(*J.fill(j))
                for h in range(MH):
                    j = jb("mk") + h
                    pe.wait_ge(*J.empty(j))
                    o = J.tile(j)
                    for c0, c1 in spans(NT):
                        ins = mm(o[0:MN, c0:c1], wk[:, h * P:h * P + MN], ckv[:, c0:c1], start=True, stop=True)
                    ins.then_inc(*J.fill(j))
                for i, tiles in enumerate((range(0, 4), range(4, 6))):
                    j = jb("mv") + i
                    pe.wait_ge(*J.empty(j))
                    o = J.tile(j)
                    for n, t in enumerate(tiles):
                        ins = mm(o[:, n * 256:(n + 1) * 256], ckv[:, t * P:(t + 1) * P],
                                 wk.rearrange("p (h n) -> p h n", h=MH)[:, :, MN:P], start=True, stop=True)
                    ins.then_inc(*J.fill(j))
                R = slice(MN, MQK)
                for h in range(MH + 1):
                    j = jb("mrot") + h
                    if h:
                        pe.wait_ge(*J.freed(jb("mq") + h - 1))
                    pe.wait_ge(*J.empty(j))
                    o = J.tile(j)
                    src = KT[R, 0, CTX:TOK] if h == 0 else QT[R, h - 1, CTX:TOK]
                    mm(o[R, 0:SEQ], K[R, K_ROT + MN:K_ROT + MQK], src, start=True, stop=True).then_inc(*J.fill(j))
                pe.wait_ge(*w_.next(S["q_roped"], MH))
                pe.wait_ge(*w_.next(S["kr_all"], MH - 1))
                for h in range(MH):
                    pe.wait_ge(*J.freed(jb("mk") + h))
                for i in range(2):
                    pe.wait_ge(*J.freed(jb("mv") + i))
                attention(l, MH, jb("matt"), 1,
                          lambda h, m, t, c0, c1: (QT[0:MQK, h, t * P:(t + 1) * P], KT[0:MQK, h, c0:c1]),
                          PM, PT_m, lambda h, k: VM[:, k, h * MV:(h + 1) * MV])
                phase()

                w = arrived(wb + 15)
                for m in range(4):
                    feature_major(jb("xbc") + m, w, m * P, P)
                w = arrived(wb + 16)
                for m in range(4, 6):
                    feature_major(jb("xbc") + m, w, (m - 4) * P, P)
                token_major(jb("dt"), w[:, :, 256:272], range(NT), 16, 16)
                w = arrived(wb + 17)
                for i in range(3):
                    token_major(jb("z") + i, w, (2 * i, 2 * i + 1), 512, 512)
                pe.wait_ge(*w_.next(S["xbc_ready"], CONV_T))
                for t in range(NT):
                    turn_tile(jb("xT") + t, lambda k: XB[:, k, t * P:(t + 1) * P], 5)
                pe.wait_ge(*w_.next(S["la_ready"]))
                j = jb("cum")
                pe.wait_ge(*J.empty(j))
                o = J.tile(j)
                la3 = LA.rearrange("p (t d n) -> p t d n", t=NT, d=2)
                mm(o[:, 0:48], kc(K_TRU), la3[:, :, 0, :], start=True, stop=True)
                mm(o[:, 48:96], kc(K_TRL), la3[:, :, 1, :], start=True, stop=True)
                mm(o[:, 96:192], ones, LA, start=True, stop=True).then_inc(*J.fill(j))
                BT, CTr = XB[:, 4, :], XB[:, 5, :]

                def chunk_inner(i):
                    t = q[i]
                    j = ssd_job(jb("ssd"), nq, i, 0)
                    pe.wait_ge(*J.empty(j))
                    o = J.tile(j)
                    for g in range(SG):
                        r = slice(g * SN, (g + 1) * SN)
                        ins = mm(o[:, g * 512:g * 512 + P], BT[r, t * P:(t + 1) * P], CTr[r, t * P:(t + 1) * P],
                                 start=True, stop=True)
                    ins.then_inc(*J.fill(j))
                    for d in range(2):
                        j = ssd_job(jb("ssd"), nq, i, 1 + d)
                        pe.wait_ge(*J.empty(j))
                        o = J.tile(j)
                        for h in range(SH):
                            c = t * 16 + 8 * d + h
                            ins = mm(o[:, h * P:(h + 1) * P], LA[:, c:c + 1].to_broadcast([P, P]),
                                     kc(K_TRU if d == 0 else K_TRL), start=True, stop=True)
                        ins.then_inc(*J.fill(j))

                def chunk_product(i):
                    pe.wait_ge(*w_.next(S["mask_ready"]))
                    j = ssd_job(jb("ssd"), nq, i, 3)
                    pe.wait_ge(*J.empty(j))
                    o = J.tile(j)
                    for h in range(SH):
                        ins = mm(o[:, h * SP:(h + 1) * SP], seg[2][:, h, :], XT[:, q[i], h * SP:(h + 1) * SP],
                                 start=True, stop=True)
                    ins.then_inc(*J.fill(j))

                chunk_inner(0)
                for i in range(nq):
                    if i + 1 < nq:
                        chunk_inner(i + 1)
                    chunk_product(i)
                for n, (d, c, t) in enumerate(chunks()):
                    j = jb("rec") + n
                    pe.wait_ge(*J.empty(j))
                    o = J.tile(j)
                    if c and t in q:
                        pe.wait_ge(*J.freed(jb("rec") + n - 2))
                        for g in range(SG):
                            r = slice(g * SN, (g + 1) * SN)
                            mm(o[:, g * 512:g * 512 + 256], CTr[r, t * P:(t + 1) * P], HS[d][r, :], start=True, stop=True)
                    pe.wait_ge(*w_.next(S["xw_ready"]))
                    for g in range(SG):
                        ins = mm(o[g * SN:(g + 1) * SN, 768:1024], XT[:, t, SI + g * SN:SI + (g + 1) * SN],
                                 XW[n % 2][:, g * 256:(g + 1) * 256], start=True, stop=True)
                    ins.then_inc(*J.fill(j))
                phase()

                for s in range(2):
                    gate_rows(jb("gm") + s, diag[s])
                wo = [arrived(wb + 18), arrived(wb + 19)]

                def mixed(i):
                    turn_tile(two_job(jb("out"), nq, i, False),
                              lambda k: Y[:, q[i], k * P:(k + 1) * P] if k < 4 else matt[:, q[i], (k - 4) * P:(k - 3) * P])

                mixed(0)
                for i in range(nq):
                    if i + 1 < nq:
                        mixed(i + 1)
                    pe.wait_ge(*J.freed(two_job(jb("out"), nq, i, False)))
                    j = two_job(jb("out"), nq, i, True)
                    pe.wait_ge(*J.empty(j))
                    o = J.tile(j)
                    for hf in range(2):
                        for k in range(KD):
                            ins = mm(o[:, hf * 512:(hf + 1) * 512], mixT[i % 2][:, k, :], wo[hf][:, k, :], start=k == 0,
                                     stop=k == KD - 1)
                    ins.then_inc(*J.fill(j))
                phase()

                def rows_turned(i):
                    pe.wait_ge(*w_.next(S["xn_ready"]))
                    turn_tile(two_job(jb("f"), nq, i, False), lambda k: htok[:, q[i], k * P:(k + 1) * P])

                wr = view(wrt[:, l * KD * NE:(l + 1) * KD * NE], k=KD)
                rows_turned(0)
                for i in range(nq):
                    if i + 1 < nq:
                        rows_turned(i + 1)
                    pe.wait_ge(*w_.next(S["h_ready"]))
                    j = two_job(jb("f"), nq, i, True)
                    pe.wait_ge(*J.empty(j))
                    o = J.tile(j)
                    for k in range(KD):
                        ins = mm(o[:, 0:NE], fhT[i % 2][:, k, :], wr[:, k, :], start=k == 0, stop=k == KD - 1)
                    ins.then_inc(*J.fill(j))
                pe.wait_ge(*w_.next(S["aff_ready"]))
                j = jb("aT")
                pe.wait_ge(*J.empty(j))
                o = J.tile(j)
                for t in q:
                    ins = pe.transpose(o[0:NE, t * P:(t + 1) * P], ex[:, t * NE:(t + 1) * NE], ident)
                ins.then_inc(*J.fill(j))
                pe.wait_ge(*w_.next(S["bd_ready"]))
                wd = NE * ns // 2
                for i in range(2):
                    j = jb("idx") + i
                    pe.wait_ge(*J.empty(j))
                    o = J.tile(j)
                    for c0, c1 in ((0, 512), (512, wd)):
                        if c0 < c1:
                            ins = mm(o[:, c0:c1], K[0:NE, K_ONE:K_ONE + P], bd[0:NE, i * wd + c0:i * wd + c1],
                                     start=True, stop=True)
                    ins.then_inc(*J.fill(j))
                pe.wait_ge(*w_.next(S["topk_ready"]))
                j = jb("idx") + 2
                pe.wait_ge(*J.empty(j))
                o = J.tile(j)
                pe.transpose(o[0:ns, 0:NE], idf[0:NE, 0:ns], K[0:NE, K_ID:K_ID + NE])
                pe.transpose(o[0:ns, NE:2 * NE], gv[0:NE, 0:ns], K[0:NE, K_ID:K_ID + NE]).then_inc(*J.fill(j))
                phase()

                def gather(j, turn, e, p):
                    pe.wait_ge(S["sel_ready"], e + (l * NE + 1))
                    pe.wait_ge(*J.empty(j, turn))
                    o = grid(J.tile(j), ns)
                    for k in range(KD):
                        for s0, s1, c, n in ((CT, NT, 0, CAP_L), (0, CT, CAP_L, CAP_C))[:2 if ns > CAP_L else 1]:
                            for t in range(s0, s1):
                                b = (t - t0) * ns + c
                                ins = mm(o[:, k // 4, k % 4, c:c + n], htok[:, t, k * P:(k + 1) * P], Sel[p][:, b:b + n],
                                         start=t == s0, stop=t == s1 - 1)
                    ins.then_inc(*J.fill(j))

                def up_proj(j, turn, blk, b_turn, p):
                    pe.wait_ge(*J.empty(j, turn))
                    o = grid(J.tile(j), ns)
                    for hf in range(2):
                        w = arrived(blk + hf, b_turn)
                        for f in range(4):
                            for k in range(KD):
                                ins = mm(o[:, hf, f, :], w[:, k, f * P:(f + 1) * P], xg[p][:, k * ns:(k + 1) * ns],
                                         start=k == 0, stop=k == KD - 1)
                        if hf == 0:
                            ins.then_inc(half_used, 1)
                    ins.then_inc(*J.fill(j))

                def down_proj(j, turn, blk, b_turn, p):
                    pe.wait_ge(*J.empty(j, turn))
                    o = J.tile(j)
                    for hf in range(2):
                        w = arrived(blk + hf, b_turn)
                        for f in range(KD):
                            ins = mm(o[0:ns, hf * 512:(hf + 1) * 512], hid[p][:, f * ns:(f + 1) * ns], w[:, f, :],
                                     start=f == 0, stop=f == KD - 1)
                        if hf == 0:
                            ins.then_inc(half_used, 1)
                    ins.then_inc(*J.fill(j))

                def scatter(j, turn, e, p):
                    pe.wait_ge(S["scat_ready"], e + (l * NE + 1))
                    for k in range(nq):
                        pe.wait_ge(*J.empty(j + k, turn))
                        o = J.tile(j + k)
                        for hf in range(2):
                            ins = mm(o[:, hf * 512:(hf + 1) * 512], Sc[p][0:ns, k * P:(k + 1) * P],
                                     yb[p][0:ns, hf * 512:(hf + 1) * 512], start=True, stop=True)
                        ins.then_inc(*J.fill(j + k))

                def pair(i, last=False):
                    first = isinstance(i, int) and i == 0
                    o, turn, end = pair_jobs(jb("moe"), nq, i, last)
                    if not first:
                        before, turn_b, _ = pair_jobs(jb("moe"), nq, i - 1)
                    for p in range(2):
                        e = i * 2 + p
                        blk = wb + 20 + 6 * p
                        pe.wait_ge(S["xg_ready"], e + (l * NE + 1))
                        up_proj(o[p]["gate"], turn, blk, i * 48, p)
                        up_proj(o[p]["up"], turn, blk + 2, i * 48, p)
                        if p:
                            pe.wait_ge(*J.freed(o[0]["down"], turn))
                            scatter(o[p]["scatter"], turn, e - 1, 0)
                        elif not first:
                            pe.wait_ge(*J.freed(before[1]["down"], turn_b))
                            scatter(o[p]["scatter"], turn, e - 1, 1)
                        if not (last and p):
                            gather(o[p]["gather"], turn, e + 1, 1 - p)
                        pe.wait_ge(*J.freed(o[p]["up"], turn))
                        down_proj(o[p]["down"], turn, blk + 4, i * 48, p)
                    return o, end, turn

                gather(jb("moe"), 0, 0, 0)
                pair(0)
                pair(1)
                with pe.Fori(2, NE // 2 - 1) as i:
                    pair(i)
                o, end, turn = pair(NE // 2 - 1, last=True)
                pe.wait_ge(*J.freed(o[1]["down"], turn))
                scatter(end, turn, NE - 1, 1)
                phase()
                for s in range(2):
                    gate_rows(jb("gf") + s, diagf[s])
                phase()


_NAMES = ['x', 'c', 'ctx', 'c_ctx', 'ada_w', 'ada_b', 'norm_mix_pre', 'norm_mix_post', 'norm_ffn_pre',
          'norm_ffn_post', 'w_in', 'ssd_conv_w', 'ssd_conv_b', 'ssd_a_log', 'ssd_dt_bias', 'ssd_d', 'ssd_norm',
          'diff_lam_q1', 'diff_lam_k1', 'diff_lam_q2', 'diff_lam_k2', 'diff_subln', 'mla_q_norm', 'mla_w_q_up',
          'mla_kv_norm', 'mla_w_kv_up', 'w_out', 'router_w', 'router_b', 'w_gate', 'w_up', 'w_down']


def kernel(**inputs):
    import concourse.bacc as bacc
    from concourse.bass_utils import run_bass_kernel_spmd

    nc = bacc.Bacc("TRN2", target_bir_lowering=False, num_devices=1)
    arrays, T = {}, {}
    for name in _NAMES:
        arrays["in_" + name] = np.ascontiguousarray(inputs[name])
    arrays["in_const"] = constants()
    for name in _NAMES + ["const"]:
        T[name] = nc.dram_tensor("in_" + name, arrays["in_" + name].shape, F32, kind="ExternalInput").ap()
    out = nc.dram_tensor("out", (1, SEQ, D), F32, kind="ExternalOutput").ap()
    build(nc, T, out)
    r = run_bass_kernel_spmd(nc, [arrays], core_ids=[0])
    return r.results[0]["out"]
```

```python
import math
from contextlib import ExitStack

import numpy as np
import concourse.bass as bass
from concourse import mybir

ALU = mybir.AluOpType
ACT = mybir.ActivationFunctionType
F32 = mybir.dt.float32
U32 = mybir.dt.uint32
AX_X = mybir.AxisListType.X

P = 128
D = 1024
KD = D // P
DEPTH = 2
CTX, SEQ, GRID_W = 256, 512, 64
TOK = CTX + SEQ
NT = TOK // P
CT = CTX // P
EPS = 1e-6
SH, SP, SG, SN = 8, 64, 2, 64
HPG = SH // SG
SI = SH * SP
CONV_T = (SI + 2 * SG * SN) // P
DH, DQ, DV = 4, 32, 64
MH, MQL, MKL, MN, MR, MV = 4, 192, 128, 64, 32, 64
MQK = MN + MR
COL_Z, COL_X, COL_B = 0, SI, 2 * SI
COL_DT = COL_B + 2 * SG * SN
COL_QK = COL_DT + 2 * SH
COL_V = COL_QK + 2 * DH * DV
COL_MLA = COL_V + DH * DV
MLA_COLS = MQL + MKL + MR
NE, FF = 16, 1024
CAP_L, CAP_C = 2 * SEQ // NE, 2 * CTX // NE
BLK = 512
RING = 4
NSLOT = 4
LAYER_BLOCKS = 12 + 2 + 1 + 3 + 2 + 6 * NE
NEG = -30000.0

K_ID, K_TRU, K_TRL, K_MF, K_MB, K_ROT, K_ONE = (i * P for i in range(7))
K_COS = 7 * P
K_SIN = K_COS + SEQ
K_IOTA = K_SIN + SEQ
K_TID = K_IOTA + TOK
K_SUM = K_TID + NT
K_EPS = K_SUM + 2 * CAP_C
K_END = K_EPS + 1

R_ADAB, R_MPRE, R_FPRE, R_MPOST, R_FPOST = 0, 48, 56, 64, 72
R_CW, R_CB, R_QN, R_KVN, R_SN, R_SUB, R_C = 80, 98, 104, 106, 107, 111, 112
B_ALOG, B_DTB, B_DSK, B_RB, B_LAM, B_END = 0, 16, 32, 40, 56, 184


def constants():
    t = np.zeros((P, K_END), np.float32)
    j = np.arange(P)
    t[:, K_ID:K_ID + P] = np.eye(P)
    t[:, K_TRU:K_TRU + P] = j[:, None] <= j[None, :]
    t[:, K_TRL:K_TRL + P] = j[:, None] >= j[None, :]
    t[:, K_MF:K_MF + P] = np.where(j[:, None] <= j[None, :], 0.0, NEG)
    t[:, K_MB:K_MB + P] = np.where(j[:, None] >= j[None, :], 0.0, NEG)
    t[:, K_ONE:K_ONE + P] = 1.0
    q = DQ // 4
    inv = np.float32(10000.0) ** (-np.arange(q, dtype=np.float32) / np.float32(q))
    pos = np.arange(SEQ)
    for p in range(P):
        d = p % DQ
        where = (pos // GRID_W if d < DQ // 2 else pos % GRID_W).astype(np.float32)
        ang = where * inv[d % q]
        t[p, K_COS:K_COS + SEQ] = np.cos(ang)
        t[p, K_SIN:K_SIN + SEQ] = np.sin(ang)
        if (d // q) % 2 == 0:
            t[p + q, K_ROT + p] = -1.0
        else:
            t[p - q, K_ROT + p] = 1.0
    t[:, K_IOTA:K_IOTA + TOK] = np.arange(TOK)[None, :]
    t[:, K_TID:K_TID + NT] = j[:, None] + P * np.arange(NT)[None, :]
    t[j, K_SUM + j // (2 * CAP_C) * CAP_C + j % CAP_C] = 1.0
    t[:, K_EPS] = EPS
    return t


def query_tiles(l):
    return list(range(NT)) if l < DEPTH - 1 else list(range(CT, NT))


def spans(t):
    return ((0, CTX),) if t < CT else ((0, 512), (512, TOK))


def scatter_parts(l):
    return [(t, c, c + 512) for t in range(CT) for c in (0, 512) if l < DEPTH - 1] + [(t, 0, D) for t in range(CT, NT)]


def n_keys(t):
    return (CT if t < CT else NT) * P


def chunks():
    fwd = list(range(NT))
    bwd = list(range(CT - 1, -1, -1)) + list(range(NT - 1, CT - 1, -1))
    return [(d, c, (fwd, bwd)[d][c]) for c in range(NT) for d in range(2)]


def job_plan():
    at, n = {}, 0
    for l in range(DEPTH):
        q = len(query_tiles(l))
        for name, c in [("par", 1), ("ada", 1), ("h", NT),
                        ("qk", 4), ("v", 2), ("rot", 4), ("datt", 4 * DH * q),
                        ("mla", 3), ("mlaT", 3), ("mq", MH), ("mk", MH), ("mv", 2), ("mrot", MH + 1),
                        ("matt", 3 * MH * q),
                        ("xbc", CONV_T), ("dt", 1), ("z", 3), ("xT", NT), ("cum", 1), ("ssd", 4 * q),
                        ("rec", 2 * NT), ("gm", 2), ("out", 2 * q), ("f", 2 * q), ("aT", 1), ("idx", 3),
                        ("moe", NE // 2 * (12 + len(scatter_parts(l)))), ("gf", 2)]:
            at[l, name] = n
            n += c
    return at


def att_job(base, maps, n, u, kind, m=0):
    def start(i):
        return base + maps + i * (maps + 1) + max(0, i - 1)
    if kind == "score":
        return base + m if u == 0 else start(u - 1) + m
    if kind == "turn":
        return start(u) + (maps if u + 1 < n else 0)
    return base + n * (maps + 2) - 1 if u == n - 1 else att_job(base, maps, n, u + 1, "turn") + 1


def two_job(base, n, i, second):
    if not second:
        return base if i == 0 else base + 2 * i - 1
    return base + (2 * n - 1 if i == n - 1 else 2 * i + 2)


def ssd_job(base, n, i, k):
    if k < 3:
        return base + k if i == 0 else base + 4 * i - 1 + k
    return base + (4 * n - 1 if i == n - 1 else 4 * i + 6)


def pair_jobs(jm, nsc, i, last=False):
    first = isinstance(i, int) and i == 0
    b = jm + 2 if first else jm + 14
    turn = 0 if first else (i - 1) * ((12 + nsc) // NSLOT)
    out = []
    for p in range(2):
        o = {"gate": b, "up": b + 1}
        b += 2
        for name, n in (("take", 0 if last and p else 1), ("hidT", 1), ("takeT", 0 if last and p else 1),
                        ("scatter", 0 if first or p else nsc), ("down", 1)):
            o[name] = b
            b += n
        out.append(o)
    return out, turn, b


class Slots:

    def __init__(self, ps, s_full, s_free, first):
        self.ps, self.s_full, self.s_free, self.first = ps, s_full, s_free, first

    def tile(self, j):
        return self.ps[j % NSLOT]

    def fill(self, j):
        return self.s_full[j % NSLOT], 1

    def free(self, j):
        return self.s_free[j % NSLOT], 1

    def filled(self, j, turn=0):
        return self.s_full[j % NSLOT], turn + (j // NSLOT + 1)

    def freed(self, j, turn=0):
        return self.s_free[j % NSLOT], turn + (j // NSLOT + 1)

    def empty(self, j, turn=0):
        return (self.s_free[j % NSLOT], turn + j // NSLOT) if j >= NSLOT else self.first


class Tally:

    def __init__(self):
        self.n = {}

    def next(self, sem, k=1):
        self.n[sem.name] = self.n.get(sem.name, 0) + k
        return sem, self.n[sem.name]


N_SMALL = 1 + NT + DEPTH * (1 + 4 + 3 + 1 + 2 + 1 + 1 + 2 + 2 + 4 + 4 + 2 + 1 + 1)


def build(nc, T, out):
    JOB = job_plan()
    with ExitStack() as ctx:
        def sb(name, cols, dt=F32):
            return ctx.enter_context(nc.sbuf_tensor(name, [P, cols], dt))

        def sem(name):
            return ctx.enter_context(nc.semaphore(name))

        ring = [sb(f"ring{i}", KD * BLK) for i in range(RING)]
        X = sb("resid", NT * D)
        K = sb("const", K_END)
        wqu = sb("w_q_up", DEPTH * 2 * MH * MQK)
        wkv = sb("w_kv_up", DEPTH * MH * (MN + MV))
        wrt = sb("w_router", DEPTH * KD * NE)
        pack = sb("pack", DEPTH * P)
        par = sb("par", DEPTH * P)
        rowp = sb("rowp", DEPTH * B_END)
        sc = sb("silu_c", 2 * KD)
        mod = sb("mod", 96)
        coef = sb("coef", 64)
        fac = sb("fac", 8)
        small = sb("small", 512)
        dummy = sb("mark", 8)
        ssum, rstd = sb("ssum", 64), sb("rstd", 64)
        nmax, esum, rcol = sb("nmax", 8), sb("esum", 8), sb("rcol", 16)
        acol = sb("acol", 16)
        lam = sb("lam", 136)
        arena_cols = 22464
        A = sb("arena", arena_cols)
        ps = [ctx.enter_context(nc.psum_tensor(f"ps{i}", [P, 1024], F32)) for i in range(NSLOT)]

        ring_full = [sem(f"ring_full{i}") for i in range(RING)]
        half_used = sem("half_used")
        s_load, s_out, s_zero = sem("small_loads"), sem("out_stored"), sem("pack_zeroed")
        J = Slots(ps, [sem(f"ps_full{i}") for i in range(NSLOT)], [sem(f"ps_free{i}") for i in range(NSLOT)],
                  (s_load, 16 * N_SMALL))
        dve_step, act_step = sem("dve_step"), sem("act_step")
        dve_ph, act_ph, pool_ph = sem("dve_phase"), sem("act_phase"), sem("pool_phase")
        S = {n: sem(n) for n in [
            "silu_ready", "xn_ready", "h_ready", "lam_dots", "lam_exps", "qk_roped", "negmax", "prob_ready",
            "o_ss", "o_rstd", "lat_ss", "lat_rstd", "lat_scaled", "kr_ready", "kr_all", "q_roped",
            "conv_mid", "conv_out", "xbc_ready", "dt_neg", "dt_exp", "dt_w", "dt_ln", "neg_a", "la_ready",
            "ac_ready", "dec_exp", "w_ready", "seg_ready", "seg_exp", "mask_ready", "xw_ready", "g_ss", "g_rstd",
            "diag_ready", "m_rstd", "router_max", "router_exp", "aff_ready", "topk_ready", "bd_ready",
            "silu_turned", "sel_ready", "scat_ready", "xg_ready", "out_ready"]}

        def kc(c, n=P):
            return K[:, c:c + n]

        ident, ones, eps = kc(K_ID), kc(K_ONE), K[:, K_EPS:K_EPS + 1]

        def Xt(t):
            return X[:, t * D:(t + 1) * D]

        def ar(at, n):
            assert at + n <= arena_cols, (at, n)
            return A[:, at:at + n]

        def view(ap, **kw):
            (k, n), = kw.items()
            return ap.rearrange(f"p ({k} n) -> p {k} n", **{k: n})

        def spread(ap, n, axis, shape):
            return ap.unsqueeze(axis).to_broadcast(shape)

        hT = view(ar(0, KD * TOK), k=KD)
        a0 = KD * TOK
        matt = view(ar(a0, NT * 512), t=NT)
        a1 = a0 + NT * 512
        xn = [ar(a1 + i * D, D) for i in range(2)]
        junk = ar(a1 + 2 * D, D)
        QK = view(ar(a1, 4 * TOK), m=4)
        V = view(ar(a1 + 4 * TOK, NT * 256), t=NT)
        a2 = a1 + 4 * TOK + NT * 256
        rope_t = [ar(a2 + i * SEQ, SEQ) for i in range(2)]
        PD = [[ar(a2 + (2 * i + m) * TOK, TOK) for m in range(2)] for i in range(2)]
        PT_d = [ar(a2 + (4 + i) * TOK, TOK) for i in range(2)]
        osq = ar(a1, NT * 256)
        QT, KT = view(ar(a1, MH * TOK), h=MH), view(ar(a1 + MH * TOK, MH * TOK), h=MH)
        VM = view(ar(a1 + 2 * MH * TOK, NT * 256), t=NT)
        a3 = a1 + 2 * MH * TOK + NT * 256
        MT = view(ar(a3, NT * MLA_COLS), t=NT)
        msq = view(ar(a1, NT * (MQL + MKL)), t=NT)
        cq0, cq1, ckv = (ar(a3 + NT * MLA_COLS + i * TOK, TOK) for i in range(3))
        PM = [[ar(a3 + i * TOK, TOK)] for i in range(2)]
        PT_m = [ar(a3 + (2 + i) * TOK, TOK) for i in range(2)]
        mrope_t = ar(a3, SEQ)
        XB = view(ar(a1, CONV_T * TOK), m=CONV_T)
        XT = view(ar(a1 + CONV_T * TOK, NT * 640), t=NT)
        a4 = a1 + CONV_T * TOK + NT * 640
        ZS = view(ar(a4, NT * SI), t=NT)
        a5 = a4 + NT * SI
        HS = [ar(a5 + i * HPG * SP, HPG * SP) for i in range(2)]
        EA, ET = ar(a5 + 2 * HPG * SP, 96), ar(a5 + 2 * HPG * SP + 96, 96)
        Y = view(ar(0, NT * SI), t=NT)
        seg = [view(ar(NT * SI + i * 1024, 1024), h=SH) for i in range(3)]
        dts = [ar(NT * SI + 96 * i, 96) for i in range(6)]
        cbs = view(ar(a1, 256), g=SG)
        xdk = ytmp = ar(a1 + 256, SI)
        XW = [ar(a1 + 256 + SI + i * SI, SI) for i in range(2)]
        ysq = ar(a1, NT * SI)
        LA, DTV, AC, TOT, WJ = (small[:, i * 96:(i + 1) * 96] for i in range(5))
        mixT = [view(ar(a1 + i * D, D), k=KD) for i in range(2)]
        GB = [ar(a1 + (2 + i) * D, D) for i in range(2)]
        diag = [view(ar(a1 + (4 + i) * D, D), k=KD) for i in range(2)]
        rn, rn2 = ar(a1 + 6 * D, D), ar(a1 + 7 * D, D)
        htok = view(ar(0, NT * D), t=NT)
        Fa = view(ar(NT * D, NT * D), t=NT)
        fhT = [view(ar(NT * D + i * D, D), k=KD) for i in range(2)]
        fj = ar(NT * D + 2 * D, D)
        b0 = 2 * NT * D
        idxB = ar(b0, NE * 96)
        b1 = b0 + NE * 96
        xg = ar(b1, 768)
        hidT = ar(b1 + 768, 768)
        sg, cg, cu, hid = (ar(b1 + 1536 + i * 512, 512) for i in range(4))
        sgT = ar(b1 + 3584, 256)
        taken = ar(b1 + 3840, 1024)
        yb = view(ar(b1 + 4864, 2048), a=2)
        Sel = ar(b1 + 6912, 320)
        Sc = ar(b1 + 7232, TOK)
        aT = [ar(b1 + i * TOK, TOK) for i in range(2)]
        bd = ar(b1, NE * 96)
        aff, ex, idu, idf, gv = (ar(b1 + 2 * TOK + i * 96, 96) for i in range(5))
        slotr = ar(b1 + 2 * TOK + 480, 4 * P)
        slotc = small[:, 480:512].rearrange("p (c e) -> p c e", c=4)
        GBf = [ar(b1 + i * D, D) for i in range(2)]
        diagf = [view(ar(b1 + (2 + i) * D, D), k=KD) for i in range(2)]
        rnf = ar(b1 + 4 * D, D)

        par_l = [par[:, l * P:(l + 1) * P] for l in range(DEPTH)]
        row_l = [rowp[:, l * B_END:(l + 1) * B_END] for l in range(DEPTH)]
        mod3 = mod[:, :].rearrange("p (m s) -> p m s", s=2)
        cA, cF, cGm, cGf = (coef[:, 16 * i:16 * i + 16].rearrange("p (k s) -> p k s", s=2) for i in range(4))
        LINIT = [0.8 - 0.6 * math.exp(-0.3 * l) for l in range(DEPTH)]

        def ringv(j):
            return ring[j % RING][:, :].rearrange("p (k n) -> p k n", k=KD)

        def ringk(j):
            return ring[j % RING][:, :].rearrange("p (k n) -> p k n", k=KD // 2)

        def halves(ap, n):
            return ap.rearrange("p (c h n) -> p c h n", h=2, n=n)

        def slots_of(l):
            return CAP_L + (CAP_C if l < DEPTH - 1 else 0)

        block = ctx.enter_context(nc.Block())

        @block.sync
        def _(sp):
            n_small = [0]

            def load(dst, src):
                sp.dma_start(dst, src).then_inc(s_load, 16)
                n_small[0] += 1

            def block_used(l, b):
                if b < 11:
                    sp.wait_ge(half_used, l * (11 + 3 * NE) + b + 1)
                    return
                n = len(query_tiles(l))
                name, k = {11: ("ada", 0), 12: ("qk", 3), 13: ("v", 1), 14: ("mla", 2), 15: ("xbc", 3),
                           16: ("dt", 0), 17: ("z", 2), 18: ("out", 2 * n - 1), 19: ("out", 2 * n - 1)}[b]
                sp.wait_ge(*J.filled(JOB[l, name] + k))

            def expert_used(l, i, k, last=False):
                p, w, hf = k // 6, k % 6 // 2, k % 2
                if hf == 0:
                    sp.wait_ge(half_used, i * 6 + (l * (11 + 3 * NE) + 11 + 3 * p + w + 1))
                    return
                o, turn, _ = pair_jobs(JOB[l, "moe"], len(scatter_parts(l)), i, last)
                sp.wait_ge(*J.filled(o[p][("gate", "up", "down")[w]], turn))

            load(K[:, :], T["const"])
            for t in range(CT):
                load(Xt(t), T["ctx"][0, t * P:(t + 1) * P, :])
            for t in range(CT, NT):
                load(Xt(t), T["x"][0, (t - CT) * P:(t - CT + 1) * P, :])
            sp.wait_ge(s_zero, 1)
            for l in range(DEPTH):
                pk = pack[:, l * P:(l + 1) * P]

                def rows(at, src, n):
                    load(pk[at:at + n, :], src.rearrange("(r c) -> r c", c=P))
                rows(R_ADAB, T["ada_b"][l], 48)
                for at, nm in ((R_MPRE, "norm_mix_pre"), (R_FPRE, "norm_ffn_pre"), (R_MPOST, "norm_mix_post"),
                               (R_FPOST, "norm_ffn_post")):
                    rows(at, T[nm][l], KD)
                for w in range(3):
                    rows(R_CW + CONV_T * w, T["ssd_conv_w"][l, w], CONV_T)
                rows(R_CB, T["ssd_conv_b"][l], CONV_T)
                rows(R_QN, T["mla_q_norm"][l, 0:P], 1)
                load(pk[R_QN + 1:R_QN + 2, 0:MQL - P], T["mla_q_norm"][l:l + 1, P:MQL])
                rows(R_KVN, T["mla_kv_norm"][l], 1)
                rows(R_SN, T["ssd_norm"][l], 4)
                for i in range(2):
                    load(pk[R_SUB:R_SUB + 1, i * DV:(i + 1) * DV], T["diff_subln"][l:l + 1, :])
                rows(R_C, T["c"][0], KD)
                rows(R_C + KD, T["c_ctx"], KD)
                rw = row_l[l]
                load(rw[:, B_ALOG:B_ALOG + 16], T["ssd_a_log"][l].rearrange("a b -> (a b)").partition_broadcast(P))
                load(rw[:, B_DTB:B_DTB + 16], T["ssd_dt_bias"][l].rearrange("a b -> (a b)").partition_broadcast(P))
                load(rw[:, B_DSK:B_DSK + 8], T["ssd_d"][l].partition_broadcast(P))
                load(rw[:, B_RB:B_RB + 16], T["router_b"][l].partition_broadcast(P))
                for i, nm in enumerate(("diff_lam_q1", "diff_lam_k1", "diff_lam_q2", "diff_lam_k2")):
                    load(rw[:, B_LAM + 32 * i:B_LAM + 32 * i + 32], T[nm][l].partition_broadcast(P))
                wq = wqu[:, l * 2 * MH * MQK:(l + 1) * 2 * MH * MQK]
                load(wq[:, 0:MH * MQK], T["mla_w_q_up"][l, 0:P, :])
                load(wq[0:MQL - P, MH * MQK:2 * MH * MQK], T["mla_w_q_up"][l, P:MQL, :])
                load(wkv[:, l * 512:(l + 1) * 512], T["mla_w_kv_up"][l])
                load(view(wrt[:, l * KD * NE:(l + 1) * KD * NE], k=KD),
                     T["router_w"][l].rearrange("(k p) n -> p k n", p=P))
            assert n_small[0] == N_SMALL, n_small[0]

            for l in range(DEPTH):
                jl = l * LAYER_BLOCKS
                aw, wi, wo = (T[n][l].rearrange("(k p) n -> p k n", p=P) for n in ("ada_w", "w_in", "w_out"))
                srcs = [aw[:, :, b * BLK:(b + 1) * BLK] for b in range(12)]
                srcs += [wi[:, :, c:c + n] for c, n in ((COL_QK, 512), (COL_V, 256), (COL_MLA, MLA_COLS), (COL_X, 512),
                                                        (COL_B, 272), (COL_Z, 512))]
                srcs += [wo[:, :, b * BLK:(b + 1) * BLK] for b in range(2)]
                for b, src in enumerate(srcs):
                    if b >= RING:
                        block_used(l, b - RING)
                    elif l:
                        expert_used(l - 1, NE // 2 - 1, 8 + b, last=True)
                    sp.dma_start(ringv(jl + b)[:, :, 0:src.shape[2]], src).then_inc(ring_full[(jl + b) % RING], 16)
                gud = [T[n].rearrange("l e (k p) n -> (l e) p k n", p=P) for n in ("w_gate", "w_up", "w_down")]

                def pair_loads(i, before):
                    for k in range(12):
                        p, w, hf = k // 6, k % 6 // 2, k % 2
                        before(k)
                        e = i * 2 + (l * NE + p)
                        src = gud[w][e] if isinstance(i, int) else gud[w][bass.ds(e, 1)][0]
                        sp.dma_start(ringk(k), src[:, 4 * hf:4 * hf + 4, :]).then_inc(ring_full[k % RING], 16)

                pair_loads(0, lambda k: block_used(l, 16 + k) if k < RING else expert_used(l, 0, k - RING))
                pair_loads(1, lambda k: expert_used(l, 0, 8 + k) if k < RING else expert_used(l, 1, k - RING))
                with sp.Fori(2, NE // 2) as i:
                    pair_loads(i, lambda k: expert_used(l, i - 1, 8 + k) if k < RING else expert_used(l, i, k - RING))
            for t in range(CT, NT):
                sp.wait_ge(S["out_ready"], t - CT + 1)
                sp.dma_start(out[0, (t - CT) * P:(t - CT + 1) * P, :], Xt(t)).then_inc(s_out, 16)
            sp.wait_ge(s_out, 16 * (NT - CT))

        @block.gpsimd
        def _(pool):
            g = Tally()
            pool.memset(pack[:, :], 0.0).then_inc(s_zero, 1)

            def phase():
                pool.memset(dummy[0:1, 0:1], 0.0).then_inc(pool_ph, 1)
                for s in (pool_ph, dve_ph, act_ph):
                    pool.wait_ge(*g.next(s))

            for l in range(DEPTH):
                phase()
                phase()
                pool.wait_ge(*g.next(S["kr_ready"]))
                for h in range(1, MH):
                    pool.tensor_copy(KT[MN:MQK, h, :], KT[MN:MQK, 0, :]).then_inc(S["kr_all"], 1)
                phase()
                pool.wait_ge(*g.next(S["w_ready"]))
                pool.wait_ge(*J.freed(JOB[l, "xT"] + NT - 1))
                for n, (d, c, t) in enumerate(chunks()):
                    if n >= 2:
                        pool.wait_ge(*J.filled(JOB[l, "rec"] + n - 2))
                    w = WJ[:, t * 16 + d * 8:t * 16 + d * 8 + 8]
                    pool.tensor_tensor(view(XW[n % 2], h=SH), view(XT[:, t, 0:SI], h=SH),
                                       w.unsqueeze(2).to_broadcast([P, SH, SP]), ALU.mult).then_inc(S["xw_ready"], 1)
                for _ in range(5):
                    phase()

        @block.scalar
        def _(act):
            a = Tally()
            act.wait_ge(s_load, 16 * N_SMALL)

            def phase():
                act.activation(dummy[0:1, 1:2], K[0:1, 0:1], ACT.Copy).then_inc(act_ph, 1)
                for s in (act_ph, dve_ph, pool_ph):
                    act.wait_ge(*a.next(s))

            def rsqrt(dst, src, n_feat, signal):
                act.activation(dst, src, ACT.Ln, bias=eps, scale=1.0 / n_feat).then_inc(act_step, 1)
                act.wait_ge(*a.next(act_step))
                act.activation(dst, dst, ACT.Exp, scale=-0.5).then_inc(signal, 1)

            def copy_out(dst, src, j, func=ACT.Copy, scale=1.0):
                act.wait_ge(*J.filled(j))
                act.activation(dst, src, func, scale=scale).then_inc(*J.free(j))

            def norm_tiles(tiles, out_of, junk_, turned):
                for t in tiles:
                    act.activation(junk_, Xt(t), ACT.Square, accum_out=ssum[:, t:t + 1]).then_inc(act_step, 1)
                    act.wait_ge(*a.next(act_step))
                r = slice(tiles[0], NT)
                act.activation(rstd[:, r], ssum[:, r], ACT.Ln, bias=eps, scale=1.0 / D).then_inc(act_step, 1)
                act.wait_ge(*a.next(act_step))
                act.activation(rstd[:, r], rstd[:, r], ACT.Exp, scale=-0.5).then_inc(act_step, 1)
                act.wait_ge(*a.next(act_step))
                for i, t in enumerate(tiles):
                    if turned is not None and i >= 2:
                        act.wait_ge(*J.filled(turned + i - 2))
                    act.activation(out_of(i, t), Xt(t), ACT.Copy, scale=rstd[:, t:t + 1]).then_inc(S["xn_ready"], 1)

            def softmax(l, heads, base, maps, P_of, PT_of):
                units = [(h, t) for h in range(heads) for t in query_tiles(l)]
                n = len(units)
                for i in range(n + 1):
                    if i < n:
                        nk = n_keys(units[i][1])
                        if i >= 2:
                            act.wait_ge(*J.filled(att_job(base, maps, n, i - 2, "turn")))
                        for m in range(maps):
                            j = att_job(base, maps, n, i, "score", m)
                            act.wait_ge(*a.next(S["negmax"]))
                            c = 2 * (i % 2) + m
                            act.activation(P_of[i % 2][m][:, 0:nk], J.tile(j)[:, 0:nk], ACT.Exp,
                                           bias=nmax[:, c:c + 1], accum_out=esum[:, c:c + 1]).then_inc(*J.free(j))
                    if i >= 1:
                        u = i - 1
                        nk = n_keys(units[u][1])
                        if u >= 2:
                            act.wait_ge(*J.filled(att_job(base, maps, n, u - 2, "value")))
                        j = att_job(base, maps, n, u, "turn")
                        copy_out(PT_of[u % 2][:, 0:nk], J.tile(j)[:, 0:nk], j)

            for l in range(DEPTH):
                def jb(n):
                    return JOB[l, n]
                rw, pc, q = row_l[l], par_l[l], query_tiles(l)
                nq, ns, nsc = len(q), slots_of(l), len(scatter_parts(l))
                ctx_on = l < DEPTH - 1
                nb = 2 if ctx_on else 1
                act.wait_ge(*J.freed(jb("par")))
                act.activation(sc[:, :], pc[:, R_C:R_C + 16], ACT.Silu).then_inc(S["silu_ready"], 1)
                norm_tiles(range(NT), lambda i, t: xn[i % 2], junk, jb("h"))
                phase()

                act.wait_ge(*a.next(S["lam_dots"]))
                act.activation(lam[:, 132:134], lam[:, 128:130], ACT.Exp).then_inc(S["lam_exps"], 1)
                for m in range(4):
                    copy_out(QK[:, m, :], J.tile(jb("qk") + m)[:, 0:TOK], jb("qk") + m, scale=DQ ** -0.5 if m < 2 else 1.0)
                for i, (t0, n) in enumerate(((0, 4), (4, 2))):
                    copy_out(V[:, t0:t0 + n, :].rearrange("p t n -> p (t n)"), J.tile(jb("v") + i)[:, 0:256 * n], jb("v") + i)
                softmax(l, DH, jb("datt"), 2, PD, PT_d)
                act.wait_ge(*a.next(S["o_ss"]))
                rsqrt(rstd[:, 4 * q[0]:4 * NT], ssum[:, 4 * q[0]:4 * NT], DV, S["o_rstd"])
                phase()

                for i in range(3):
                    j = jb("mla") + i
                    copy_out(MT[:, 2 * i:2 * i + 2, :],
                             J.tile(j)[:, :].rearrange("p (b n) -> p b n", b=2)[:, :, 0:MLA_COLS], j)
                act.wait_ge(*a.next(S["lat_ss"]))
                act.activation(rstd[:, 0:NT], ssum[:, 0:NT], ACT.Ln, bias=eps, scale=1.0 / MQL)
                act.activation(rstd[:, 8:8 + NT], ssum[:, 8:8 + NT], ACT.Ln, bias=eps, scale=1.0 / MKL).then_inc(act_step, 1)
                act.wait_ge(*a.next(act_step))
                act.activation(rstd[:, 0:NT], rstd[:, 0:NT], ACT.Exp, scale=-0.5)
                act.activation(rstd[:, 8:8 + NT], rstd[:, 8:8 + NT], ACT.Exp, scale=-0.5).then_inc(S["lat_rstd"], 1)
                for i in range(3):
                    j = jb("mlaT") + i
                    act.wait_ge(*J.filled(j))
                    v4 = J.tile(j)[:, :].rearrange("p (b q n) -> p b q n", b=2, q=4)
                    for s, (dst, r0, r1, col) in enumerate(((cq0, 0, P, R_QN), (cq1, 0, MQL - P, R_QN + 1),
                                                            (ckv, 0, P, R_KVN), (KT[:, 0, :], MN, MQK, None))):
                        ins = act.activation(dst[r0:r1, i * 256:i * 256 + 256].rearrange("p (b n) -> p b n", b=2),
                                             v4[r0:r1, :, s, :], ACT.Copy,
                                             scale=1.0 if col is None else pc[r0:r1, col:col + 1])
                    ins.then_inc(*J.free(j))
                for h in range(MH):
                    copy_out(QT[0:MQK, h, :], J.tile(jb("mq") + h)[0:MQK, 0:TOK], jb("mq") + h, scale=MQK ** -0.5)
                for h in range(MH):
                    copy_out(KT[0:MN, h, :], J.tile(jb("mk") + h)[0:MN, 0:TOK], jb("mk") + h)
                for i, (t0, n) in enumerate(((0, 4), (4, 2))):
                    copy_out(VM[:, t0:t0 + n, :].rearrange("p t n -> p (t n)"), J.tile(jb("mv") + i)[:, 0:256 * n],
                             jb("mv") + i)
                softmax(l, MH, jb("matt"), 1, PM, PT_m)
                phase()

                for m in range(CONV_T + 1):
                    if m < CONV_T:
                        j = jb("xbc") + m
                        act.wait_ge(*J.filled(j))
                        act.activation(XB[:, m, :], J.tile(j)[:, 0:TOK], ACT.Identity, bias=pc[:, R_CB + m:R_CB + m + 1],
                                       scale=pc[:, R_CW + CONV_T + m:R_CW + CONV_T + m + 1]).then_inc(S["conv_mid"], 1)
                    if m >= 1:
                        act.wait_ge(*J.freed(jb("xbc") + m - 1))
                        act.activation(XB[:, m - 1, :], XB[:, m - 1, :], ACT.Silu).then_inc(S["xbc_ready"], 1)
                for i in range(3):
                    copy_out(ZS[:, 2 * i:2 * i + 2, :].rearrange("p t n -> p (t n)"), J.tile(jb("z") + i)[:, :],
                             jb("z") + i, func=ACT.Silu)
                for t in range(NT):
                    copy_out(XT[:, t, :], J.tile(jb("xT") + t)[:, 0:640], jb("xT") + t)
                act.wait_ge(*a.next(S["dt_neg"]))
                act.activation(dts[1], dts[1], ACT.Exp).then_inc(S["dt_exp"], 1)
                act.activation(acol[:, 0:16], rw[:, B_ALOG:B_ALOG + 16], ACT.Exp).then_inc(S["neg_a"], 1)
                act.wait_ge(*a.next(S["dt_w"]))
                act.activation(dts[3], dts[2], ACT.Ln).then_inc(S["dt_ln"], 1)
                act.wait_ge(*a.next(S["ac_ready"]))
                act.activation(WJ, WJ, ACT.Exp)
                act.activation(EA, AC, ACT.Exp)
                act.activation(ET, TOT, ACT.Exp).then_inc(S["dec_exp"], 1)
                for i in range(nq):
                    for d in range(2):
                        act.wait_ge(*a.next(S["seg_ready"]))
                        act.activation(seg[d], seg[d], ACT.Exp).then_inc(S["seg_exp"], 1)
                act.wait_ge(*a.next(S["g_ss"]))
                rsqrt(rstd[:, 2 * q[0]:2 * NT], ssum[:, 2 * q[0]:2 * NT], SI // SG, S["g_rstd"])
                phase()

                for s in range(2):
                    copy_out(GB[s], J.tile(jb("gm") + s)[:, :], jb("gm") + s)
                for i, t in enumerate(q):
                    j = two_job(jb("out"), nq, i, True)
                    act.wait_ge(*J.filled(j))
                    act.activation(rn, J.tile(j)[:, :], ACT.Square, accum_out=ssum[:, t:t + 1]).then_inc(act_step, 1)
                    act.wait_ge(*a.next(act_step))
                    rsqrt(rstd[:, t:t + 1], ssum[:, t:t + 1], D, S["m_rstd"])
                phase()

                norm_tiles(q, lambda i, t: htok[:, t, :], fj, None)
                act.wait_ge(*a.next(S["router_max"]))
                act.activation(ex, ex, ACT.Exp).then_inc(S["router_exp"], 1)
                w = NE * ns // 2
                for i in range(2):
                    copy_out(idxB[:, i * w:(i + 1) * w], J.tile(jb("idx") + i)[:, 0:w], jb("idx") + i)
                phase()

                def pair(i, last=False):
                    o, turn, _ = pair_jobs(jb("moe"), nsc, i, last)
                    before, b_turn, _ = pair_jobs(jb("moe"), nsc, i - 1) if not (isinstance(i, int) and i == 0) \
                        else (None, 0, 0)
                    for p in range(2):
                        act.wait_ge(*J.filled(o[p]["gate"], turn))
                        if p:
                            act.wait_ge(*J.freed(o[0]["up"], turn))
                            act.wait_ge(*J.filled(o[0]["hidT"], turn))
                        elif before:
                            act.wait_ge(*J.freed(before[1]["up"], b_turn))
                            act.wait_ge(*J.filled(before[1]["hidT"], b_turn))
                        t_ = J.tile(o[p]["gate"])
                        ins = act.activation(sg, t_[:, 0:512], ACT.Silu)
                        if ctx_on:
                            ins = act.activation(cg, t_[:, 512:1024], ACT.Copy)
                        ins.then_inc(*J.free(o[p]["gate"]))
                        if not (last and p):
                            take(o[p]["take"], turn)
                        act.wait_ge(*J.filled(o[p]["hidT"], turn))
                        t_ = J.tile(o[p]["hidT"])
                        if ctx_on:
                            if p:
                                act.wait_ge(*J.freed(o[0]["hidT"], turn))
                            elif before:
                                act.wait_ge(*J.freed(before[1]["hidT"], b_turn))
                            act.activation(hidT[:, 0:512], t_[:, 0:512], ACT.Copy)
                            act.activation(sgT, t_[:, 512:768], ACT.Silu).then_inc(S["silu_turned"], 1)
                        else:
                            act.activation(hidT[:, 0:512], t_[:, 0:512], ACT.Copy).then_inc(*J.free(o[p]["hidT"]))
                        act.wait_ge(*J.filled(o[p]["down"], turn))
                        for hf in range(2):
                            ins = act.activation(yb[p * 64:p * 64 + 64, 0:nb, hf * 512:hf * 512 + 512],
                                                 J.tile(o[p]["down"])[hf * 64:hf * 64 + 64, 0:nb * 512]
                                                 .rearrange("p (a n) -> p a n", a=nb), ACT.Copy)
                        ins.then_inc(*J.free(o[p]["down"]))

                def take(j, turn):
                    act.wait_ge(*J.filled(j, turn))
                    act.activation(taken[:, 0:nb * 512], J.tile(j)[:, 0:nb * 512], ACT.Copy).then_inc(*J.free(j))

                take(jb("moe"), 0)
                pair(0)
                pair(1)
                with act.Fori(2, NE // 2 - 1) as i:
                    pair(i)
                pair(NE // 2 - 1, last=True)
                phase()

                for s in range(2):
                    copy_out(GBf[s], J.tile(jb("gf") + s)[:, :], jb("gf") + s)
                for t in q:
                    act.activation(rnf, Fa[:, t, :], ACT.Square, accum_out=ssum[:, t:t + 1]).then_inc(act_step, 1)
                    act.wait_ge(*a.next(act_step))
                    rsqrt(rstd[:, t:t + 1], ssum[:, t:t + 1], D, S["m_rstd"])
                phase()

        @block.vector
        def _(dve):
            v = Tally()
            dve.wait_ge(s_load, 16 * N_SMALL)
            TT = dve.tensor_tensor

            def phase():
                dve.memset(dummy[0:1, 4:5], 0.0).then_inc(dve_ph, 1)
                for s in (dve_ph, act_ph, pool_ph):
                    dve.wait_ge(*v.next(s))

            def modulate(dst, j, c_scale, c_shift, s):
                dve.wait_ge(*J.filled(j))
                TT(dst, view(J.tile(j)[:, :], k=KD), c_scale[:, :, s].unsqueeze(2).to_broadcast([P, KD, P]),
                   ALU.mult).then_inc(*J.free(j))
                dve.wait_ge(*J.freed(j))
                return TT(dst, dst, c_shift[:, :, s].unsqueeze(2).to_broadcast([P, KD, P]), ALU.add)

            def attend(l, base, maps, heads, weigh, finish):
                units = [(h, t) for h in range(heads) for t in query_tiles(l)]
                n = len(units)
                for i in range(n + 2):
                    if i < n:
                        nk = n_keys(units[i][1])
                        for m in range(maps):
                            j = att_job(base, maps, n, i, "score", m)
                            dve.wait_ge(*J.filled(j))
                            if i >= 2:
                                dve.wait_ge(*J.freed(att_job(base, maps, n, i - 2, "score", m)))
                            c = 2 * (i % 2) + m
                            dve.tensor_reduce(nmax[:, c:c + 1], J.tile(j)[:, 0:nk], AX_X, ALU.max,
                                              negate=True).then_inc(S["negmax"], 1)
                    if 1 <= i <= n:
                        for m in range(maps):
                            dve.wait_ge(*J.freed(att_job(base, maps, n, i - 1, "score", m)))
                        if i >= 3:
                            dve.wait_ge(*J.freed(att_job(base, maps, n, i - 3, "value")))
                        weigh(i - 1, n_keys(units[i - 1][1]))
                    if i >= 2:
                        h, t = units[i - 2]
                        j = att_job(base, maps, n, i - 2, "value")
                        dve.wait_ge(*J.filled(j))
                        finish(i - 2, h, t, j)

            for l in range(DEPTH):
                def jb(n):
                    return JOB[l, n]
                rw, pc, q = row_l[l], par_l[l], query_tiles(l)
                nq, ns, t0, nsc = len(q), slots_of(l), q[0], len(scatter_parts(l))
                ctx_on = l < DEPTH - 1
                j = jb("par")
                dve.wait_ge(*J.filled(j))
                dve.tensor_copy(pc, J.tile(j)[:, 0:P]).then_inc(*J.free(j))
                dve.wait_ge(*J.freed(j))
                dve.tensor_copy(fac[:, 0:4], pc[:, R_SN:R_SN + 4])
                for i in range(2):
                    dve.tensor_scalar(fac[:, 4 + i:5 + i], pc[:, R_SUB:R_SUB + 1], 1.0 - LINIT[l], None, ALU.mult)
                dve.memset(fac[:, 6:8], 1.0)
                j = jb("ada")
                dve.wait_ge(*J.filled(j))
                TT(mod3, J.tile(j)[:, 0:96].rearrange("p (m s) -> p m s", s=2),
                   pc[:, R_ADAB:R_ADAB + 48].unsqueeze(2).to_broadcast([P, 48, 2]), ALU.add).then_inc(*J.free(j))
                dve.wait_ge(*J.freed(j))
                for dst, m0, col, one in ((cF, 32, R_FPRE, 1.0), (cGm, 16, R_MPOST, 0.0), (cGf, 40, R_FPOST, 0.0),
                                          (cA, 8, R_MPRE, 1.0)):
                    ins = dve.scalar_tensor_tensor(dst, mod3[:, m0:m0 + 8, :], one,
                                                   pc[:, col:col + 8].unsqueeze(2).to_broadcast([P, KD, 2]),
                                                   ALU.add, ALU.mult)
                ins.then_inc(dve_step, 1)
                dve.wait_ge(*v.next(dve_step))
                for t in range(NT):
                    modulate(hT[:, :, t * P:(t + 1) * P], jb("h") + t, cA, mod3[:, 0:8, :],
                             1 if t < CT else 0).then_inc(S["h_ready"], 1)
                phase()

                for i in range(2):
                    c = B_LAM + 64 * i
                    ins = TT(lam[:, 32 * i:32 * i + 32], rw[:, c:c + 32], rw[:, c + 32:c + 64], ALU.mult)
                ins.then_inc(dve_step, 1)
                dve.wait_ge(*v.next(dve_step))
                dve.tensor_reduce(lam[:, 128:130], view(lam[:, 0:64], a=2), AX_X, ALU.add).then_inc(S["lam_dots"], 1)
                dve.wait_ge(*v.next(S["lam_exps"]))
                TT(lam[:, 134:135], lam[:, 133:134], lam[:, 132:133], ALU.subtract).then_inc(dve_step, 1)
                dve.wait_ge(*v.next(dve_step))
                dve.tensor_scalar(lam[:, 135:136], lam[:, 134:135], -LINIT[l], None, ALU.add).then_inc(dve_step, 1)
                dve.wait_ge(*v.next(dve_step))
                for m in range(4):
                    dve.wait_ge(*J.freed(jb("qk") + m))
                    lat = QK[:, m, CTX:TOK]
                    TT(rope_t[0], lat, kc(K_COS, SEQ), ALU.mult)
                    j = jb("rot") + m
                    dve.wait_ge(*J.filled(j))
                    TT(rope_t[1], J.tile(j)[:, 0:SEQ], kc(K_SIN, SEQ), ALU.mult).then_inc(*J.free(j))
                    dve.wait_ge(*J.freed(j))
                    TT(lat, rope_t[0], rope_t[1], ALU.add).then_inc(S["qk_roped"], 1)
                    dve.wait_ge(*v.next(S["qk_roped"]))

                def diff_weigh(u, nk):
                    c = 2 * (u % 2)
                    dve.reciprocal(rcol[:, c:c + 2], esum[:, c:c + 2]).then_inc(dve_step, 1)
                    dve.wait_ge(*v.next(dve_step))
                    dve.scalar_tensor_tensor(rcol[:, 8 + c:9 + c], esum[:, c:c + 1], lam[:, 135:136],
                                             rcol[:, c + 1:c + 2], ALU.mult, ALU.mult).then_inc(dve_step, 1)
                    dve.wait_ge(*v.next(dve_step))
                    p1, p2 = PD[u % 2]
                    dve.scalar_tensor_tensor(p1[:, 0:nk], p2[:, 0:nk], rcol[:, 8 + c:9 + c], p1[:, 0:nk],
                                             ALU.mult, ALU.add).then_inc(S["prob_ready"], 1)

                def diff_finish(u, h, t, j):
                    dve.tensor_scalar(matt[:, t, h * DV:(h + 1) * DV], J.tile(j)[:, 0:DV],
                                      rcol[:, 2 * (u % 2):2 * (u % 2) + 1], None, ALU.mult).then_inc(*J.free(j))

                attend(l, jb("datt"), 2, DH, diff_weigh, diff_finish)
                dve.wait_ge(*J.freed(att_job(jb("datt"), 2, DH * nq, DH * nq - 1, "value")))
                TT(view(osq[:, 0:nq * 256], t=nq), matt[:, t0:NT, 0:256], matt[:, t0:NT, 0:256], ALU.mult).then_inc(dve_step, 1)
                dve.wait_ge(*v.next(dve_step))
                dve.tensor_reduce(ssum[:, 4 * t0:4 * NT], osq[:, 0:nq * 256].rearrange("p (a n) -> p a n", n=DV),
                                  AX_X, ALU.add).then_inc(S["o_ss"], 1)
                dve.wait_ge(*v.next(S["o_rstd"]))
                for t in q:
                    o = matt[:, t, 0:256].rearrange("p (h n) -> p h n", h=DH)
                    TT(o, o, rstd[:, 4 * t:4 * t + 4].unsqueeze(2).to_broadcast([P, DH, DV]), ALU.mult)
                phase()

                for i in range(3):
                    dve.wait_ge(*J.freed(jb("mla") + i))
                TT(msq, MT[:, :, 0:MQL + MKL], MT[:, :, 0:MQL + MKL], ALU.mult).then_inc(dve_step, 1)
                dve.wait_ge(*v.next(dve_step))
                dve.tensor_reduce(ssum[:, 0:NT], msq[:, :, 0:MQL], AX_X, ALU.add)
                dve.tensor_reduce(ssum[:, 8:8 + NT], msq[:, :, MQL:MQL + MKL], AX_X, ALU.add).then_inc(S["lat_ss"], 1)
                dve.wait_ge(*v.next(S["lat_rstd"]))
                TT(MT[:, :, 0:MQL], MT[:, :, 0:MQL], rstd[:, 0:NT].unsqueeze(2).to_broadcast([P, NT, MQL]), ALU.mult)
                TT(MT[:, :, MQL:MQL + MKL], MT[:, :, MQL:MQL + MKL],
                   rstd[:, 8:8 + NT].unsqueeze(2).to_broadcast([P, NT, MKL]), ALU.mult).then_inc(S["lat_scaled"], 1)
                R = slice(MN, MQK)
                for h in range(MH + 1):
                    if h == 0:
                        dve.wait_ge(*J.freed(jb("mlaT") + 2))
                    else:
                        dve.wait_ge(*J.freed(jb("mq") + h - 1))
                    lat = KT[R, 0, CTX:TOK] if h == 0 else QT[R, h - 1, CTX:TOK]
                    j = jb("mrot") + h
                    dve.wait_ge(*J.filled(j))
                    TT(mrope_t[R, :], lat, K[R, K_COS:K_COS + SEQ], ALU.mult).then_inc(dve_step, 1)
                    dve.wait_ge(*v.next(dve_step))
                    TT(lat, J.tile(j)[R, 0:SEQ], K[R, K_SIN:K_SIN + SEQ], ALU.mult).then_inc(*J.free(j))
                    dve.wait_ge(*J.freed(j))
                    ins = TT(lat, lat, mrope_t[R, :], ALU.add)
                    ins.then_inc(S["kr_ready"] if h == 0 else S["q_roped"], 1)
                    dve.wait_ge(*v.next(S["kr_ready"] if h == 0 else S["q_roped"]))

                def mla_weigh(u, nk):
                    c = 2 * (u % 2)
                    dve.reciprocal(rcol[:, c:c + 1], esum[:, c:c + 1]).then_inc(S["prob_ready"], 1)

                def mla_finish(u, h, t, j):
                    dve.tensor_scalar(matt[:, t, 256 + h * MV:256 + (h + 1) * MV], J.tile(j)[:, 0:MV],
                                      rcol[:, 2 * (u % 2):2 * (u % 2) + 1], None, ALU.mult).then_inc(*J.free(j))

                attend(l, jb("matt"), 1, MH, mla_weigh, mla_finish)
                phase()

                for m in range(CONV_T):
                    j = jb("xbc") + m
                    dve.wait_ge(*v.next(S["conv_mid"]))
                    src, dst = J.tile(j), XB[:, m, :]
                    for tap, sh in ((0, -1), (2, 1)):
                        w = pc[:, R_CW + tap * CONV_T + m:R_CW + tap * CONV_T + m + 1]
                        for s0, s1 in ((0, CTX), (CTX, TOK)):
                            lo, hi = (s0 + 1, s1) if sh < 0 else (s0, s1 - 1)
                            ins = dve.scalar_tensor_tensor(dst[:, lo:hi], src[:, lo + sh:hi + sh], w, dst[:, lo:hi],
                                                           ALU.mult, ALU.add)
                        if sh < 0:
                            ins.then_inc(dve_step, 1)
                            dve.wait_ge(*v.next(dve_step))
                    ins.then_inc(*J.free(j))
                j = jb("dt")
                dve.wait_ge(*J.filled(j))
                dve.wait_ge(*J.filled(jb("z") + 2))
                TT(view(dts[0], t=NT), view(J.tile(j)[:, 0:96], t=NT),
                   rw[:, B_DTB:B_DTB + 16].unsqueeze(1).to_broadcast([P, NT, 16]), ALU.add).then_inc(*J.free(j))
                dve.wait_ge(*J.freed(j))
                dve.scalar_tensor_tensor(dts[1], dts[0], -1.0, dts[0], ALU.mult, ALU.min).then_inc(S["dt_neg"], 1)
                dve.wait_ge(*v.next(S["dt_exp"]))
                dve.tensor_scalar(dts[2], dts[1], 1.0, None, ALU.add).then_inc(S["dt_w"], 1)
                dve.wait_ge(*v.next(S["dt_ln"]))
                dve.tensor_scalar(dts[4], dts[2], 1.0, 1e-30, ALU.subtract, ALU.max).then_inc(dve_step, 1)
                dve.wait_ge(*v.next(dve_step))
                dve.reciprocal(dts[5], dts[4]).then_inc(dve_step, 1)
                dve.wait_ge(*v.next(dve_step))
                TT(dts[5], dts[5], dts[1], ALU.mult).then_inc(dve_step, 1)
                dve.wait_ge(*v.next(dve_step))
                TT(dts[3], dts[3], dts[5], ALU.mult).then_inc(dve_step, 1)
                dve.wait_ge(*v.next(dve_step))
                dve.tensor_scalar(dts[4], dts[2], 1.0, None, ALU.is_equal).then_inc(dve_step, 1)
                dve.wait_ge(*v.next(dve_step))
                TT(dts[4], dts[4], dts[1], ALU.mult).then_inc(dve_step, 1)
                dve.wait_ge(*v.next(dve_step))
                TT(dts[3], dts[3], dts[4], ALU.add).then_inc(dve_step, 1)
                dve.wait_ge(*v.next(dve_step))
                dve.scalar_tensor_tensor(DTV, dts[0], 0.0, dts[3], ALU.max, ALU.add).then_inc(dve_step, 1)
                dve.wait_ge(*v.next(dve_step))
                dve.wait_ge(*v.next(S["neg_a"]))
                dve.scalar_tensor_tensor(view(LA, t=NT), view(DTV, t=NT), -1.0,
                                         acol[:, 0:16].unsqueeze(1).to_broadcast([P, NT, 16]),
                                         ALU.mult, ALU.mult).then_inc(S["la_ready"], 1)
                j = jb("cum")
                dve.wait_ge(*J.filled(j))
                ac4 = AC.rearrange("p (t d n) -> p t d n", t=NT, d=2)
                for d in range(2):
                    dve.tensor_copy(ac4[:, :, d, :], view(J.tile(j)[:, 48 * d:48 * d + 48], t=NT))
                dve.tensor_copy(TOT, J.tile(j)[:, 96:192]).then_inc(*J.free(j))
                dve.wait_ge(*J.freed(j))
                TT(WJ, TOT, AC, ALU.subtract).then_inc(S["ac_ready"], 1)
                dve.wait_ge(*v.next(S["dec_exp"]))
                TT(WJ, WJ, DTV, ALU.mult).then_inc(S["w_ready"], 1)
                for t in range(NT):
                    dve.wait_ge(*J.freed(jb("xT") + t))
                for i, t in enumerate(q):
                    sj = [ssd_job(jb("ssd"), nq, i, k) for k in range(4)]
                    dve.wait_ge(*J.filled(sj[0]))
                    dve.tensor_copy(cbs, view(J.tile(sj[0])[:, :], g=SG)[:, :, 0:P]).then_inc(*J.free(sj[0]))
                    dve.wait_ge(*J.freed(sj[0]))
                    for d in range(2):
                        dve.wait_ge(*J.filled(sj[1 + d]))
                        ac = AC[:, t * 16 + 8 * d:t * 16 + 8 * d + 8].unsqueeze(2).to_broadcast([P, SH, P])
                        TT(seg[d], view(J.tile(sj[1 + d])[:, :], h=SH), ac, ALU.subtract).then_inc(*J.free(sj[1 + d]))
                        dve.wait_ge(*J.freed(sj[1 + d]))
                        mk = kc(K_MF if d == 0 else K_MB).unsqueeze(1).to_broadcast([P, SH, P])
                        TT(seg[d], seg[d], mk, ALU.min).then_inc(S["seg_ready"], 1)
                    for d in range(2):
                        dve.wait_ge(*v.next(S["seg_exp"]))
                        dt_ = DTV[:, t * 16 + 8 * d:t * 16 + 8 * d + 8].unsqueeze(2).to_broadcast([P, SH, P])
                        TT(seg[d], seg[d], dt_, ALU.mult).then_inc(dve_step, 1)
                        dve.wait_ge(*v.next(dve_step))
                    TT(seg[2], seg[0], seg[1], ALU.add).then_inc(dve_step, 1)
                    dve.wait_ge(*v.next(dve_step))
                    for g in range(SG):
                        hs = slice(g * HPG, (g + 1) * HPG)
                        ins = TT(seg[2][:, hs, :], seg[2][:, hs, :], cbs[:, g, :].unsqueeze(1).to_broadcast([P, HPG, P]),
                                 ALU.mult)
                    ins.then_inc(S["mask_ready"], 1)
                    TT(view(xdk, h=SH), view(XT[:, t, 0:SI], h=SH),
                       rw[:, B_DSK:B_DSK + 8].unsqueeze(2).to_broadcast([P, SH, SP]), ALU.mult).then_inc(dve_step, 1)
                    dve.wait_ge(*v.next(dve_step))
                    dve.wait_ge(*J.filled(sj[3]))
                    TT(Y[:, t, :], J.tile(sj[3])[:, 0:SI], xdk, ALU.add).then_inc(*J.free(sj[3]))
                dve.wait_ge(*J.freed(ssd_job(jb("ssd"), nq, nq - 1, 3)))
                for n, (d, c, t) in enumerate(chunks()):
                    j = jb("rec") + n
                    dve.wait_ge(*J.filled(j))
                    if c and t in q:
                        ea = EA[:, t * 16 + 8 * d:t * 16 + 8 * d + 8].rearrange("p (g h) -> p g h", g=SG)
                        TT(ytmp.rearrange("p (g h n) -> p g h n", g=SG, h=HPG),
                           view(J.tile(j)[:, :], g=SG)[:, :, 0:256].rearrange("p g (h n) -> p g h n", h=HPG),
                           ea.unsqueeze(3).to_broadcast([P, SG, HPG, SP]), ALU.mult).then_inc(dve_step, 1)
                        dve.wait_ge(*v.next(dve_step))
                        TT(Y[:, t, :], Y[:, t, :], ytmp, ALU.add).then_inc(dve_step, 1)
                        dve.wait_ge(*v.next(dve_step))
                    if c:
                        for g in range(SG):
                            et = ET[g * SN:(g + 1) * SN, t * 16 + 8 * d + g * HPG:t * 16 + 8 * d + (g + 1) * HPG]
                            hv = view(HS[d][g * SN:(g + 1) * SN, :], h=HPG)
                            ins = TT(hv, hv, et.unsqueeze(2).to_broadcast([SN, HPG, SP]), ALU.mult)
                        ins.then_inc(dve_step, 1)
                        dve.wait_ge(*v.next(dve_step))
                        TT(HS[d], HS[d], J.tile(j)[:, 768:1024], ALU.add).then_inc(*J.free(j))
                        dve.wait_ge(*J.freed(j))
                    else:
                        dve.tensor_copy(HS[d], J.tile(j)[:, 768:1024]).then_inc(*J.free(j))
                        dve.wait_ge(*J.freed(j))
                TT(Y[:, t0:NT, :], Y[:, t0:NT, :], ZS[:, t0:NT, :], ALU.mult).then_inc(dve_step, 1)
                dve.wait_ge(*v.next(dve_step))
                TT(view(ysq[:, 0:nq * SI], t=nq), Y[:, t0:NT, :], Y[:, t0:NT, :], ALU.mult).then_inc(dve_step, 1)
                dve.wait_ge(*v.next(dve_step))
                dve.tensor_reduce(ssum[:, 2 * t0:2 * NT], ysq[:, 0:nq * SI].rearrange("p (a n) -> p a n", n=SI // SG),
                                  AX_X, ALU.add).then_inc(S["g_ss"], 1)
                dve.wait_ge(*v.next(S["g_rstd"]))
                for t in q:
                    y3 = view(Y[:, t, :], g=SG)
                    TT(y3, y3, rstd[:, 2 * t:2 * t + 2].unsqueeze(2).to_broadcast([P, SG, SI // SG]), ALU.mult)
                phase()

                for s in range(2):
                    TT(diag[s], ident.unsqueeze(1).to_broadcast([P, KD, P]),
                       cGm[:, :, s].unsqueeze(2).to_broadcast([P, KD, P]), ALU.mult).then_inc(S["diag_ready"], 1)
                for i in range(nq + 1):
                    if i < nq:
                        j = two_job(jb("out"), nq, i, False)
                        dve.wait_ge(*J.filled(j))
                        if i >= 2:
                            dve.wait_ge(*J.filled(two_job(jb("out"), nq, i - 2, True)))
                        TT(mixT[i % 2], view(J.tile(j)[:, :], k=KD),
                           fac[:, 0:8].unsqueeze(2).to_broadcast([P, KD, P]), ALU.mult).then_inc(*J.free(j))
                    if i >= 1:
                        t = q[i - 1]
                        j = two_job(jb("out"), nq, i - 1, True)
                        dve.wait_ge(*J.filled(j))
                        dve.wait_ge(*v.next(S["m_rstd"]))
                        dve.wait_ge(*J.freed(jb("gm") + (1 if t < CT else 0)))
                        dve.scalar_tensor_tensor(rn2, J.tile(j)[:, :], rstd[:, t:t + 1], GB[1 if t < CT else 0],
                                                 ALU.mult, ALU.mult).then_inc(*J.free(j))
                        dve.wait_ge(*J.freed(j))
                        TT(Xt(t), Xt(t), rn2, ALU.add).then_inc(dve_step, 1)
                        dve.wait_ge(*v.next(dve_step))
                phase()

                def logits(i):
                    j = two_job(jb("f"), nq, i, True)
                    dve.wait_ge(*J.filled(j))
                    TT(aff[:, q[i] * NE:(q[i] + 1) * NE], J.tile(j)[:, 0:NE], rw[:, B_RB:B_RB + NE], ALU.add).then_inc(*J.free(j))

                for i, t in enumerate(q):
                    if i >= 2:
                        dve.wait_ge(*J.filled(two_job(jb("f"), nq, i - 2, True)))
                    modulate(fhT[i % 2], two_job(jb("f"), nq, i, False), cF, mod3[:, 24:32, :],
                             1 if t < CT else 0).then_inc(S["h_ready"], 1)
                    if i:
                        logits(i - 1)
                logits(nq - 1)
                for i in range(nq):
                    dve.wait_ge(*J.freed(two_job(jb("f"), nq, i, True)))
                lg, e3 = (x[:, t0 * NE:NT * NE].rearrange("p (t n) -> p t n", n=NE) for x in (aff, ex))
                if t0:
                    dve.memset(ex[:, 0:t0 * NE], 0.0)
                dve.tensor_reduce(ssum[:, 32:32 + nq], lg, AX_X, ALU.max).then_inc(dve_step, 1)
                dve.wait_ge(*v.next(dve_step))
                TT(e3, lg, ssum[:, 32:32 + nq].unsqueeze(2).to_broadcast([P, nq, NE]), ALU.subtract)\
                    .then_inc(S["router_max"], 1)
                dve.wait_ge(*v.next(S["router_exp"]))
                dve.tensor_reduce(ssum[:, 40:40 + nq], e3, AX_X, ALU.add).then_inc(dve_step, 1)
                dve.wait_ge(*v.next(dve_step))
                dve.reciprocal(ssum[:, 48:48 + nq], ssum[:, 40:40 + nq]).then_inc(dve_step, 1)
                dve.wait_ge(*v.next(dve_step))
                TT(e3, e3, ssum[:, 48:48 + nq].unsqueeze(2).to_broadcast([P, nq, NE]), ALU.mult)\
                    .then_inc(S["aff_ready"], 1)
                j = jb("aT")
                dve.wait_ge(*J.filled(j))
                dve.tensor_copy(aT[0][0:NE, t0 * P:TOK], J.tile(j)[0:NE, t0 * P:TOK]).then_inc(*J.free(j))
                dve.wait_ge(*J.freed(j))
                idi = idu.bitcast(U32)
                for s0, s1, c0, cap in ((CTX, TOK, 0, CAP_L), (0, CTX, CAP_L, CAP_C)):
                    if s0 < t0 * P:
                        continue
                    for r in range(cap // 8):
                        c = c0 + 8 * r
                        src = aT[r % 2][0:NE, s0:s1]
                        dve.max(gv[0:NE, c:c + 8], src).then_inc(dve_step, 1)
                        dve.wait_ge(*v.next(dve_step))
                        dve.max_index(idi[0:NE, c:c + 8], gv[0:NE, c:c + 8], src)
                        dve.match_replace(aT[1 - r % 2][0:NE, s0:s1], gv[0:NE, c:c + 8], src, -1.0).then_inc(dve_step, 1)
                        dve.wait_ge(*v.next(dve_step))
                    dve.tensor_copy(idf[0:NE, c0:c0 + cap], idi[0:NE, c0:c0 + cap]).then_inc(dve_step, 1)
                    dve.wait_ge(*v.next(dve_step))
                    if s0:
                        dve.tensor_scalar(idf[0:NE, c0:c0 + cap], idf[0:NE, c0:c0 + cap], float(s0), None, ALU.add).then_inc(dve_step, 1)
                        dve.wait_ge(*v.next(dve_step))
                for i, (src, c0, n) in enumerate(((idf, 0, CAP_L), (gv, 0, CAP_L), (idf, CAP_L, CAP_C),
                                                  (gv, CAP_L, CAP_C))[:4 if ctx_on else 2]):
                    ins = dve.tensor_copy(slotr[0:NE, i * P:(i + 1) * P].rearrange("p (a n) -> p a n", n=n),
                                          src[0:NE, c0:c0 + n].unsqueeze(1).to_broadcast([NE, P // n, n]))
                ins.then_inc(S["topk_ready"], 1)
                TT(bd[0:NE, 0:NE * ns].rearrange("p (e n) -> p e n", e=NE),
                   idf[0:NE, 0:ns].unsqueeze(1).to_broadcast([NE, NE, ns]),
                   K[0:NE, K_ID:K_ID + NE].unsqueeze(2).to_broadcast([NE, NE, ns]), ALU.mult).then_inc(S["bd_ready"], 1)
                j = jb("idx") + 2
                dve.wait_ge(*J.filled(j))
                nc4 = 4 if ctx_on else 2
                for p in range(2):
                    r = slice(p * 64, p * 64 + 64)
                    ins = dve.tensor_copy(slotc[r, 0:nc4, :], J.tile(j)[r, 0:nc4 * NE]
                                          .rearrange("p (c e two) -> p c e two", c=nc4, two=2)[:, :, :, p])
                ins.then_inc(*J.free(j))
                phase()

                parts = ((0, 0, 0, CAP_L, 0, CT, NT), (1, 512, CAP_L, CAP_C, 256, 0, CT))[:2 if ctx_on else 1]
                dve.memset(Fa[:, t0:NT, :], 0.0).then_inc(dve_step, 1)
                dve.wait_ge(*v.next(dve_step))

                def select(e):
                    for s, c, at, n, sc_, ta, tb in parts:
                        src = idxB[:, e * ns + at:e * ns + at + n] if isinstance(e, int) else idxB[:, bass.ds(e * ns + at, n)]
                        ins = TT(view(Sel[:, sc_:sc_ + (tb - ta) * n], t=tb - ta),
                                 src.unsqueeze(1).to_broadcast([P, tb - ta, n]),
                                 K[:, K_TID + ta:K_TID + tb].unsqueeze(2).to_broadcast([P, tb - ta, n]), ALU.is_equal)
                    ins.then_inc(S["sel_ready"], 1)

                def scatter_mask(i):
                    for c, k0, k1 in ((0, CTX, TOK), (2, 0, CTX))[:2 if ctx_on else 1]:
                        tok_, gate_ = (slotc[:, c + a, i:i + 1] if isinstance(i, int) else slotc[:, c + a, bass.ds(i, 1)]
                                       for a in range(2))
                        ins = dve.tensor_scalar(Sc[:, k0:k1], K[:, K_IOTA + k0:K_IOTA + k1], tok_, gate_,
                                                ALU.is_equal, ALU.mult)
                    ins.then_inc(S["scat_ready"], 1)

                def gathered(j, turn):
                    dve.wait_ge(*J.filled(j, turn))
                    for s, c, at, n, sc_, ta, tb in parts:
                        ins = TT(halves(xg[:, c:c + 8 * n], n), halves(J.tile(j)[:, c:c + 8 * n], n),
                                 cF[:, :, s].rearrange("p (h c) -> p c h", h=2).unsqueeze(3).to_broadcast([P, 4, 2, n]),
                                 ALU.mult)
                    ins.then_inc(*J.free(j))
                    dve.wait_ge(*J.freed(j, turn))
                    for s, c, at, n, sc_, ta, tb in parts:
                        x4 = halves(xg[:, c:c + 8 * n], n)
                        ins = TT(x4, x4, mod3[:, 24:32, s].rearrange("p (h c) -> p c h", h=2).unsqueeze(3)
                                 .to_broadcast([P, 4, 2, n]), ALU.add)
                    ins.then_inc(S["xg_ready"], 1)

                def scattered(j, turn):
                    for k, (t, c0, c1) in enumerate(scatter_parts(l)):
                        dve.wait_ge(*J.filled(j + k, turn))
                        TT(Fa[:, t, c0:c1], Fa[:, t, c0:c1], J.tile(j + k)[:, c0:c1], ALU.add).then_inc(*J.free(j + k))

                def pair(i, last=False):
                    first = isinstance(i, int) and i == 0
                    o, turn, end = pair_jobs(jb("moe"), nsc, i, last)
                    for p in range(2):
                        if not (last and p):
                            select(i * 2 + p + 1)
                        if p:
                            scatter_mask(i)
                        u = J.tile(o[p]["up"])
                        dve.wait_ge(*J.filled(o[p]["up"], turn))
                        dve.wait_ge(*J.freed(o[p]["gate"], turn))
                        ins = TT(hid, sg, u[:, 0:512], ALU.mult)
                        if ctx_on:
                            ins = dve.tensor_copy(cu, u[:, 512:1024])
                        ins.then_inc(*J.free(o[p]["up"]))
                        if ctx_on:
                            n_silu = i * 2 + (l * NE + p + 1)
                            dve.wait_ge(S["silu_turned"], n_silu)
                            TT(hidT[:, 512:768], sgT, J.tile(o[p]["hidT"])[:, 768:1024], ALU.mult).then_inc(*J.free(o[p]["hidT"]))
                        if not (last and p):
                            gathered(o[p]["takeT"], turn)
                        if not first and p == 0:
                            scattered(o[p]["scatter"], turn)
                    return end, turn

                select(0)
                gathered(jb("moe") + 1, 0)
                pair(0)
                with dve.Fori(1, NE // 2 - 1) as i:
                    pair(i)
                end, turn = pair(NE // 2 - 1, last=True)
                scattered(end, turn)
                phase()

                for s in range(2):
                    TT(diagf[s], ident.unsqueeze(1).to_broadcast([P, KD, P]),
                       cGf[:, :, s].unsqueeze(2).to_broadcast([P, KD, P]), ALU.mult).then_inc(S["diag_ready"], 1)
                for s in range(2):
                    dve.wait_ge(*J.freed(jb("gf") + s))
                for t in q:
                    dve.wait_ge(*v.next(S["m_rstd"]))
                    dve.scalar_tensor_tensor(Fa[:, t, :], Fa[:, t, :], rstd[:, t:t + 1], GBf[1 if t < CT else 0],
                                             ALU.mult, ALU.mult).then_inc(dve_step, 1)
                    dve.wait_ge(*v.next(dve_step))
                    ins = TT(Xt(t), Xt(t), Fa[:, t, :], ALU.add)
                    if l == DEPTH - 1:
                        ins.then_inc(S["out_ready"], 1)
                phase()

        @block.tensor
        def _(pe):
            w_ = Tally()
            pe.wait_ge(s_load, 16 * N_SMALL)
            mm = pe.matmul

            def phase():
                for s in (dve_ph, act_ph, pool_ph):
                    pe.wait_ge(*w_.next(s))

            def arrived(j, turn=0):
                pe.wait_ge(ring_full[j % RING], turn + (j // RING + 1) * 16)
                return ringv(j)

            def feature_major(j, w, col, n):
                pe.wait_ge(*J.empty(j))
                o = J.tile(j)
                for c0, c1 in spans(NT):
                    for k in range(KD):
                        ins = mm(o[0:n, c0:c1], w[:, k, col:col + n], hT[:, k, c0:c1], start=k == 0, stop=k == KD - 1)
                ins.then_inc(*J.fill(j))

            def token_major(j, w, tiles, n, stride):
                pe.wait_ge(*J.empty(j))
                o = J.tile(j)
                for i, t in enumerate(tiles):
                    for k in range(KD):
                        ins = mm(o[:, i * stride:i * stride + n], hT[:, k, t * P:(t + 1) * P], w[:, k, :],
                                 start=k == 0, stop=k == KD - 1)
                ins.then_inc(*J.fill(j))

            def turn_tile(j, src, n=KD):
                pe.wait_ge(*J.empty(j))
                o = J.tile(j)
                for k in range(n):
                    ins = pe.transpose(o[:, k * P:(k + 1) * P], src(k), ident)
                ins.then_inc(*J.fill(j))

            def attention(l, heads, base, maps, score, P_of, PT_of, v_of):
                units = [(h, t) for h in range(heads) for t in query_tiles(l)]
                n = len(units)

                def scores(u):
                    h, t = units[u]
                    for m in range(maps):
                        j = att_job(base, maps, n, u, "score", m)
                        pe.wait_ge(*J.empty(j))
                        o = J.tile(j)
                        for c0, c1 in spans(t):
                            lhs, rhs = score(h, m, t, c0, c1)
                            ins = mm(o[:, c0:c1], lhs, rhs, start=True, stop=True)
                        ins.then_inc(*J.fill(j))

                def values(u):
                    h, t = units[u]
                    pe.wait_ge(*J.freed(att_job(base, maps, n, u, "turn")))
                    j = att_job(base, maps, n, u, "value")
                    pe.wait_ge(*J.empty(j))
                    o = J.tile(j)
                    nk = n_keys(t) // P
                    for k in range(nk):
                        ins = mm(o[:, 0:64], PT_of[u % 2][:, k * P:(k + 1) * P], v_of(h, k), start=k == 0, stop=k == nk - 1)
                    ins.then_inc(*J.fill(j))

                scores(0)
                for u in range(n):
                    if u + 1 < n:
                        scores(u + 1)
                    pe.wait_ge(*w_.next(S["prob_ready"]))
                    turn_tile(att_job(base, maps, n, u, "turn"), lambda k: P_of[u % 2][0][:, k * P:(k + 1) * P],
                              n_keys(units[u][1]) // P)
                    if u:
                        values(u - 1)
                values(n - 1)

            def gate_rows(j, dg):
                pe.wait_ge(*w_.next(S["diag_ready"]))
                pe.wait_ge(*J.empty(j))
                o = J.tile(j)
                for hf in range(2):
                    ins = mm(o[:, hf * 512:(hf + 1) * 512], ones, dg[:, 4 * hf:4 * hf + 4, :].rearrange("p k n -> p (k n)"),
                             start=True, stop=True)
                ins.then_inc(*J.fill(j))

            for l in range(DEPTH):
                def jb(n):
                    return JOB[l, n]
                wb, q = l * LAYER_BLOCKS, query_tiles(l)
                nq, ns, t0, nsc = len(q), slots_of(l), q[0], len(scatter_parts(l))
                ctx_on = l < DEPTH - 1
                j = jb("par")
                pe.wait_ge(*J.empty(j))
                o = J.tile(j)
                pe.transpose(o[:, 0:P], pack[:, l * P:(l + 1) * P], ident).then_inc(*J.fill(j))
                pe.wait_ge(*w_.next(S["silu_ready"]))
                j = jb("ada")
                pe.wait_ge(*J.empty(j))
                o = J.tile(j)
                sc3 = sc[:, :].rearrange("p (s k) -> p s k", s=2)
                for b in range(12):
                    w = arrived(wb + b)
                    for m in range(4):
                        c = 2 * (4 * b + m)
                        for k in range(KD):
                            ins = mm(o[:, c:c + 2], w[:, k, m * P:(m + 1) * P], sc3[:, :, k], start=k == 0, stop=k == KD - 1)
                    if b < 11:
                        ins.then_inc(half_used, 1)
                ins.then_inc(*J.fill(j))
                for t in range(NT):
                    pe.wait_ge(*w_.next(S["xn_ready"]))
                    turn_tile(jb("h") + t, lambda k: xn[t % 2][:, k * P:(k + 1) * P])
                pe.wait_ge(*w_.next(S["h_ready"], NT))
                phase()

                w = arrived(wb + 12)
                for m in range(4):
                    feature_major(jb("qk") + m, w, m * P, P)
                w = arrived(wb + 13)
                token_major(jb("v"), w[:, :, 0:256], range(0, 4), 256, 256)
                token_major(jb("v") + 1, w[:, :, 0:256], range(4, 6), 256, 256)
                for m in range(4):
                    j = jb("rot") + m
                    pe.wait_ge(*J.freed(jb("qk") + m))
                    pe.wait_ge(*J.empty(j))
                    o = J.tile(j)
                    mm(o[:, 0:SEQ], kc(K_ROT), QK[:, m, CTX:TOK], start=True, stop=True).then_inc(*J.fill(j))
                pe.wait_ge(*w_.next(S["qk_roped"], 4))
                pe.wait_ge(*J.freed(jb("v")))
                pe.wait_ge(*J.freed(jb("v") + 1))

                def diff_score(h, m, t, c0, c1):
                    r = slice(64 * (h % 2) + 32 * m, 64 * (h % 2) + 32 * m + 32)
                    return QK[r, h // 2, t * P:(t + 1) * P], QK[r, 2 + h // 2, c0:c1]

                attention(l, DH, jb("datt"), 2, diff_score, PD, PT_d, lambda h, k: V[:, k, h * DV:(h + 1) * DV])
                phase()

                w = arrived(wb + 14)
                for i in range(3):
                    token_major(jb("mla") + i, w[:, :, 0:MLA_COLS], (2 * i, 2 * i + 1), MLA_COLS, 512)
                pe.wait_ge(*w_.next(S["lat_scaled"]))
                for i in range(3):
                    j = jb("mlaT") + i
                    pe.wait_ge(*J.empty(j))
                    o = J.tile(j)
                    for b in range(2):
                        m_ = MT[:, 2 * i + b, :]
                        for s, (c0, n) in enumerate(((0, P), (P, MQL - P), (MQL, P), (MLA_COLS - MQK, MQK))):
                            c = 512 * b + P * s
                            ins = pe.transpose(o[0:n, c:c + P], m_[:, c0:c0 + n], ident)
                    ins.then_inc(*J.fill(j))
                for i in range(3):
                    pe.wait_ge(*J.freed(jb("mlaT") + i))
                wq = wqu[:, l * 2 * MH * MQK:(l + 1) * 2 * MH * MQK]
                wk = wkv[:, l * 512:(l + 1) * 512]
                for h in range(MH):
                    j = jb("mq") + h
                    pe.wait_ge(*J.empty(j))
                    o = J.tile(j)
                    for c0, c1 in spans(NT):
                        mm(o[0:MQK, c0:c1], wq[:, h * MQK:(h + 1) * MQK], cq0[:, c0:c1], start=True, stop=False)
                        ins = mm(o[0:MQK, c0:c1], wq[0:MQL - P, (MH + h) * MQK:(MH + h + 1) * MQK], cq1[0:MQL - P, c0:c1],
                                 start=False, stop=True)
                    ins.then_inc(*J.fill(j))
                for h in range(MH):
                    j = jb("mk") + h
                    pe.wait_ge(*J.empty(j))
                    o = J.tile(j)
                    for c0, c1 in spans(NT):
                        ins = mm(o[0:MN, c0:c1], wk[:, h * P:h * P + MN], ckv[:, c0:c1], start=True, stop=True)
                    ins.then_inc(*J.fill(j))
                for i, tiles in enumerate((range(0, 4), range(4, 6))):
                    j = jb("mv") + i
                    pe.wait_ge(*J.empty(j))
                    o = J.tile(j)
                    for n, t in enumerate(tiles):
                        ins = mm(o[:, n * 256:(n + 1) * 256], ckv[:, t * P:(t + 1) * P],
                                 wk.rearrange("p (h n) -> p h n", h=MH)[:, :, MN:P], start=True, stop=True)
                    ins.then_inc(*J.fill(j))
                R = slice(MN, MQK)
                for h in range(MH + 1):
                    j = jb("mrot") + h
                    if h:
                        pe.wait_ge(*J.freed(jb("mq") + h - 1))
                    pe.wait_ge(*J.empty(j))
                    o = J.tile(j)
                    src = KT[R, 0, CTX:TOK] if h == 0 else QT[R, h - 1, CTX:TOK]
                    mm(o[R, 0:SEQ], K[R, K_ROT + MN:K_ROT + MQK], src, start=True, stop=True).then_inc(*J.fill(j))
                pe.wait_ge(*w_.next(S["q_roped"], MH))
                pe.wait_ge(*w_.next(S["kr_all"], MH - 1))
                for h in range(MH):
                    pe.wait_ge(*J.freed(jb("mk") + h))
                for i in range(2):
                    pe.wait_ge(*J.freed(jb("mv") + i))
                attention(l, MH, jb("matt"), 1,
                          lambda h, m, t, c0, c1: (QT[0:MQK, h, t * P:(t + 1) * P], KT[0:MQK, h, c0:c1]),
                          PM, PT_m, lambda h, k: VM[:, k, h * MV:(h + 1) * MV])
                phase()

                w = arrived(wb + 15)
                for m in range(4):
                    feature_major(jb("xbc") + m, w, m * P, P)
                w = arrived(wb + 16)
                for m in range(4, 6):
                    feature_major(jb("xbc") + m, w, (m - 4) * P, P)
                token_major(jb("dt"), w[:, :, 256:272], range(NT), 16, 16)
                w = arrived(wb + 17)
                for i in range(3):
                    token_major(jb("z") + i, w, (2 * i, 2 * i + 1), 512, 512)
                pe.wait_ge(*w_.next(S["xbc_ready"], CONV_T))
                for t in range(NT):
                    turn_tile(jb("xT") + t, lambda k: XB[:, k, t * P:(t + 1) * P], 5)
                pe.wait_ge(*w_.next(S["la_ready"]))
                j = jb("cum")
                pe.wait_ge(*J.empty(j))
                o = J.tile(j)
                la3 = LA.rearrange("p (t d n) -> p t d n", t=NT, d=2)
                mm(o[:, 0:48], kc(K_TRU), la3[:, :, 0, :], start=True, stop=True)
                mm(o[:, 48:96], kc(K_TRL), la3[:, :, 1, :], start=True, stop=True)
                mm(o[:, 96:192], ones, LA, start=True, stop=True).then_inc(*J.fill(j))
                BT, CTr = XB[:, 4, :], XB[:, 5, :]

                def chunk_inner(i):
                    t = q[i]
                    j = ssd_job(jb("ssd"), nq, i, 0)
                    pe.wait_ge(*J.empty(j))
                    o = J.tile(j)
                    for g in range(SG):
                        r = slice(g * SN, (g + 1) * SN)
                        ins = mm(o[:, g * 512:g * 512 + P], BT[r, t * P:(t + 1) * P], CTr[r, t * P:(t + 1) * P],
                                 start=True, stop=True)
                    ins.then_inc(*J.fill(j))
                    for d in range(2):
                        j = ssd_job(jb("ssd"), nq, i, 1 + d)
                        pe.wait_ge(*J.empty(j))
                        o = J.tile(j)
                        for h in range(SH):
                            c = t * 16 + 8 * d + h
                            ins = mm(o[:, h * P:(h + 1) * P], LA[:, c:c + 1].to_broadcast([P, P]),
                                     kc(K_TRU if d == 0 else K_TRL), start=True, stop=True)
                        ins.then_inc(*J.fill(j))

                def chunk_product(i):
                    pe.wait_ge(*w_.next(S["mask_ready"]))
                    j = ssd_job(jb("ssd"), nq, i, 3)
                    pe.wait_ge(*J.empty(j))
                    o = J.tile(j)
                    for h in range(SH):
                        ins = mm(o[:, h * SP:(h + 1) * SP], seg[2][:, h, :], XT[:, q[i], h * SP:(h + 1) * SP],
                                 start=True, stop=True)
                    ins.then_inc(*J.fill(j))

                chunk_inner(0)
                for i in range(nq):
                    if i + 1 < nq:
                        chunk_inner(i + 1)
                    chunk_product(i)
                for n, (d, c, t) in enumerate(chunks()):
                    j = jb("rec") + n
                    pe.wait_ge(*J.empty(j))
                    o = J.tile(j)
                    if c and t in q:
                        pe.wait_ge(*J.freed(jb("rec") + n - 2))
                        for g in range(SG):
                            r = slice(g * SN, (g + 1) * SN)
                            mm(o[:, g * 512:g * 512 + 256], CTr[r, t * P:(t + 1) * P], HS[d][r, :], start=True, stop=True)
                    pe.wait_ge(*w_.next(S["xw_ready"]))
                    for g in range(SG):
                        ins = mm(o[g * SN:(g + 1) * SN, 768:1024], XT[:, t, SI + g * SN:SI + (g + 1) * SN],
                                 XW[n % 2][:, g * 256:(g + 1) * 256], start=True, stop=True)
                    ins.then_inc(*J.fill(j))
                phase()

                for s in range(2):
                    gate_rows(jb("gm") + s, diag[s])
                wo = [arrived(wb + 18), arrived(wb + 19)]

                def mixed(i):
                    turn_tile(two_job(jb("out"), nq, i, False),
                              lambda k: Y[:, q[i], k * P:(k + 1) * P] if k < 4 else matt[:, q[i], (k - 4) * P:(k - 3) * P])

                mixed(0)
                for i in range(nq):
                    if i + 1 < nq:
                        mixed(i + 1)
                    pe.wait_ge(*J.freed(two_job(jb("out"), nq, i, False)))
                    j = two_job(jb("out"), nq, i, True)
                    pe.wait_ge(*J.empty(j))
                    o = J.tile(j)
                    for hf in range(2):
                        for k in range(KD):
                            ins = mm(o[:, hf * 512:(hf + 1) * 512], mixT[i % 2][:, k, :], wo[hf][:, k, :], start=k == 0,
                                     stop=k == KD - 1)
                    ins.then_inc(*J.fill(j))
                phase()

                def latents_turned(i):
                    pe.wait_ge(*w_.next(S["xn_ready"]))
                    turn_tile(two_job(jb("f"), nq, i, False), lambda k: htok[:, q[i], k * P:(k + 1) * P])

                wr = view(wrt[:, l * KD * NE:(l + 1) * KD * NE], k=KD)
                latents_turned(0)
                for i in range(nq):
                    if i + 1 < nq:
                        latents_turned(i + 1)
                    pe.wait_ge(*w_.next(S["h_ready"]))
                    j = two_job(jb("f"), nq, i, True)
                    pe.wait_ge(*J.empty(j))
                    o = J.tile(j)
                    for k in range(KD):
                        ins = mm(o[:, 0:NE], fhT[i % 2][:, k, :], wr[:, k, :], start=k == 0, stop=k == KD - 1)
                    ins.then_inc(*J.fill(j))
                pe.wait_ge(*w_.next(S["aff_ready"]))
                j = jb("aT")
                pe.wait_ge(*J.empty(j))
                o = J.tile(j)
                for t in q:
                    ins = pe.transpose(o[0:NE, t * P:(t + 1) * P], ex[:, t * NE:(t + 1) * NE], ident)
                ins.then_inc(*J.fill(j))
                pe.wait_ge(*w_.next(S["bd_ready"]))
                wd = NE * ns // 2
                for i in range(2):
                    j = jb("idx") + i
                    pe.wait_ge(*J.empty(j))
                    o = J.tile(j)
                    for c0, c1 in ((0, 512), (512, wd)):
                        if c0 < c1:
                            ins = mm(o[:, c0:c1], K[0:NE, K_ONE:K_ONE + P], bd[0:NE, i * wd + c0:i * wd + c1],
                                     start=True, stop=True)
                    ins.then_inc(*J.fill(j))
                pe.wait_ge(*w_.next(S["topk_ready"]))
                j = jb("idx") + 2
                pe.wait_ge(*J.empty(j))
                o = J.tile(j)
                for i in range(4 if ctx_on else 2):
                    ins = pe.transpose(o[:, i * NE:(i + 1) * NE], slotr[0:NE, i * P:(i + 1) * P], K[0:NE, K_ID:K_ID + NE])
                ins.then_inc(*J.fill(j))
                phase()

                def take(j, turn, e):
                    pe.wait_ge(S["sel_ready"], e + (l * NE + 1))
                    pe.wait_ge(*J.empty(j, turn))
                    o = J.tile(j)
                    for t in range(CT, NT):
                        for hf in range(2):
                            ins = mm(o[hf * 64:hf * 64 + 64, 0:512], Sel[:, (t - CT) * CAP_L:(t - CT + 1) * CAP_L],
                                     htok[:, t, hf * 512:hf * 512 + 512], start=t == CT, stop=t == NT - 1)
                    if ctx_on:
                        for hf in range(2):
                            for t in range(CT):
                                r = 32 * (2 * hf + t)
                                ins = mm(o[r:r + 32, 512:1024], Sel[:, 256 + t * CAP_C:256 + (t + 1) * CAP_C],
                                         htok[:, t, hf * 512:hf * 512 + 512], start=True, stop=True)
                    ins.then_inc(*J.fill(j))

                def rows_turned(o, col, src, c):
                    for k in range(4):
                        ins = pe.transpose(o[:, col + k * P:col + (k + 1) * P], src[:, c + k * P:c + (k + 1) * P], ident)
                    return ins

                def rows_summed(o, col, src, c):
                    for k in range(4):
                        ins = mm(o[:, col + k * 64:col + (k + 1) * 64], src[:, c + k * P:c + (k + 1) * P], kc(K_SUM, 64),
                                 start=True, stop=True)
                    return ins

                def take_turned(j, turn):
                    pe.wait_ge(*J.freed(j["take"], turn))
                    pe.wait_ge(*J.empty(j["takeT"], turn))
                    o = J.tile(j["takeT"])
                    ins = rows_turned(o, 0, taken, 0)
                    if ctx_on:
                        ins = rows_summed(o, 512, taken, 512)
                    ins.then_inc(*J.fill(j["takeT"]))

                def project(j, turn, blk, b_turn, rows):
                    pe.wait_ge(*J.empty(j, turn))
                    o = J.tile(j)
                    for b in range(2):
                        arrived(blk + b, b_turn)
                        w = ringk(blk + b)
                        for c in range(4):
                            for hf in range(2):
                                at = c * P + b * CAP_L
                                ins = mm(o[hf * 64:hf * 64 + 64, 0:512], rows[:, at:at + CAP_L],
                                         w[:, c, hf * 512:hf * 512 + 512], start=b + c == 0, stop=b * c == 3)
                        for c in range(4 if ctx_on else 0):
                            for hf in range(2):
                                at = 512 + c * 64 + b * CAP_C
                                r = 32 * (2 * hf + c % 2)
                                ins = mm(o[r:r + 32, 512:1024], rows[:, at:at + CAP_C], w[:, c, hf * 512:hf * 512 + 512],
                                         start=b + c // 2 == 0, stop=b * (c // 2) == 1)
                        if b == 0:
                            ins.then_inc(half_used, 1)
                    ins.then_inc(*J.fill(j))

                def hidden_turned(j, turn):
                    pe.wait_ge(*J.freed(j["up"], turn))
                    pe.wait_ge(*J.empty(j["hidT"], turn))
                    o = J.tile(j["hidT"])
                    ins = rows_turned(o, 0, hid, 0)
                    if ctx_on:
                        rows_summed(o, 512, cg, 0)
                        ins = rows_summed(o, 768, cu, 0)
                    ins.then_inc(*J.fill(j["hidT"]))

                def scatter(j, turn, i):
                    pe.wait_ge(S["scat_ready"], i + (l * NE // 2 + 1))
                    for k, (t, c0, c1) in enumerate(scatter_parts(l)):
                        pe.wait_ge(*J.empty(j + k, turn))
                        o = J.tile(j + k)
                        for c in range(c0, c1, 512):
                            ins = mm(o[:, c:c + 512], Sc[:, t * P:(t + 1) * P], yb[:, 1 if t < CT else 0, c:c + 512],
                                     start=True, stop=True)
                        ins.then_inc(*J.fill(j + k))

                def pair(i, last=False):
                    first = isinstance(i, int) and i == 0
                    o, turn, end = pair_jobs(jb("moe"), nsc, i, last)
                    if not first:
                        before, turn_b, _ = pair_jobs(jb("moe"), nsc, i - 1)
                    for p in range(2):
                        e, blk = i * 2 + p, wb + 20 + 6 * p
                        pe.wait_ge(S["xg_ready"], e + (l * NE + 1))
                        project(o[p]["gate"], turn, blk, i * 48, xg)
                        project(o[p]["up"], turn, blk + 2, i * 48, xg)
                        if not (last and p):
                            take(o[p]["take"], turn, e + 1)
                        hidden_turned(o[p], turn)
                        if not (last and p):
                            take_turned(o[p], turn)
                        if not first and p == 0:
                            pe.wait_ge(*J.freed(before[1]["down"], turn_b))
                            scatter(o[p]["scatter"], turn, i - 1)
                        pe.wait_ge(*J.freed(o[p]["hidT"], turn))
                        project(o[p]["down"], turn, blk + 4, i * 48, hidT)
                    return o, end, turn

                take(jb("moe"), 0, 0)
                take_turned({"take": jb("moe"), "takeT": jb("moe") + 1}, 0)
                pair(0)
                pair(1)
                with pe.Fori(2, NE // 2 - 1) as i:
                    pair(i)
                o, end, turn = pair(NE // 2 - 1, last=True)
                pe.wait_ge(*J.freed(o[1]["down"], turn))
                scatter(end, turn, NE // 2 - 1)
                phase()
                for s in range(2):
                    gate_rows(jb("gf") + s, diagf[s])
                phase()


_NAMES = ['x', 'c', 'ctx', 'c_ctx', 'ada_w', 'ada_b', 'norm_mix_pre', 'norm_mix_post', 'norm_ffn_pre',
          'norm_ffn_post', 'w_in', 'ssd_conv_w', 'ssd_conv_b', 'ssd_a_log', 'ssd_dt_bias', 'ssd_d', 'ssd_norm',
          'diff_lam_q1', 'diff_lam_k1', 'diff_lam_q2', 'diff_lam_k2', 'diff_subln', 'mla_q_norm', 'mla_w_q_up',
          'mla_kv_norm', 'mla_w_kv_up', 'w_out', 'router_w', 'router_b', 'w_gate', 'w_up', 'w_down']


def kernel(**inputs):
    import concourse.bacc as bacc
    from concourse.bass_utils import run_bass_kernel_spmd

    nc = bacc.Bacc("TRN2", target_bir_lowering=False, num_devices=1)
    arrays, T = {}, {}
    for name in _NAMES:
        arrays["in_" + name] = np.ascontiguousarray(inputs[name])
    arrays["in_const"] = constants()
    for name in _NAMES + ["const"]:
        T[name] = nc.dram_tensor("in_" + name, arrays["in_" + name].shape, F32, kind="ExternalInput").ap()
    out = nc.dram_tensor("out", (1, SEQ, D), F32, kind="ExternalOutput").ap()
    build(nc, T, out)
    r = run_bass_kernel_spmd(nc, [arrays], core_ids=[0])
    return r.results[0]["out"]
```

```python
import math
from contextlib import ExitStack

import numpy as np
import concourse.bass as bass
from concourse import mybir

ALU = mybir.AluOpType
ACT = mybir.ActivationFunctionType
F32 = mybir.dt.float32
U32 = mybir.dt.uint32
AX_X = mybir.AxisListType.X

P = 128
D = 1024
KD = D // P
DEPTH = 2
CTX, SEQ, GRID_W = 256, 512, 64
TOK = CTX + SEQ
NT = TOK // P
CT = CTX // P
EPS = 1e-6
SH, SP, SG, SN = 8, 64, 2, 64
HPG = SH // SG
SI = SH * SP
CONV_T = (SI + 2 * SG * SN) // P
DH, DQ, DV = 4, 32, 64
MH, MQL, MKL, MN, MR, MV = 4, 192, 128, 64, 32, 64
MQK = MN + MR
COL_Z, COL_X, COL_B = 0, SI, 2 * SI
COL_DT = COL_B + 2 * SG * SN
COL_QK = COL_DT + 2 * SH
COL_V = COL_QK + 2 * DH * DV
COL_MLA = COL_V + DH * DV
MLA_COLS = MQL + MKL + MR
NE, FF = 16, 1024
CAP_L, CAP_C = 2 * SEQ // NE, 2 * CTX // NE
BLK = 512
RING = 4
NSLOT = 4
LAYER_BLOCKS = 12 + 2 + 1 + 3 + 2 + 6 * NE

K_ID, K_TRU, K_TRL, K_AFT, K_BEF, K_ROT, K_ONE = (i * P for i in range(7))
K_COS = 7 * P
K_SIN = K_COS + SEQ
K_IOTA = K_SIN + SEQ
K_TID = K_IOTA + TOK
K_SUM = K_TID + NT
K_EPS = K_SUM + 2 * CAP_C
K_MAP = K_EPS + 1
K_TWO = K_MAP + 4
K_END = K_TWO + 2

R_ADAB, R_MPRE, R_FPRE, R_MPOST, R_FPOST = 0, 48, 56, 64, 72
R_CW, R_CB, R_QN, R_KVN, R_SN, R_SUB, R_C = 80, 98, 104, 106, 107, 111, 112
B_ALOG, B_DTB, B_DSK, B_RB, B_LAM, B_END = 0, 16, 32, 40, 56, 184


def constants():
    t = np.zeros((P, K_END), np.float32)
    j = np.arange(P)
    t[:, K_ID:K_ID + P] = np.eye(P)
    t[:, K_TRU:K_TRU + P] = j[:, None] <= j[None, :]
    t[:, K_TRL:K_TRL + P] = j[:, None] >= j[None, :]
    t[:, K_AFT:K_AFT + P] = j[:, None] > j[None, :]
    t[:, K_BEF:K_BEF + P] = j[:, None] < j[None, :]
    t[:, K_ONE:K_ONE + P] = 1.0
    q = DQ // 4
    inv = np.float32(10000.0) ** (-np.arange(q, dtype=np.float32) / np.float32(q))
    pos = np.arange(SEQ)
    for p in range(P):
        d = p % DQ
        where = (pos // GRID_W if d < DQ // 2 else pos % GRID_W).astype(np.float32)
        ang = where * inv[d % q]
        t[p, K_COS:K_COS + SEQ] = np.cos(ang)
        t[p, K_SIN:K_SIN + SEQ] = np.sin(ang)
        if (d // q) % 2 == 0:
            t[p + q, K_ROT + p] = -1.0
        else:
            t[p - q, K_ROT + p] = 1.0
    t[:, K_IOTA:K_IOTA + TOK] = np.arange(TOK)[None, :]
    t[:, K_TID:K_TID + NT] = j[:, None] + P * np.arange(NT)[None, :]
    t[j, K_SUM + j // (2 * CAP_C) * CAP_C + j % CAP_C] = 1.0
    t[:, K_EPS] = EPS
    for m in range(4):
        t[:, K_MAP + m] = j // DQ == m
    for m in range(2):
        t[:, K_TWO + m] = j % 32 == m
    return t


def query_tiles(l):
    return list(range(NT)) if l < DEPTH - 1 else list(range(CT, NT))


def spans(t):
    return ((0, CTX),) if t < CT else ((0, 512), (512, TOK))


def scatter_parts(l):
    return [(t, c, c + 512) for t in range(CT) for c in (0, 512) if l < DEPTH - 1] + [(t, 0, D) for t in range(CT, NT)]


def n_keys(t):
    return (CT if t < CT else NT) * P


def chunks():
    fwd = list(range(NT))
    bwd = list(range(CT - 1, -1, -1)) + list(range(NT - 1, CT - 1, -1))
    return [(d, c, (fwd, bwd)[d][c]) for c in range(NT) for d in range(2)]


def job_plan():
    at, n = {}, 0
    for l in range(DEPTH):
        q = len(query_tiles(l))
        for name, c in [("par", 1), ("ada0", 4), ("h", NT),
                        ("qk", 4), ("rot", 4), ("v", 2), ("datt", 4 * DH * q),
                        ("mla", 3), ("ada1", 4), ("mlaT", 3), ("mq", MH), ("mrot", MH + 1), ("mk", MH), ("mv", 2),
                        ("matt", 3 * MH * q),
                        ("ada2", 4), ("xbc", CONV_T), ("dt", 1), ("z", q // 2), ("cum", 1), ("xT", NT),
                        ("ssd", 3 * q + 2 * NT),
                        ("gm", 2), ("out", 2 * q), ("f", 2 * q), ("aT", 1), ("idx", 3),
                        ("moe", NE // 2 * (12 + len(scatter_parts(l)))), ("gf", 2)]:
            at[l, name] = n
            n += c
    return at


def att_job(base, maps, n, u, kind, m=0):
    def start(i):
        return base + maps + i * (maps + 1) + max(0, i - 1)
    if kind == "score":
        return base + m if u == 0 else start(u - 1) + m
    if kind == "turn":
        return start(u) + (maps if u + 1 < n else 0)
    return base + n * (maps + 2) - 1 if u == n - 1 else att_job(base, maps, n, u + 1, "turn") + 1


def two_job(base, n, i, second):
    if not second:
        return base if i == 0 else base + 2 * i - 1
    return base + (2 * n - 1 if i == n - 1 else 2 * i + 2)


def router_job(base, n, i, second):
    if not second:
        return base + (i if i < 3 else 2 * i - 2)
    return base + (2 * i + 3 if i + 2 < n else n + i)


def ssd_jobs(base, n):
    at, j = {}, base
    for i in range(-1, NT):
        if i + 1 < n:
            at["cb", i + 1], at["seg", i + 1] = j, j + 1
            j += 2
        if 0 <= i < n:
            at["y", i] = j
            j += 1
        if i >= 0:
            at["rec", 2 * i], at["rec", 2 * i + 1] = j, j + 1
            j += 2
    return at


def completed(c, q):
    step = {t: [q.index(t)] for t in q}
    for _, n, t in chunks():
        if t in q:
            step[t].append(n)
    return [t for t in q if max(step[t]) == c]


def pair_jobs(jm, nsc, i, last=False):
    first = isinstance(i, int) and i == 0
    b = jm + 2 if first else jm + 14
    turn = 0 if first else (i - 1) * ((12 + nsc) // NSLOT)
    out = []
    for p in range(2):
        o = {"gate": b, "up": b + 1}
        b += 2
        for name, n in (("take", 0 if last and p else 1), ("hidT", 1), ("takeT", 0 if last and p else 1),
                        ("scatter", 0 if first or p else nsc), ("down", 1)):
            o[name] = b
            b += n
        out.append(o)
    return out, turn, b


class Slots:

    def __init__(self, ps, s_full, s_free, first):
        self.ps, self.s_full, self.s_free, self.first = ps, s_full, s_free, first

    def tile(self, j):
        return self.ps[j % NSLOT]

    def fill(self, j):
        return self.s_full[j % NSLOT], 1

    def free(self, j):
        return self.s_free[j % NSLOT], 1

    def filled(self, j, turn=0):
        return self.s_full[j % NSLOT], turn + (j // NSLOT + 1)

    def freed(self, j, turn=0):
        return self.s_free[j % NSLOT], turn + (j // NSLOT + 1)

    def empty(self, j, turn=0):
        return (self.s_free[j % NSLOT], turn + j // NSLOT) if j >= NSLOT else self.first


class Tally:

    def __init__(self):
        self.n = {}

    def next(self, sem, k=1):
        self.n[sem.name] = self.n.get(sem.name, 0) + k
        return sem, self.n[sem.name]


N_PACK, N_ROWS, N_UPS = 17, 8, 4
N_FIRST, N_LATE = 1 + N_PACK + N_ROWS, N_UPS + (DEPTH - 1) * (N_PACK + N_ROWS + N_UPS)



def build(nc, T, out):
    JOB = job_plan()
    with ExitStack() as ctx:
        def sb(name, cols, dt=F32):
            return ctx.enter_context(nc.sbuf_tensor(name, [P, cols], dt))

        def sem(name):
            return ctx.enter_context(nc.semaphore(name))

        ring = [sb(f"ring{i}", KD * BLK) for i in range(RING)]
        X = sb("resid", NT * D)
        K = sb("const", K_END)
        wqu = sb("w_q_up", DEPTH * 2 * MH * MQK)
        wkv = sb("w_kv_up", DEPTH * MH * (MN + MV))
        wrt = sb("w_router", DEPTH * KD * NE)
        pack = sb("pack", DEPTH * P)
        par = sb("par", DEPTH * P)
        rowp = sb("rowp", DEPTH * B_END)
        sc = sb("silu_c", KD * 32)
        mrow = [sb(f"mod_rows{i}", BLK) for i in range(2)]
        mraw = sb("mod_raw", 96)
        mod = sb("mod", 96)
        coef = sb("coef", 64)
        fac = sb("fac", 8)
        small = sb("small", 512)
        dummy = sb("mark", 8)
        ssum, rstd = sb("ssum", 64), sb("rstd", 64)
        nmax, esum, rcol = sb("nmax", 8), sb("esum", 8), sb("rcol", 16)
        acol = sb("acol", 16)
        lam = sb("lam", 136)
        arena_cols = 21824
        A = sb("arena", arena_cols)
        ps = [ctx.enter_context(nc.psum_tensor(f"ps{i}", [P, 1024], F32)) for i in range(NSLOT)]

        ring_full = [sem(f"ring_full{i}") for i in range(RING)]
        half_used = sem("half_used")
        s_load, s_x, s_late = sem("first_loads"), sem("residual_loads"), sem("late_loads")
        s_out, s_zero = sem("out_stored"), sem("pack_zeroed")
        J = Slots(ps, [sem(f"ps_full{i}") for i in range(NSLOT)], [sem(f"ps_free{i}") for i in range(NSLOT)],
                  (s_load, 16 * N_FIRST))
        dve_step, act_step = sem("dve_step"), sem("act_step")
        dve_ph, act_ph, pool_ph = sem("dve_phase"), sem("act_phase"), sem("pool_phase")
        S = {n: sem(n) for n in [
            "silu_ready", "mod_rows", "xn_ready", "h_ready", "lam_dots", "lam_exps", "qk_roped", "q_split",
            "negmax", "prob_ready", "o_ss", "o_rstd", "lat_ss", "lat_rstd", "lat_scaled", "kr_ready", "kr_all",
            "q_roped", "conv_mid", "xbc_ready", "dt_neg", "dt_exp", "dt_w", "dt_ln", "neg_a", "la_ready",
            "lf_ready", "lb_ready", "xdt_ready", "gated", "sum_zero", "x_ready", "coef_ready", "ac_ready",
            "dec_exp", "w_ready", "mask_ready", "xw_ready", "g_rstd", "diag_ready", "m_rstd", "router_max",
            "router_exp", "aff_ready", "topk_ready", "bd_ready", "silu_turned", "sel_ready", "scat_ready",
            "xg_ready", "out_ready"]}

        def kc(c, n=P):
            return K[:, c:c + n]

        ident, ones, eps = kc(K_ID), kc(K_ONE), K[:, K_EPS:K_EPS + 1]

        def Xt(t):
            return X[:, t * D:(t + 1) * D]

        def ar(at, n):
            assert at + n <= arena_cols, (at, n)
            return A[:, at:at + n]

        def view(ap, **kw):
            (k, n), = kw.items()
            return ap.rearrange(f"p ({k} n) -> p {k} n", **{k: n})

        def spread(ap, n, axis, shape):
            return ap.unsqueeze(axis).to_broadcast(shape)

        hT = view(ar(0, KD * TOK), k=KD)
        a0 = KD * TOK
        matt = view(ar(a0, NT * 512), t=NT)
        a1 = a0 + NT * 512
        xn = [ar(a1 + i * D, D) for i in range(2)]
        junk = ar(a1 + 2 * D, D)
        QK = view(ar(a1, 4 * TOK), m=4)
        V = view(ar(a1 + 4 * TOK, NT * 256), t=NT)
        a2 = a1 + 4 * TOK + NT * 256
        rope_t = [ar(a2 + i * SEQ, SEQ) for i in range(2)]
        PD = [[ar(a2 + (2 * i + m) * TOK, TOK) for m in range(2)] for i in range(2)]
        PT_d = [ar(a2 + (4 + i) * TOK, TOK) for i in range(2)]
        QS = view(ar(a2 + 6 * TOK, 4 * TOK), m=4)
        osq = ar(a1, NT * 256)
        QT, KT = view(ar(a1, MH * TOK), h=MH), view(ar(a1 + MH * TOK, MH * TOK), h=MH)
        VM = view(ar(a1 + 2 * MH * TOK, NT * 256), t=NT)
        a3 = a1 + 2 * MH * TOK + NT * 256
        MT = view(ar(a3, NT * MLA_COLS), t=NT)
        msq = view(ar(a1, NT * (MQL + MKL)), t=NT)
        cq0, cq1, ckv = (ar(a3 + NT * MLA_COLS + i * TOK, TOK) for i in range(3))
        PM = [[ar(a3 + i * TOK, TOK)] for i in range(2)]
        PT_m = [ar(a3 + (2 + i) * TOK, TOK) for i in range(2)]
        mrope_t = ar(a3, SEQ)
        XB = view(ar(a1, CONV_T * TOK), m=CONV_T)
        XT = view(ar(a1 + CONV_T * TOK, NT * 640), t=NT)
        a4 = a1 + CONV_T * TOK + NT * 640
        ZS = view(ar(a4, NT * SI), t=NT)
        a5 = a4 + NT * SI
        HS = [ar(a5 + i * HPG * SP, HPG * SP) for i in range(2)]
        EA, ET = ar(a5 + 2 * HPG * SP, 96), ar(a5 + 2 * HPG * SP + 96, 96)
        Y = view(ar(0, NT * SI), t=NT)
        LM = [view(ar(NT * SI + i * 1024, 1024), h=SH) for i in range(2)]
        EB = view(ar(NT * SI + 2048, 1024), h=SH)
        dts = [ar(a5 + 2 * HPG * SP + 192 + 96 * i, 96) for i in range(4)] + [mrow[d][:, 0:96] for d in range(2)]
        WF = view(ar(a1, 1024), h=SH)
        CBM = [view(ar(a1 + 1024 + 256 * d, 256), g=SG) for d in range(2)]
        ytmp = ar(a1 + 1536, SI)
        XW = [ar(a1 + 2048 + i * SI, SI) for i in range(2)]
        xdt = [mrow[d][:, :] for d in range(2)]
        gsq = ar(a5 + 2 * HPG * SP + 192, 256)
        LA, DTV, AC, TOT, WJ = (small[:, i * 96:(i + 1) * 96] for i in range(5))
        mixT = [view(ar(a1 + i * D, D), k=KD) for i in range(2)]
        GB = [ar(a1 + (2 + i) * D, D) for i in range(2)]
        diag = [view(ar(a1 + (4 + i) * D, D), k=KD) for i in range(2)]
        rn, rn2 = ar(a1 + 8 * D, D), ar(a1 + 9 * D, D)
        htok = view(ar(0, NT * D), t=NT)
        Fa = view(ar(NT * D, NT * D), t=NT)
        fhT = [view(ar(NT * D + i * D, D), k=KD) for i in range(4)]
        b0 = 2 * NT * D
        idxB = ar(b0, NE * 96)
        b1 = b0 + NE * 96
        xg = ar(b1, 768)
        hidT = ar(b1 + 768, 768)
        sg, cg, cu, hid = (ar(b1 + 1536 + i * 512, 512) for i in range(4))
        sgT = ar(b1 + 3584, 256)
        sumsq = ar(b1 + 512, 1024)
        taken = ar(b1 + 3840, 1024)
        yb = view(ar(b1 + 4864, 2048), a=2)
        Sel = ar(b1 + 6912, 320)
        Sc = ar(b1 + 7232, TOK)
        aT = [ar(b1 + i * TOK, TOK) for i in range(2)]
        bd = ar(b1, NE * 96)
        aff, ex, idu, idf, gv = (ar(b1 + 2 * TOK + i * 96, 96) for i in range(5))
        slotr = ar(b1 + 2 * TOK + 480, 4 * P)
        slotc = small[:, 480:512].rearrange("p (c e) -> p c e", c=4)
        GBf = [ar(b1 + i * D, D) for i in range(2)]
        diagf = [view(ar(b1 + (2 + i) * D, D), k=KD) for i in range(2)]
        sq_f = ar(b1 + 4 * D, D)

        par_l = [par[:, l * P:(l + 1) * P] for l in range(DEPTH)]
        row_l = [rowp[:, l * B_END:(l + 1) * B_END] for l in range(DEPTH)]
        mod3 = mod[:, :].rearrange("p (m s) -> p m s", s=2)
        cA, cF, cGm, cGf = (coef[:, 16 * i:16 * i + 16].rearrange("p (k s) -> p k s", s=2) for i in range(4))
        LINIT = [0.8 - 0.6 * math.exp(-0.3 * l) for l in range(DEPTH)]

        def ringv(j):
            return ring[j % RING][:, :].rearrange("p (k n) -> p k n", k=KD)

        def ringk(j):
            return ring[j % RING][:, :].rearrange("p (k n) -> p k n", k=KD // 2)

        def halves(ap, n):
            return ap.rearrange("p (c h n) -> p c h n", h=2, n=n)

        def slots_of(l):
            return CAP_L + (CAP_C if l < DEPTH - 1 else 0)

        block = ctx.enter_context(nc.Block())

        @block.sync
        def _(sp):
            count = {}

            def load(dst, src, signal):
                sp.dma_start(dst, src).then_inc(signal, 16)
                count[signal.name] = count.get(signal.name, 0) + 1

            def block_used(l, b):
                if b < 4:
                    sp.wait_ge(half_used, l * (12 + 3 * NE) + b + 1)
                    return
                if 7 <= b < 15:
                    sp.wait_ge(half_used, l * (12 + 3 * NE) + b - 2)
                    return
                n = len(query_tiles(l))
                name, k = {4: ("qk", 3), 5: ("v", 1), 6: ("mla", 2), 15: ("xbc", 3),
                           16: ("dt", 0), 17: ("z", n // 2 - 1), 18: ("out", 2 * n - 1), 19: ("out", 2 * n - 1)}[b]
                sp.wait_ge(*J.filled(JOB[l, name] + k))

            def expert_used(l, i, k, last=False):
                p, w, hf = k // 6, k % 6 // 2, k % 2
                if hf == 0:
                    sp.wait_ge(half_used, i * 6 + (l * (12 + 3 * NE) + 12 + 3 * p + w + 1))
                    return
                o, turn, _ = pair_jobs(JOB[l, "moe"], len(scatter_parts(l)), i, last)
                sp.wait_ge(*J.filled(o[p][("gate", "up", "down")[w]], turn))

            def small_loads(l, rows_to, ups_to):
                pk = pack[:, l * P:(l + 1) * P]

                def rows(at, src, n):
                    load(pk[at:at + n, :], src.rearrange("(r c) -> r c", c=P), rows_to)
                if rows_to is not None:
                    rows(R_C, T["c"][0], KD)
                    rows(R_C + KD, T["c_ctx"], KD)
                    rows(R_ADAB, T["ada_b"][l], 48)
                    for at, nm in ((R_MPRE, "norm_mix_pre"), (R_FPRE, "norm_ffn_pre"), (R_MPOST, "norm_mix_post"),
                                   (R_FPOST, "norm_ffn_post")):
                        rows(at, T[nm][l], KD)
                    for w in range(3):
                        rows(R_CW + CONV_T * w, T["ssd_conv_w"][l, w], CONV_T)
                    rows(R_CB, T["ssd_conv_b"][l], CONV_T)
                    rows(R_QN, T["mla_q_norm"][l, 0:P], 1)
                    load(pk[R_QN + 1:R_QN + 2, 0:MQL - P], T["mla_q_norm"][l:l + 1, P:MQL], rows_to)
                    rows(R_KVN, T["mla_kv_norm"][l], 1)
                    rows(R_SN, T["ssd_norm"][l], 4)
                    for i in range(2):
                        load(pk[R_SUB:R_SUB + 1, i * DV:(i + 1) * DV], T["diff_subln"][l:l + 1, :], rows_to)
                    for at, n, nm in ((B_ALOG, 16, "ssd_a_log"), (B_DTB, 16, "ssd_dt_bias"), (B_DSK, 8, "ssd_d"),
                                      (B_RB, 16, "router_b"), (B_LAM, 32, "diff_lam_q1"), (B_LAM + 32, 32, "diff_lam_k1"),
                                      (B_LAM + 64, 32, "diff_lam_q2"), (B_LAM + 96, 32, "diff_lam_k2")):
                        src = T[nm][l]
                        if n == 16 and nm != "router_b":
                            src = src.rearrange("a b -> (a b)")
                        load(row_l[l][:, at:at + n], src.partition_broadcast(P), rows_to)
                if ups_to is not None:
                    wq = wqu[:, l * 2 * MH * MQK:(l + 1) * 2 * MH * MQK]
                    load(wq[:, 0:MH * MQK], T["mla_w_q_up"][l, 0:P, :], ups_to)
                    load(wq[0:MQL - P, MH * MQK:2 * MH * MQK], T["mla_w_q_up"][l, P:MQL, :], ups_to)
                    load(wkv[:, l * 512:(l + 1) * 512], T["mla_w_kv_up"][l], ups_to)
                    load(view(wrt[:, l * KD * NE:(l + 1) * KD * NE], k=KD),
                         T["router_w"][l].rearrange("(k p) n -> p k n", p=P), ups_to)

            for l in range(DEPTH):
                jl = l * LAYER_BLOCKS
                aw, wi, wo = (T[n][l].rearrange("(k p) n -> p k n", p=P) for n in ("ada_w", "w_in", "w_out"))
                srcs = [aw[:, :, b * BLK:(b + 1) * BLK] for b in range(4)]
                srcs += [wi[:, :, c:c + n] for c, n in ((COL_QK, 512), (COL_V, 256), (COL_MLA, MLA_COLS))]
                srcs += [aw[:, :, b * BLK:(b + 1) * BLK] for b in range(4, 12)]
                srcs += [wi[:, :, c:c + n] for c, n in ((COL_X, 512), (COL_B, 272), (COL_Z, 512))]
                srcs += [wo[:, :, b * BLK:(b + 1) * BLK] for b in range(2)]
                for b, src in enumerate(srcs):
                    if l == 0:
                        if b == 0:
                            load(K[:, :], T["const"], s_load)
                        if b == 1:
                            sp.wait_ge(s_zero, 2)
                            small_loads(0, s_load, None)
                            assert count[s_load.name] == N_FIRST
                        if b == 2:
                            for t in range(NT):
                                load(Xt(t), T["ctx"][0, t * P:(t + 1) * P, :] if t < CT
                                     else T["x"][0, (t - CT) * P:(t - CT + 1) * P, :], s_x)
                        if b == 4:
                            small_loads(0, None, s_late)
                            for l1 in range(1, DEPTH):
                                small_loads(l1, s_late, s_late)
                            assert count[s_late.name] == N_LATE
                    if b >= RING:
                        block_used(l, b - RING)
                    elif l:
                        expert_used(l - 1, NE // 2 - 1, 8 + b, last=True)
                    sp.dma_start(ringv(jl + b)[:, :, 0:src.shape[2]], src).then_inc(ring_full[(jl + b) % RING], 16)
                gud = [T[n].rearrange("l e (k p) n -> (l e) p k n", p=P) for n in ("w_gate", "w_up", "w_down")]

                def pair_loads(i, before):
                    for k in range(12):
                        p, w, hf = k // 6, k % 6 // 2, k % 2
                        before(k)
                        e = i * 2 + (l * NE + p)
                        src = gud[w][e] if isinstance(i, int) else gud[w][bass.ds(e, 1)][0]
                        sp.dma_start(ringk(k), src[:, 4 * hf:4 * hf + 4, :]).then_inc(ring_full[k % RING], 16)

                pair_loads(0, lambda k: block_used(l, 16 + k) if k < RING else expert_used(l, 0, k - RING))
                pair_loads(1, lambda k: expert_used(l, 0, 8 + k) if k < RING else expert_used(l, 1, k - RING))
                with sp.Fori(2, NE // 2) as i:
                    pair_loads(i, lambda k: expert_used(l, i - 1, 8 + k) if k < RING else expert_used(l, i, k - RING))
            for t in range(CT, NT):
                sp.wait_ge(S["out_ready"], t - CT + 1)
                sp.dma_start(out[0, (t - CT) * P:(t - CT + 1) * P, :], Xt(t)).then_inc(s_out, 16)
            sp.wait_ge(s_out, 16 * (NT - CT))

        @block.gpsimd
        def _(pool):
            g = Tally()
            pool.memset(sc[:, :], 0.0).then_inc(s_zero, 1)
            pool.memset(pack[:, :], 0.0).then_inc(s_zero, 1)

            def phase():
                pool.memset(dummy[0:1, 0:1], 0.0).then_inc(pool_ph, 1)
                for s in (pool_ph, dve_ph, act_ph):
                    pool.wait_ge(*g.next(s))

            for l in range(DEPTH):
                phase()
                phase()
                pool.wait_ge(*g.next(S["kr_ready"]))
                for h in range(1, MH):
                    pool.tensor_copy(KT[MN:MQK, h, :], KT[MN:MQK, 0, :]).then_inc(S["kr_all"], 1)
                phase()
                q, jobs = query_tiles(l), ssd_jobs(JOB[l, "ssd"], len(query_tiles(l)))
                nq = len(q)
                pool.wait_ge(*g.next(S["la_ready"]))
                pool.wait_ge(*J.filled(JOB[l, "z"] + nq // 2 - 1))

                def masked_decays(i):
                    if i:
                        pool.wait_ge(*J.filled(jobs["seg", i - 1]))
                    la = LA[:, q[i] * 16:q[i] * 16 + 8]
                    pool.tensor_tensor(LM[0], kc(K_AFT).unsqueeze(1).to_broadcast([P, SH, P]),
                                       la.unsqueeze(2).to_broadcast([P, SH, P]), ALU.mult).then_inc(S["lf_ready"], 1)

                masked_decays(0)
                pool.wait_ge(*J.freed(JOB[l, "xT"] + NT - 1))
                for i in range(NT):
                    if i + 1 < nq:
                        masked_decays(i + 1)
                    if i < nq:
                        if i:
                            pool.wait_ge(*J.filled(jobs["y", i - 1]))
                        for d in range(2):
                            w = DTV[:, q[i] * 16 + d * 8:q[i] * 16 + d * 8 + 8]
                            pool.tensor_tensor(view(xdt[d], h=SH), view(XT[:, q[i], 0:SI], h=SH),
                                               w.unsqueeze(2).to_broadcast([P, SH, SP]), ALU.mult).then_inc(S["xdt_ready"], 1)
                    if i == 0:
                        pool.wait_ge(*g.next(S["w_ready"]))
                    for n in (2 * i, 2 * i + 1):
                        d, c, t = chunks()[n]
                        if n >= 2:
                            pool.wait_ge(*J.filled(jobs["rec", n - 2]))
                        w = WJ[:, t * 16 + d * 8:t * 16 + d * 8 + 8]
                        pool.tensor_tensor(view(XW[n % 2], h=SH), view(XT[:, t, 0:SI], h=SH),
                                           w.unsqueeze(2).to_broadcast([P, SH, SP]), ALU.mult).then_inc(S["xw_ready"], 1)
                for _ in range(2):
                    phase()
                pool.memset(Fa[:, q[0]:NT, :], 0.0).then_inc(S["sum_zero"], 1)
                for _ in range(2):
                    phase()

        @block.scalar
        def _(act):
            a = Tally()
            act.wait_ge(s_load, 16 * N_FIRST)

            def phase():
                act.activation(dummy[0:1, 1:2], K[0:1, 0:1], ACT.Copy).then_inc(act_ph, 1)
                for s in (act_ph, dve_ph, pool_ph):
                    act.wait_ge(*a.next(s))

            def log_exp_table():
                act.preload_act_table_set("natural_log_exp_and_others")

            def rsqrt(dst, src, n_feat, signal):
                act.activation(dst, src, ACT.Ln, bias=eps, scale=1.0 / n_feat).then_inc(act_step, 1)
                act.wait_ge(*a.next(act_step))
                act.activation(dst, dst, ACT.Exp, scale=-0.5).then_inc(signal, 1)

            def copy_out(dst, src, j, func=ACT.Copy, scale=1.0):
                act.wait_ge(*J.filled(j))
                act.activation(dst, src, func, scale=scale).then_inc(*J.free(j))

            def square(t, junk_):
                act.activation(junk_, Xt(t), ACT.Square, accum_out=ssum[:, 56 + t:57 + t]).then_inc(act_step, 1)
                act.wait_ge(*a.next(act_step))

            def latent_norms():
                act.wait_ge(*a.next(S["lat_ss"]))
                act.activation(rstd[:, 0:NT], ssum[:, 0:NT], ACT.Ln, bias=eps, scale=1.0 / MQL)
                act.activation(rstd[:, 8:8 + NT], ssum[:, 8:8 + NT], ACT.Ln, bias=eps, scale=1.0 / MKL).then_inc(act_step, 1)
                act.wait_ge(*a.next(act_step))
                act.activation(rstd[:, 0:NT], rstd[:, 0:NT], ACT.Exp, scale=-0.5)
                act.activation(rstd[:, 8:8 + NT], rstd[:, 8:8 + NT], ACT.Exp, scale=-0.5).then_inc(S["lat_rstd"], 1)

            def modulation(l, part):
                for b in range(5):
                    j = JOB[l, f"ada{part}"] + b
                    if l == 0 and part == 0 and b == 2:
                        act.wait_ge(s_x, 16 * NT)
                        for t in range(NT):
                            square(t, junk)
                    if part == 1 and b == 1:
                        latent_norms()
                    if b < 4:
                        n = l * (12 + 3 * NE) + 4 * part + b + 1
                        act.wait_ge(half_used, n)
                        if 4 * part + b >= 2:
                            before = JOB[l, f"ada{part}"] + b - 2 if b >= 2 else JOB[l, f"ada{part - 1}"] + b + 2
                            act.wait_ge(*J.filled(before))
                        act.activation(mrow[b % 2][:, :], J.tile(j)[:, 0:BLK], ACT.Copy).then_inc(S["mod_rows"], 1)
                    if b >= 1:
                        act.wait_ge(*J.filled(j - 1))
                        c = 8 * (4 * part + b - 1)
                        act.activation(mraw[:, c:c + 8], J.tile(j - 1)[:, BLK:BLK + 8], ACT.Copy).then_inc(*J.free(j - 1))

            def residual_rstd(t0, t1):
                r = slice(56 + t0, 56 + t1)
                act.activation(rstd[:, r], ssum[:, r], ACT.Ln, bias=eps, scale=1.0 / D).then_inc(act_step, 1)
                act.wait_ge(*a.next(act_step))
                act.activation(rstd[:, r], rstd[:, r], ACT.Exp, scale=-0.5).then_inc(act_step, 1)
                act.wait_ge(*a.next(act_step))

            def norm_tile(dst, t):
                act.activation(dst, Xt(t), ACT.Copy, scale=rstd[:, 56 + t:57 + t]).then_inc(S["xn_ready"], 1)

            def modulate(dst, j, c_scale, c_shift, s):
                act.wait_ge(*J.filled(j))
                for k in range(KD):
                    ins = act.activation(dst[:, k, :], J.tile(j)[:, k * P:(k + 1) * P], ACT.Identity,
                                         bias=c_shift[:, k, s:s + 1], scale=c_scale[:, k, s:s + 1])
                ins.then_inc(*J.free(j))

            def conditioning(l):
                act.wait_ge(*J.freed(JOB[l, "par"]))
                act.wait_ge(s_zero, 1)
                act.activation(view(sc[:, :], k=KD)[:, :, 0:2],
                               par_l[l][:, R_C:R_C + 16].rearrange("p (s k) -> p k s", s=2), ACT.Silu)\
                    .then_inc(S["silu_ready"], 1)
                log_exp_table()
                modulation(l, 0)

            def softmax(l, heads, base, maps, P_of, PT_of, after_exps=None):
                units = [(h, t) for h in range(heads) for t in query_tiles(l)]
                n = len(units)
                for i in range(n + 1):
                    if i < n:
                        nk = n_keys(units[i][1])
                        if i >= 2:
                            act.wait_ge(*J.filled(att_job(base, maps, n, i - 2, "turn")))
                        for m in range(maps):
                            j = att_job(base, maps, n, i, "score", m)
                            act.wait_ge(*a.next(S["negmax"]))
                            c = 2 * (i % 2) + m
                            act.activation(P_of[i % 2][m][:, 0:nk], J.tile(j)[:, 0:nk], ACT.Exp,
                                           bias=nmax[:, c:c + 1], accum_out=esum[:, c:c + 1]).then_inc(*J.free(j))
                        if after_exps:
                            after_exps(i)
                    if i >= 1:
                        u = i - 1
                        nk = n_keys(units[u][1])
                        if u >= 2:
                            act.wait_ge(*J.filled(att_job(base, maps, n, u - 2, "value")))
                        j = att_job(base, maps, n, u, "turn")
                        copy_out(PT_of[u % 2][:, 0:nk], J.tile(j)[:, 0:nk], j)

            for l in range(DEPTH):
                def jb(n):
                    return JOB[l, n]
                rw, pc, q = row_l[l], par_l[l], query_tiles(l)
                nq, ns, nsc = len(q), slots_of(l), len(scatter_parts(l))
                ctx_on = l < DEPTH - 1
                nb = 2 if ctx_on else 1
                if l == 0:
                    conditioning(0)
                def h_tile(t):
                    if l == 0 and t == 1:
                        act.wait_ge(S["coef_ready"], 1)
                    modulate(hT[:, :, t * P:(t + 1) * P], jb("h") + t, cA, mod3[:, 0:8, :], 1 if t < CT else 0)

                residual_rstd(0, NT)
                for t in range(NT):
                    if t >= 2:
                        act.wait_ge(*J.filled(jb("h") + t - 2))
                    norm_tile(xn[t % 2], t)
                    if t % 2 == 0 and t:
                        h_tile(t - 1)
                h_tile(NT - 1)
                phase()

                act.wait_ge(*a.next(S["lam_dots"]))
                act.activation(lam[:, 132:134], lam[:, 128:130], ACT.Exp).then_inc(S["lam_exps"], 1)
                tq = q[0] * P
                for m in range(4):
                    c = tq if m < 2 else 0
                    copy_out(QK[:, m, c:TOK], J.tile(jb("qk") + m)[:, c:TOK], jb("qk") + m, scale=DQ ** -0.5 if m < 2 else 1.0)
                def split_queries(h):
                    for m in range(2):
                        i = 2 * (h % 2) + m
                        act.activation(QS[:, i, tq:TOK], QK[:, h // 2, tq:TOK], ACT.Copy,
                                       scale=K[:, K_MAP + i:K_MAP + i + 1]).then_inc(S["q_split"], 1)

                def after_exps(i):
                    h = i // nq
                    if i % nq == 0 and 1 <= h < DH - 1:
                        split_queries(h + 1)

                act.wait_ge(*a.next(S["qk_roped"]))
                split_queries(0)
                split_queries(1)
                for i, (t0, n) in enumerate(((0, 4), (4, 2))):
                    copy_out(V[:, t0:t0 + n, :].rearrange("p t n -> p (t n)"), J.tile(jb("v") + i)[:, 0:256 * n], jb("v") + i)
                act.wait_ge(*a.next(S["qk_roped"], 3))
                softmax(l, DH, jb("datt"), 2, PD, PT_d, after_exps)
                act.wait_ge(*a.next(S["o_ss"]))
                rsqrt(rstd[:, 4 * q[0]:4 * NT], ssum[:, 4 * q[0]:4 * NT], DV, S["o_rstd"])
                phase()

                for i in range(3):
                    j = jb("mla") + i
                    copy_out(MT[:, 2 * i:2 * i + 2, :],
                             J.tile(j)[:, :].rearrange("p (b n) -> p b n", b=2)[:, :, 0:MLA_COLS], j)
                modulation(l, 1)
                for i in range(3):
                    j = jb("mlaT") + i
                    act.wait_ge(*J.filled(j))
                    v4 = J.tile(j)[:, :].rearrange("p (b q n) -> p b q n", b=2, q=4)
                    for s, (dst, r0, r1, col) in enumerate(((cq0, 0, P, R_QN), (cq1, 0, MQL - P, R_QN + 1),
                                                            (ckv, 0, P, R_KVN), (KT[:, 0, :], MN, MQK, None))):
                        ins = act.activation(dst[r0:r1, i * 256:i * 256 + 256].rearrange("p (b n) -> p b n", b=2),
                                             v4[r0:r1, :, s, :], ACT.Copy,
                                             scale=1.0 if col is None else pc[r0:r1, col:col + 1])
                    ins.then_inc(*J.free(j))
                for h in range(MH):
                    copy_out(QT[0:MQK, h, tq:TOK], J.tile(jb("mq") + h)[0:MQK, tq:TOK], jb("mq") + h, scale=MQK ** -0.5)
                for h in range(MH):
                    copy_out(KT[0:MN, h, :], J.tile(jb("mk") + h)[0:MN, 0:TOK], jb("mk") + h)
                for i, (t0, n) in enumerate(((0, 4), (4, 2))):
                    copy_out(VM[:, t0:t0 + n, :].rearrange("p t n -> p (t n)"), J.tile(jb("mv") + i)[:, 0:256 * n],
                             jb("mv") + i)
                softmax(l, MH, jb("matt"), 1, PM, PT_m)
                phase()

                modulation(l, 2)
                for m in range(CONV_T + 1):
                    if m < CONV_T:
                        j = jb("xbc") + m
                        act.wait_ge(*J.filled(j))
                        act.activation(XB[:, m, :], J.tile(j)[:, 0:TOK], ACT.Identity, bias=pc[:, R_CB + m:R_CB + m + 1],
                                       scale=pc[:, R_CW + CONV_T + m:R_CW + CONV_T + m + 1]).then_inc(S["conv_mid"], 1)
                    if m >= 1:
                        act.wait_ge(*J.freed(jb("xbc") + m - 1))
                        act.activation(XB[:, m - 1, :], XB[:, m - 1, :], ACT.Silu).then_inc(S["xbc_ready"], 1)
                log_exp_table()
                act.wait_ge(*a.next(S["dt_neg"]))
                act.activation(dts[1], dts[1], ACT.Exp).then_inc(S["dt_exp"], 1)
                act.activation(acol[:, 0:16], rw[:, B_ALOG:B_ALOG + 16], ACT.Exp).then_inc(S["neg_a"], 1)
                act.wait_ge(*a.next(S["dt_w"]))
                act.activation(dts[3], dts[2], ACT.Ln).then_inc(S["dt_ln"], 1)
                for i in range(nq // 2):
                    copy_out(ZS[:, q[2 * i]:q[2 * i] + 2, :].rearrange("p t n -> p (t n)"), J.tile(jb("z") + i)[:, :],
                             jb("z") + i, func=ACT.Silu)
                log_exp_table()
                act.wait_ge(*a.next(S["la_ready"]))
                act.wait_ge(*a.next(S["ac_ready"]))
                act.activation(WJ, WJ, ACT.Exp)
                act.activation(EA, AC, ACT.Exp)
                act.activation(ET, TOT, ACT.Exp).then_inc(S["dec_exp"], 1)
                for t in range(NT):
                    copy_out(XT[:, t, :], J.tile(jb("xT") + t)[:, 0:640], jb("xT") + t)
                jobs = ssd_jobs(jb("ssd"), nq)

                def masked_decays(i):
                    if i:
                        act.wait_ge(*J.filled(jobs["seg", i - 1]))
                    for h in range(SH):
                        c = q[i] * 16 + 8 + h
                        ins = act.activation(LM[1][:, h, :], kc(K_BEF), ACT.Copy, scale=LA[:, c:c + 1])
                    ins.then_inc(S["lb_ready"], 1)

                def gate_squares(c):
                    for t in completed(c, q):
                        act.wait_ge(*a.next(S["gated"]))
                        for g in range(SG):
                            act.activation(gsq, Y[:, t, g * 256:g * 256 + 256], ACT.Square,
                                           accum_out=ssum[:, 2 * t + g:2 * t + g + 1]).then_inc(act_step, 1)
                            act.wait_ge(*a.next(act_step))

                masked_decays(0)
                for i in range(nq):
                    if i + 1 < nq:
                        masked_decays(i + 1)
                    act.wait_ge(*J.filled(jobs["seg", i]))
                    if i:
                        act.wait_ge(*J.filled(jobs["y", i - 1]))
                    act.activation(EB, view(J.tile(jobs["seg", i])[:, :], h=SH), ACT.Exp).then_inc(*J.free(jobs["seg", i]))
                    if i:
                        gate_squares(i - 1)
                for c in range(nq - 1, NT):
                    gate_squares(c)
                rsqrt(rstd[:, 2 * q[0]:2 * NT], ssum[:, 2 * q[0]:2 * NT], SI // SG, S["g_rstd"])
                act.wait_ge(*a.next(S["g_rstd"]))
                for t in q[nq // 2:]:
                    for g in range(SG):
                        y_ = Y[:, t, g * 256:g * 256 + 256]
                        act.activation(y_, y_, ACT.Copy, scale=rstd[:, 2 * t + g:2 * t + g + 1])
                phase()

                for s in range(2):
                    copy_out(GB[s], J.tile(jb("gm") + s)[:, :], jb("gm") + s)
                def f_tile(i):
                    if i >= 4:
                        act.wait_ge(*J.filled(router_job(jb("f"), nq, i - 4, True)))
                    modulate(fhT[i % 4], router_job(jb("f"), nq, i, False), cF, mod3[:, 24:32, :], 1 if q[i] < CT else 0)

                for i, t in enumerate(q):
                    if i:
                        act.wait_ge(*a.next(S["x_ready"]))
                        square(q[i - 1], rn)
                    if i == nq - 1:
                        act.wait_ge(*J.filled(two_job(jb("out"), nq, i, False)))
                        residual_rstd(q[0], NT - 1)
                        for t_ in q[:-1]:
                            norm_tile(htok[:, t_, :], t_)
                    j = two_job(jb("out"), nq, i, True)
                    act.wait_ge(*J.filled(j))
                    act.activation(rn, J.tile(j)[:, :], ACT.Square, accum_out=ssum[:, t:t + 1]).then_inc(act_step, 1)
                    act.wait_ge(*a.next(act_step))
                    rsqrt(rstd[:, t:t + 1], ssum[:, t:t + 1], D, S["m_rstd"])

                f_tile(1)
                act.wait_ge(*a.next(S["x_ready"]))
                square(NT - 1, rn)
                residual_rstd(NT - 1, NT)
                norm_tile(htok[:, NT - 1, :], NT - 1)
                for i in range(3, nq, 2):
                    f_tile(i)
                act.wait_ge(*a.next(S["router_max"]))
                act.activation(ex, ex, ACT.Exp).then_inc(S["router_exp"], 1)
                w = NE * ns // 2
                for i in range(2):
                    copy_out(idxB[:, i * w:(i + 1) * w], J.tile(jb("idx") + i)[:, 0:w], jb("idx") + i)
                phase()

                def pair(i, last=False):
                    o, turn, _ = pair_jobs(jb("moe"), nsc, i, last)
                    before, b_turn, _ = pair_jobs(jb("moe"), nsc, i - 1) if not (isinstance(i, int) and i == 0) \
                        else (None, 0, 0)
                    for p in range(2):
                        act.wait_ge(*J.filled(o[p]["gate"], turn))
                        if p:
                            act.wait_ge(*J.freed(o[0]["up"], turn))
                            act.wait_ge(*J.filled(o[0]["hidT"], turn))
                        elif before:
                            act.wait_ge(*J.freed(before[1]["up"], b_turn))
                            act.wait_ge(*J.filled(before[1]["hidT"], b_turn))
                        t_ = J.tile(o[p]["gate"])
                        ins = act.activation(sg, t_[:, 0:512], ACT.Silu)
                        if ctx_on:
                            ins = act.activation(cg, t_[:, 512:1024], ACT.Copy)
                        ins.then_inc(*J.free(o[p]["gate"]))
                        if not (last and p):
                            take(o[p]["take"], turn)
                        act.wait_ge(*J.filled(o[p]["hidT"], turn))
                        t_ = J.tile(o[p]["hidT"])
                        if ctx_on:
                            if p:
                                act.wait_ge(*J.freed(o[0]["hidT"], turn))
                            elif before:
                                act.wait_ge(*J.freed(before[1]["hidT"], b_turn))
                            act.activation(hidT[:, 0:512], t_[:, 0:512], ACT.Copy)
                            act.activation(sgT, t_[:, 512:768], ACT.Silu).then_inc(S["silu_turned"], 1)
                        else:
                            act.activation(hidT[:, 0:512], t_[:, 0:512], ACT.Copy).then_inc(*J.free(o[p]["hidT"]))
                        act.wait_ge(*J.filled(o[p]["down"], turn))
                        for hf in range(2):
                            ins = act.activation(yb[p * 64:p * 64 + 64, 0:nb, hf * 512:hf * 512 + 512],
                                                 J.tile(o[p]["down"])[hf * 64:hf * 64 + 64, 0:nb * 512]
                                                 .rearrange("p (a n) -> p a n", a=nb), ACT.Copy)
                        ins.then_inc(*J.free(o[p]["down"]))

                def take(j, turn):
                    act.wait_ge(*J.filled(j, turn))
                    act.activation(taken[:, 0:nb * 512], J.tile(j)[:, 0:nb * 512], ACT.Copy).then_inc(*J.free(j))

                take(jb("moe"), 0)
                pair(0)
                pair(1)
                with act.Fori(2, NE // 2 - 1) as i:
                    pair(i)
                pair(NE // 2 - 1, last=True)
                log_exp_table()
                _, turn, end = pair_jobs(jb("moe"), nsc, NE // 2 - 1, last=True)
                for k, (t, c0, c1) in enumerate(scatter_parts(l)):
                    if c1 < D:
                        continue
                    act.wait_ge(*J.freed(end + k, turn))
                    act.activation(sumsq, Fa[:, t, :], ACT.Square, accum_out=ssum[:, t:t + 1]).then_inc(act_step, 1)
                    act.wait_ge(*a.next(act_step))
                phase()

                t0 = q[0]
                rsqrt(rstd[:, t0:NT], ssum[:, t0:NT], D, S["m_rstd"])
                for s in range(2):
                    copy_out(GBf[s], J.tile(jb("gf") + s)[:, :], jb("gf") + s)
                if l + 1 < DEPTH:
                    conditioning(l + 1)
                    for t in q:
                        act.wait_ge(*a.next(S["x_ready"]))
                        square(t, sq_f)
                phase()

        @block.vector
        def _(dve):
            v = Tally()
            dve.wait_ge(s_load, 16 * N_FIRST)
            TT = dve.tensor_tensor

            def phase():
                dve.memset(dummy[0:1, 4:5], 0.0).then_inc(dve_ph, 1)
                for s in (dve_ph, act_ph, pool_ph):
                    dve.wait_ge(*v.next(s))

            def modulate(dst, j, c_scale, c_shift, s):
                dve.wait_ge(*J.filled(j))
                TT(dst, view(J.tile(j)[:, :], k=KD), c_scale[:, :, s].unsqueeze(2).to_broadcast([P, KD, P]),
                   ALU.mult).then_inc(*J.free(j))
                dve.wait_ge(*J.freed(j))
                return TT(dst, dst, c_shift[:, :, s].unsqueeze(2).to_broadcast([P, KD, P]), ALU.add)

            def attend(l, base, maps, heads, weigh, finish):
                units = [(h, t) for h in range(heads) for t in query_tiles(l)]
                n = len(units)
                for i in range(n + 2):
                    if 1 <= i <= n:
                        for m in range(maps):
                            dve.wait_ge(*J.freed(att_job(base, maps, n, i - 1, "score", m)))
                        if i >= 3:
                            dve.wait_ge(*J.freed(att_job(base, maps, n, i - 3, "value")))
                        weigh(i - 1, n_keys(units[i - 1][1]))
                    if i < n:
                        nk = n_keys(units[i][1])
                        for m in range(maps):
                            j = att_job(base, maps, n, i, "score", m)
                            dve.wait_ge(*J.filled(j))
                            if i >= 2:
                                dve.wait_ge(*J.freed(att_job(base, maps, n, i - 2, "score", m)))
                            c = 2 * (i % 2) + m
                            dve.tensor_reduce(nmax[:, c:c + 1], J.tile(j)[:, 0:nk], AX_X, ALU.max,
                                              negate=True).then_inc(S["negmax"], 1)
                    if i >= 2:
                        h, t = units[i - 2]
                        j = att_job(base, maps, n, i - 2, "value")
                        dve.wait_ge(*J.filled(j))
                        finish(i - 2, h, t, j)

            def parameters(l):
                j, pc = JOB[l, "par"], par_l[l]
                dve.wait_ge(*J.filled(j))
                dve.tensor_copy(pc, J.tile(j)[:, 0:P]).then_inc(*J.free(j))
                dve.wait_ge(*J.freed(j))
                dve.tensor_copy(fac[:, 0:4], pc[:, R_SN:R_SN + 4])
                for i in range(2):
                    dve.tensor_scalar(fac[:, 4 + i:5 + i], pc[:, R_SUB:R_SUB + 1], 1.0 - LINIT[l], None, ALU.mult)
                dve.memset(fac[:, 6:8], 1.0)

            def add_bias(l, part, b0, b1):
                for b in range(4):
                    dve.wait_ge(*J.freed(JOB[l, part] + b))
                TT(mod3[:, 4 * b0:4 * b1, :], mraw[:, 8 * b0:8 * b1].rearrange("p (m s) -> p m s", s=2),
                   par_l[l][:, R_ADAB + 4 * b0:R_ADAB + 4 * b1].unsqueeze(2).to_broadcast([P, 4 * (b1 - b0), 2]),
                   ALU.add).then_inc(dve_step, 1)
                dve.wait_ge(*v.next(dve_step))

            def coefficients(l, which):
                for dst, m0, col, one in which:
                    ins = dve.scalar_tensor_tensor(dst, mod3[:, m0:m0 + 8, :], one,
                                                   par_l[l][:, col:col + 8].unsqueeze(2).to_broadcast([P, KD, 2]),
                                                   ALU.add, ALU.mult)
                ins.then_inc(dve_step, 1)
                dve.wait_ge(*v.next(dve_step))

            def first_modulation(l):
                add_bias(l, "ada0", 0, 4)
                coefficients(l, ((cA, 8, R_MPRE, 1.0),))

            for l in range(DEPTH):
                def jb(n):
                    return JOB[l, n]
                rw, pc, q = row_l[l], par_l[l], query_tiles(l)
                nq, ns, t0, nsc = len(q), slots_of(l), q[0], len(scatter_parts(l))
                ctx_on = l < DEPTH - 1
                if l == 0:
                    parameters(0)
                    first_modulation(0)
                    dve.memset(dummy[0:1, 5:6], 0.0).then_inc(S["coef_ready"], 1)
                for t in range(0, NT, 2):
                    modulate(hT[:, :, t * P:(t + 1) * P], jb("h") + t, cA, mod3[:, 0:8, :],
                             1 if t < CT else 0).then_inc(S["h_ready"], 1)
                phase()

                for i in range(2):
                    c = B_LAM + 64 * i
                    ins = TT(lam[:, 32 * i:32 * i + 32], rw[:, c:c + 32], rw[:, c + 32:c + 64], ALU.mult)
                ins.then_inc(dve_step, 1)
                dve.wait_ge(*v.next(dve_step))
                dve.tensor_reduce(lam[:, 128:130], view(lam[:, 0:64], a=2), AX_X, ALU.add).then_inc(S["lam_dots"], 1)
                dve.wait_ge(*v.next(S["lam_exps"]))
                TT(lam[:, 134:135], lam[:, 133:134], lam[:, 132:133], ALU.subtract).then_inc(dve_step, 1)
                dve.wait_ge(*v.next(dve_step))
                dve.tensor_scalar(lam[:, 135:136], lam[:, 134:135], -LINIT[l], None, ALU.add).then_inc(dve_step, 1)
                dve.wait_ge(*v.next(dve_step))
                for m in range(4):
                    dve.wait_ge(*J.freed(jb("qk") + m))
                    lat = QK[:, m, CTX:TOK]
                    TT(rope_t[0], lat, kc(K_COS, SEQ), ALU.mult)
                    j = jb("rot") + m
                    dve.wait_ge(*J.filled(j))
                    TT(rope_t[1], J.tile(j)[:, 0:SEQ], kc(K_SIN, SEQ), ALU.mult).then_inc(*J.free(j))
                    dve.wait_ge(*J.freed(j))
                    TT(lat, rope_t[0], rope_t[1], ALU.add).then_inc(S["qk_roped"], 1)
                    dve.wait_ge(*v.next(S["qk_roped"]))

                def diff_weigh(u, nk):
                    c = 2 * (u % 2)
                    dve.reciprocal(rcol[:, c:c + 2], esum[:, c:c + 2]).then_inc(dve_step, 1)
                    dve.wait_ge(*v.next(dve_step))
                    dve.scalar_tensor_tensor(rcol[:, 8 + c:9 + c], esum[:, c:c + 1], lam[:, 135:136],
                                             rcol[:, c + 1:c + 2], ALU.mult, ALU.mult).then_inc(dve_step, 1)
                    dve.wait_ge(*v.next(dve_step))
                    p1, p2 = PD[u % 2]
                    dve.scalar_tensor_tensor(p1[:, 0:nk], p2[:, 0:nk], rcol[:, 8 + c:9 + c], p1[:, 0:nk],
                                             ALU.mult, ALU.add).then_inc(S["prob_ready"], 1)

                def diff_finish(u, h, t, j):
                    dve.tensor_scalar(matt[:, t, h * DV:(h + 1) * DV], J.tile(j)[:, 0:DV],
                                      rcol[:, 2 * (u % 2):2 * (u % 2) + 1], None, ALU.mult).then_inc(*J.free(j))

                attend(l, jb("datt"), 2, DH, diff_weigh, diff_finish)
                dve.wait_ge(*J.freed(att_job(jb("datt"), 2, DH * nq, DH * nq - 1, "value")))
                TT(view(osq[:, 0:nq * 256], t=nq), matt[:, t0:NT, 0:256], matt[:, t0:NT, 0:256], ALU.mult).then_inc(dve_step, 1)
                dve.wait_ge(*v.next(dve_step))
                dve.tensor_reduce(ssum[:, 4 * t0:4 * NT], osq[:, 0:nq * 256].rearrange("p (a n) -> p a n", n=DV),
                                  AX_X, ALU.add).then_inc(S["o_ss"], 1)
                dve.wait_ge(*v.next(S["o_rstd"]))
                for t in q:
                    o = matt[:, t, 0:256].rearrange("p (h n) -> p h n", h=DH)
                    TT(o, o, rstd[:, 4 * t:4 * t + 4].unsqueeze(2).to_broadcast([P, DH, DV]), ALU.mult)
                phase()

                for i in range(3):
                    dve.wait_ge(*J.freed(jb("mla") + i))
                TT(msq, MT[:, :, 0:MQL + MKL], MT[:, :, 0:MQL + MKL], ALU.mult).then_inc(dve_step, 1)
                dve.wait_ge(*v.next(dve_step))
                dve.tensor_reduce(ssum[:, 0:NT], msq[:, :, 0:MQL], AX_X, ALU.add)
                dve.tensor_reduce(ssum[:, 8:8 + NT], msq[:, :, MQL:MQL + MKL], AX_X, ALU.add).then_inc(S["lat_ss"], 1)
                dve.wait_ge(*v.next(S["lat_rstd"]))
                TT(MT[:, :, 0:MQL], MT[:, :, 0:MQL], rstd[:, 0:NT].unsqueeze(2).to_broadcast([P, NT, MQL]), ALU.mult)
                TT(MT[:, :, MQL:MQL + MKL], MT[:, :, MQL:MQL + MKL],
                   rstd[:, 8:8 + NT].unsqueeze(2).to_broadcast([P, NT, MKL]), ALU.mult).then_inc(S["lat_scaled"], 1)
                R = slice(MN, MQK)
                for h in range(MH + 1):
                    if h == 0:
                        dve.wait_ge(*J.freed(jb("mlaT") + 2))
                    else:
                        dve.wait_ge(*J.freed(jb("mq") + h - 1))
                    lat = KT[R, 0, CTX:TOK] if h == 0 else QT[R, h - 1, CTX:TOK]
                    j = jb("mrot") + h
                    dve.wait_ge(*J.filled(j))
                    TT(mrope_t[R, :], lat, K[R, K_COS:K_COS + SEQ], ALU.mult).then_inc(dve_step, 1)
                    dve.wait_ge(*v.next(dve_step))
                    TT(lat, J.tile(j)[R, 0:SEQ], K[R, K_SIN:K_SIN + SEQ], ALU.mult).then_inc(*J.free(j))
                    dve.wait_ge(*J.freed(j))
                    ins = TT(lat, lat, mrope_t[R, :], ALU.add)
                    ins.then_inc(S["kr_ready"] if h == 0 else S["q_roped"], 1)
                    dve.wait_ge(*v.next(S["kr_ready"] if h == 0 else S["q_roped"]))

                def mla_weigh(u, nk):
                    c = 2 * (u % 2)
                    dve.reciprocal(rcol[:, c:c + 1], esum[:, c:c + 1]).then_inc(S["prob_ready"], 1)

                def mla_finish(u, h, t, j):
                    dve.tensor_scalar(matt[:, t, 256 + h * MV:256 + (h + 1) * MV], J.tile(j)[:, 0:MV],
                                      rcol[:, 2 * (u % 2):2 * (u % 2) + 1], None, ALU.mult).then_inc(*J.free(j))

                attend(l, jb("matt"), 1, MH, mla_weigh, mla_finish)
                phase()

                for m in range(CONV_T):
                    j = jb("xbc") + m
                    dve.wait_ge(*v.next(S["conv_mid"]))
                    src, dst = J.tile(j), XB[:, m, :]
                    for tap, sh in ((0, -1), (2, 1)):
                        w = pc[:, R_CW + tap * CONV_T + m:R_CW + tap * CONV_T + m + 1]
                        for s0, s1 in ((0, CTX), (CTX, TOK)):
                            lo, hi = (s0 + 1, s1) if sh < 0 else (s0, s1 - 1)
                            ins = dve.scalar_tensor_tensor(dst[:, lo:hi], src[:, lo + sh:hi + sh], w, dst[:, lo:hi],
                                                           ALU.mult, ALU.add)
                        if sh < 0:
                            ins.then_inc(dve_step, 1)
                            dve.wait_ge(*v.next(dve_step))
                    ins.then_inc(*J.free(j))
                j = jb("dt")
                dve.wait_ge(*J.filled(j))
                TT(view(dts[0], t=NT), view(J.tile(j)[:, 0:96], t=NT),
                   rw[:, B_DTB:B_DTB + 16].unsqueeze(1).to_broadcast([P, NT, 16]), ALU.add).then_inc(*J.free(j))
                dve.wait_ge(*J.freed(j))
                dve.scalar_tensor_tensor(dts[1], dts[0], -1.0, dts[0], ALU.mult, ALU.min).then_inc(S["dt_neg"], 1)
                dve.wait_ge(*v.next(S["dt_exp"]))
                dve.tensor_scalar(dts[2], dts[1], 1.0, None, ALU.add).then_inc(S["dt_w"], 1)
                dve.wait_ge(*v.next(S["dt_ln"]))
                dve.tensor_scalar(dts[4], dts[2], 1.0, 1e-30, ALU.subtract, ALU.max).then_inc(dve_step, 1)
                dve.wait_ge(*v.next(dve_step))
                dve.reciprocal(dts[5], dts[4]).then_inc(dve_step, 1)
                dve.wait_ge(*v.next(dve_step))
                TT(dts[5], dts[5], dts[1], ALU.mult).then_inc(dve_step, 1)
                dve.wait_ge(*v.next(dve_step))
                TT(dts[3], dts[3], dts[5], ALU.mult).then_inc(dve_step, 1)
                dve.wait_ge(*v.next(dve_step))
                dve.tensor_scalar(dts[4], dts[2], 1.0, None, ALU.is_equal).then_inc(dve_step, 1)
                dve.wait_ge(*v.next(dve_step))
                TT(dts[4], dts[4], dts[1], ALU.mult).then_inc(dve_step, 1)
                dve.wait_ge(*v.next(dve_step))
                TT(dts[3], dts[3], dts[4], ALU.add).then_inc(dve_step, 1)
                dve.wait_ge(*v.next(dve_step))
                dve.scalar_tensor_tensor(DTV, dts[0], 0.0, dts[3], ALU.max, ALU.add).then_inc(dve_step, 1)
                dve.wait_ge(*v.next(dve_step))
                dve.wait_ge(*v.next(S["neg_a"]))
                dve.scalar_tensor_tensor(view(LA, t=NT), view(DTV, t=NT), -1.0,
                                         acol[:, 0:16].unsqueeze(1).to_broadcast([P, NT, 16]),
                                         ALU.mult, ALU.mult).then_inc(S["la_ready"], 1)
                j = jb("cum")
                dve.wait_ge(*J.filled(j))
                ac4 = AC.rearrange("p (t d n) -> p t d n", t=NT, d=2)
                for d in range(2):
                    dve.tensor_copy(ac4[:, :, d, :], view(J.tile(j)[:, 48 * d:48 * d + 48], t=NT))
                dve.tensor_copy(TOT, J.tile(j)[:, 96:192]).then_inc(*J.free(j))
                dve.wait_ge(*J.freed(j))
                TT(WJ, TOT, AC, ALU.subtract).then_inc(S["ac_ready"], 1)
                dve.wait_ge(*v.next(S["dec_exp"]))
                TT(WJ, WJ, DTV, ALU.mult).then_inc(S["w_ready"], 1)
                for t in range(NT):
                    dve.wait_ge(*J.freed(jb("xT") + t))
                dve.wait_ge(*J.filled(jb("z") + nq // 2 - 1))
                for t in q:
                    ins = TT(view(Y[:, t, :], h=SH), view(XT[:, t, 0:SI], h=SH),
                             rw[:, B_DSK:B_DSK + 8].unsqueeze(2).to_broadcast([P, SH, SP]), ALU.mult)
                ins.then_inc(dve_step, 1)
                dve.wait_ge(*v.next(dve_step))
                jobs = ssd_jobs(jb("ssd"), nq)

                def masked_products(i):
                    j = jobs["cb", i]
                    dve.wait_ge(*J.filled(j))
                    for d, mk in ((0, K_TRU), (1, K_TRL)):
                        ins = TT(CBM[d], view(J.tile(j)[:, :], g=SG)[:, :, 0:P],
                                 kc(mk).unsqueeze(1).to_broadcast([P, SG, P]), ALU.mult)
                    ins.then_inc(*J.free(j))
                    dve.wait_ge(*J.freed(j))

                def weigh(i):
                    dve.wait_ge(*J.freed(jobs["seg", i]))
                    for dst, cb in ((WF, CBM[0]), (EB, CBM[1])):
                        for g in range(SG):
                            hs = slice(g * HPG, (g + 1) * HPG)
                            ins = TT(dst[:, hs, :], EB[:, hs, :], cb[:, g, :].unsqueeze(1).to_broadcast([P, HPG, P]), ALU.mult)
                    ins.then_inc(S["mask_ready"], 1)
                    dve.wait_ge(*v.next(S["mask_ready"]))

                def add_product(i):
                    j = jobs["y", i]
                    dve.wait_ge(*J.filled(j))
                    TT(Y[:, q[i], :], Y[:, q[i], :], J.tile(j)[:, 0:SI], ALU.add).then_inc(*J.free(j))
                    dve.wait_ge(*J.freed(j))

                def recur(n):
                    d, c, t = chunks()[n]
                    j = jobs["rec", n]
                    dve.wait_ge(*J.filled(j))
                    if c and t in q:
                        ea = EA[:, t * 16 + 8 * d:t * 16 + 8 * d + 8].rearrange("p (g h) -> p g h", g=SG)
                        TT(ytmp.rearrange("p (g h n) -> p g h n", g=SG, h=HPG),
                           view(J.tile(j)[:, :], g=SG)[:, :, 0:256].rearrange("p g (h n) -> p g h n", h=HPG),
                           ea.unsqueeze(3).to_broadcast([P, SG, HPG, SP]), ALU.mult).then_inc(dve_step, 1)
                        dve.wait_ge(*v.next(dve_step))
                        TT(Y[:, t, :], Y[:, t, :], ytmp, ALU.add).then_inc(dve_step, 1)
                        dve.wait_ge(*v.next(dve_step))
                    if c:
                        for g in range(SG):
                            et = ET[g * SN:(g + 1) * SN, t * 16 + 8 * d + g * HPG:t * 16 + 8 * d + (g + 1) * HPG]
                            hv = view(HS[d][g * SN:(g + 1) * SN, :], h=HPG)
                            ins = TT(hv, hv, et.unsqueeze(2).to_broadcast([SN, HPG, SP]), ALU.mult)
                        ins.then_inc(dve_step, 1)
                        dve.wait_ge(*v.next(dve_step))
                        TT(HS[d], HS[d], J.tile(j)[:, 768:1024], ALU.add).then_inc(*J.free(j))
                        dve.wait_ge(*J.freed(j))
                    else:
                        dve.tensor_copy(HS[d], J.tile(j)[:, 768:1024]).then_inc(*J.free(j))
                        dve.wait_ge(*J.freed(j))

                masked_products(0)
                weigh(0)
                for i in range(NT):
                    if i + 1 < nq:
                        masked_products(i + 1)
                    if i < nq:
                        add_product(i)
                    if i + 1 < nq:
                        weigh(i + 1)
                    recur(2 * i)
                    recur(2 * i + 1)
                    for t in completed(i, q):
                        TT(Y[:, t, :], Y[:, t, :], ZS[:, t, :], ALU.mult).then_inc(S["gated"], 1)
                add_bias(l, "ada2", 4, 12)
                coefficients(l, ((cGm, 16, R_MPOST, 0.0), (cF, 32, R_FPRE, 1.0), (cGf, 40, R_FPOST, 0.0)))
                for s in range(2):
                    TT(diag[s], ident.unsqueeze(1).to_broadcast([P, KD, P]),
                       cGm[:, :, s].unsqueeze(2).to_broadcast([P, KD, P]), ALU.mult).then_inc(S["diag_ready"], 1)
                dve.wait_ge(*v.next(S["g_rstd"]))
                for t in q[:nq // 2]:
                    y3 = view(Y[:, t, :], g=SG)
                    TT(y3, y3, rstd[:, 2 * t:2 * t + 2].unsqueeze(2).to_broadcast([P, SG, SI // SG]), ALU.mult)
                phase()

                for i in range(nq + 1):
                    if i < nq:
                        j = two_job(jb("out"), nq, i, False)
                        dve.wait_ge(*J.filled(j))
                        if i >= 2:
                            dve.wait_ge(*J.filled(two_job(jb("out"), nq, i - 2, True)))
                        TT(mixT[i % 2], view(J.tile(j)[:, :], k=KD),
                           fac[:, 0:8].unsqueeze(2).to_broadcast([P, KD, P]), ALU.mult).then_inc(*J.free(j))
                    if i >= 1:
                        t = q[i - 1]
                        j = two_job(jb("out"), nq, i - 1, True)
                        dve.wait_ge(*J.filled(j))
                        dve.wait_ge(*v.next(S["m_rstd"]))
                        dve.wait_ge(*J.freed(jb("gm") + (1 if t < CT else 0)))
                        dve.scalar_tensor_tensor(rn2, J.tile(j)[:, :], rstd[:, t:t + 1], GB[1 if t < CT else 0],
                                                 ALU.mult, ALU.mult).then_inc(*J.free(j))
                        dve.wait_ge(*J.freed(j))
                        TT(Xt(t), Xt(t), rn2, ALU.add).then_inc(S["x_ready"], 1)
                        dve.wait_ge(*v.next(S["x_ready"]))

                def logits(i):
                    j = router_job(jb("f"), nq, i, True)
                    dve.wait_ge(*J.filled(j))
                    TT(aff[:, q[i] * NE:(q[i] + 1) * NE], J.tile(j)[:, 0:NE], rw[:, B_RB:B_RB + NE], ALU.add).then_inc(*J.free(j))

                for i, t in enumerate(q):
                    if i % 2 == 0:
                        if i >= 4:
                            dve.wait_ge(*J.filled(router_job(jb("f"), nq, i - 4, True)))
                        modulate(fhT[i % 4], router_job(jb("f"), nq, i, False), cF, mod3[:, 24:32, :],
                                 1 if t < CT else 0).then_inc(S["h_ready"], 1)
                    if i:
                        logits(i - 1)
                logits(nq - 1)
                for i in range(nq):
                    dve.wait_ge(*J.freed(router_job(jb("f"), nq, i, True)))
                lg, e3 = (x[:, t0 * NE:NT * NE].rearrange("p (t n) -> p t n", n=NE) for x in (aff, ex))
                if t0:
                    dve.memset(ex[:, 0:t0 * NE], 0.0)
                dve.tensor_reduce(ssum[:, 32:32 + nq], lg, AX_X, ALU.max).then_inc(dve_step, 1)
                dve.wait_ge(*v.next(dve_step))
                TT(e3, lg, ssum[:, 32:32 + nq].unsqueeze(2).to_broadcast([P, nq, NE]), ALU.subtract)\
                    .then_inc(S["router_max"], 1)
                dve.wait_ge(*v.next(S["router_exp"]))
                dve.tensor_reduce(ssum[:, 40:40 + nq], e3, AX_X, ALU.add).then_inc(dve_step, 1)
                dve.wait_ge(*v.next(dve_step))
                dve.reciprocal(ssum[:, 48:48 + nq], ssum[:, 40:40 + nq]).then_inc(dve_step, 1)
                dve.wait_ge(*v.next(dve_step))
                TT(e3, e3, ssum[:, 48:48 + nq].unsqueeze(2).to_broadcast([P, nq, NE]), ALU.mult)\
                    .then_inc(S["aff_ready"], 1)
                j = jb("aT")
                dve.wait_ge(*J.filled(j))
                dve.tensor_copy(aT[0][0:NE, t0 * P:TOK], J.tile(j)[0:NE, t0 * P:TOK]).then_inc(*J.free(j))
                dve.wait_ge(*J.freed(j))
                idi = idu.bitcast(U32)
                for s0, s1, c0, cap in ((CTX, TOK, 0, CAP_L), (0, CTX, CAP_L, CAP_C)):
                    if s0 < t0 * P:
                        continue
                    for r in range(cap // 8):
                        c = c0 + 8 * r
                        src = aT[r % 2][0:NE, s0:s1]
                        dve.max(gv[0:NE, c:c + 8], src).then_inc(dve_step, 1)
                        dve.wait_ge(*v.next(dve_step))
                        dve.max_index(idi[0:NE, c:c + 8], gv[0:NE, c:c + 8], src)
                        dve.match_replace(aT[1 - r % 2][0:NE, s0:s1], gv[0:NE, c:c + 8], src, -1.0).then_inc(dve_step, 1)
                        dve.wait_ge(*v.next(dve_step))
                    dve.tensor_copy(idf[0:NE, c0:c0 + cap], idi[0:NE, c0:c0 + cap]).then_inc(dve_step, 1)
                    dve.wait_ge(*v.next(dve_step))
                    if s0:
                        dve.tensor_scalar(idf[0:NE, c0:c0 + cap], idf[0:NE, c0:c0 + cap], float(s0), None, ALU.add).then_inc(dve_step, 1)
                        dve.wait_ge(*v.next(dve_step))
                for i in range(2):
                    es = slice(i * NE // 2, (i + 1) * NE // 2)
                    TT(bd[0:NE, 0:NE * ns].rearrange("p (e n) -> p e n", e=NE)[:, es, :],
                       idf[0:NE, 0:ns].unsqueeze(1).to_broadcast([NE, NE // 2, ns]),
                       K[0:NE, K_ID:K_ID + NE][:, es].unsqueeze(2).to_broadcast([NE, NE // 2, ns]),
                       ALU.mult).then_inc(S["bd_ready"], 1)
                for i, (src, c0, n) in enumerate(((idf, 0, CAP_L), (gv, 0, CAP_L), (idf, CAP_L, CAP_C),
                                                  (gv, CAP_L, CAP_C))[:4 if ctx_on else 2]):
                    ins = dve.tensor_copy(slotr[0:NE, i * P:(i + 1) * P].rearrange("p (a n) -> p a n", n=n),
                                          src[0:NE, c0:c0 + n].unsqueeze(1).to_broadcast([NE, P // n, n]))
                ins.then_inc(S["topk_ready"], 1)
                j = jb("idx") + 2
                dve.wait_ge(*J.filled(j))
                nc4 = 4 if ctx_on else 2
                for p in range(2):
                    r = slice(p * 64, p * 64 + 64)
                    ins = dve.tensor_copy(slotc[r, 0:nc4, :], J.tile(j)[r, 0:nc4 * NE]
                                          .rearrange("p (c e two) -> p c e two", c=nc4, two=2)[:, :, :, p])
                ins.then_inc(*J.free(j))
                phase()

                parts = ((0, 0, 0, CAP_L, 0, CT, NT), (1, 512, CAP_L, CAP_C, 256, 0, CT))[:2 if ctx_on else 1]

                def select(e):
                    for s, c, at, n, sc_, ta, tb in parts:
                        src = idxB[:, e * ns + at:e * ns + at + n] if isinstance(e, int) else idxB[:, bass.ds(e * ns + at, n)]
                        ins = TT(view(Sel[:, sc_:sc_ + (tb - ta) * n], t=tb - ta),
                                 src.unsqueeze(1).to_broadcast([P, tb - ta, n]),
                                 K[:, K_TID + ta:K_TID + tb].unsqueeze(2).to_broadcast([P, tb - ta, n]), ALU.is_equal)
                    ins.then_inc(S["sel_ready"], 1)

                def scatter_mask(i):
                    for c, k0, k1 in ((0, CTX, TOK), (2, 0, CTX))[:2 if ctx_on else 1]:
                        tok_, gate_ = (slotc[:, c + a, i:i + 1] if isinstance(i, int) else slotc[:, c + a, bass.ds(i, 1)]
                                       for a in range(2))
                        ins = dve.tensor_scalar(Sc[:, k0:k1], K[:, K_IOTA + k0:K_IOTA + k1], tok_, gate_,
                                                ALU.is_equal, ALU.mult)
                    ins.then_inc(S["scat_ready"], 1)

                def gathered(j, turn):
                    dve.wait_ge(*J.filled(j, turn))
                    for s, c, at, n, sc_, ta, tb in parts:
                        ins = TT(halves(xg[:, c:c + 8 * n], n), halves(J.tile(j)[:, c:c + 8 * n], n),
                                 cF[:, :, s].rearrange("p (h c) -> p c h", h=2).unsqueeze(3).to_broadcast([P, 4, 2, n]),
                                 ALU.mult)
                    ins.then_inc(*J.free(j))
                    dve.wait_ge(*J.freed(j, turn))
                    for s, c, at, n, sc_, ta, tb in parts:
                        x4 = halves(xg[:, c:c + 8 * n], n)
                        ins = TT(x4, x4, mod3[:, 24:32, s].rearrange("p (h c) -> p c h", h=2).unsqueeze(3)
                                 .to_broadcast([P, 4, 2, n]), ALU.add)
                    ins.then_inc(S["xg_ready"], 1)

                def scattered(j, turn):
                    for k, (t, c0, c1) in enumerate(scatter_parts(l)):
                        dve.wait_ge(*J.filled(j + k, turn))
                        TT(Fa[:, t, c0:c1], Fa[:, t, c0:c1], J.tile(j + k)[:, c0:c1], ALU.add).then_inc(*J.free(j + k))

                def pair(i, last=False):
                    first = isinstance(i, int) and i == 0
                    o, turn, end = pair_jobs(jb("moe"), nsc, i, last)
                    for p in range(2):
                        if not (last and p):
                            select(i * 2 + p + 1)
                        if p:
                            scatter_mask(i)
                        u = J.tile(o[p]["up"])
                        dve.wait_ge(*J.filled(o[p]["up"], turn))
                        dve.wait_ge(*J.freed(o[p]["gate"], turn))
                        ins = TT(hid, sg, u[:, 0:512], ALU.mult)
                        if ctx_on:
                            ins = dve.tensor_copy(cu, u[:, 512:1024])
                        ins.then_inc(*J.free(o[p]["up"]))
                        if ctx_on:
                            n_silu = i * 2 + (l * NE + p + 1)
                            dve.wait_ge(S["silu_turned"], n_silu)
                            TT(hidT[:, 512:768], sgT, J.tile(o[p]["hidT"])[:, 768:1024], ALU.mult).then_inc(*J.free(o[p]["hidT"]))
                        if not (last and p):
                            gathered(o[p]["takeT"], turn)
                        if not first and p == 0:
                            scattered(o[p]["scatter"], turn)
                    return end, turn

                select(0)
                gathered(jb("moe") + 1, 0)
                pair(0)
                dve.wait_ge(*v.next(S["sum_zero"]))
                with dve.Fori(1, NE // 2 - 1) as i:
                    pair(i)
                end, turn = pair(NE // 2 - 1, last=True)
                dve.wait_ge(*J.filled(end - 1, turn))
                for s in range(2):
                    TT(diagf[s], ident.unsqueeze(1).to_broadcast([P, KD, P]),
                       cGf[:, :, s].unsqueeze(2).to_broadcast([P, KD, P]), ALU.mult).then_inc(S["diag_ready"], 1)
                scattered(end, turn)
                phase()

                if l + 1 < DEPTH:
                    dve.wait_ge(s_late, 16 * N_LATE)
                    parameters(l + 1)
                for s in range(2):
                    dve.wait_ge(*J.freed(jb("gf") + s))
                dve.wait_ge(*v.next(S["m_rstd"]))
                for t in q:
                    dve.scalar_tensor_tensor(Fa[:, t, :], Fa[:, t, :], rstd[:, t:t + 1], GBf[1 if t < CT else 0],
                                             ALU.mult, ALU.mult).then_inc(dve_step, 1)
                    dve.wait_ge(*v.next(dve_step))
                    TT(Xt(t), Xt(t), Fa[:, t, :], ALU.add).then_inc(S["x_ready"] if l + 1 < DEPTH else S["out_ready"], 1)
                if l + 1 < DEPTH:
                    dve.wait_ge(*v.next(S["x_ready"], nq))
                    first_modulation(l + 1)
                phase()

        @block.tensor
        def _(pe):
            w_ = Tally()
            pe.wait_ge(s_load, 16 * N_FIRST)
            mm = pe.matmul

            def phase(n):
                for s in (dve_ph, act_ph, pool_ph):
                    pe.wait_ge(*w_.next(s, n))

            def arrived(j, turn=0):
                pe.wait_ge(ring_full[j % RING], turn + (j // RING + 1) * 16)
                return ringv(j)

            def feature_major(j, w, col, n, t0=0, late=None):
                pe.wait_ge(*J.empty(j))
                o = J.tile(j)
                for c0, c1 in ((t0 * P, 512), (512, TOK)):
                    if late and c0 == 512:
                        late()
                    for k in range(KD):
                        ins = mm(o[0:n, c0:c1], w[:, k, col:col + n], hT[:, k, c0:c1], start=k == 0, stop=k == KD - 1)
                ins.then_inc(*J.fill(j))

            def token_major(j, w, tiles, n, stride):
                pe.wait_ge(*J.empty(j))
                o = J.tile(j)
                for i, t in enumerate(tiles):
                    for k in range(KD):
                        ins = mm(o[:, i * stride:i * stride + n], hT[:, k, t * P:(t + 1) * P], w[:, k, :],
                                 start=k == 0, stop=k == KD - 1)
                ins.then_inc(*J.fill(j))

            def turn_tile(j, src, n=KD):
                pe.wait_ge(*J.empty(j))
                o = J.tile(j)
                for k in range(n):
                    ins = pe.transpose(o[:, k * P:(k + 1) * P], src(k), ident)
                ins.then_inc(*J.fill(j))

            def attention(l, heads, base, maps, score, P_of, PT_of, v_of):
                units = [(h, t) for h in range(heads) for t in query_tiles(l)]
                n = len(units)

                def scores(u):
                    h, t = units[u]
                    for m in range(maps):
                        j = att_job(base, maps, n, u, "score", m)
                        pe.wait_ge(*J.empty(j))
                        o = J.tile(j)
                        for c0, c1 in spans(t):
                            lhs, rhs = score(h, m, t, c0, c1)
                            ins = mm(o[:, c0:c1], lhs, rhs, start=True, stop=True)
                        ins.then_inc(*J.fill(j))

                def values(u):
                    h, t = units[u]
                    pe.wait_ge(*J.freed(att_job(base, maps, n, u, "turn")))
                    j = att_job(base, maps, n, u, "value")
                    pe.wait_ge(*J.empty(j))
                    o = J.tile(j)
                    nk = n_keys(t) // P
                    for k in range(nk):
                        ins = mm(o[:, 0:64], PT_of[u % 2][:, k * P:(k + 1) * P], v_of(h, k), start=k == 0, stop=k == nk - 1)
                    ins.then_inc(*J.fill(j))

                scores(0)
                for u in range(n):
                    if u + 1 < n:
                        scores(u + 1)
                    pe.wait_ge(*w_.next(S["prob_ready"]))
                    turn_tile(att_job(base, maps, n, u, "turn"), lambda k: P_of[u % 2][0][:, k * P:(k + 1) * P],
                              n_keys(units[u][1]) // P)
                    if u:
                        values(u - 1)
                values(n - 1)

            def modulation(l, part, blk):
                sc3 = view(sc[:, :], k=KD)
                for b in range(5):
                    j = JOB[l, f"ada{part}"] + b
                    if b < 4:
                        pe.wait_ge(*J.empty(j))
                        o = J.tile(j)
                        w = arrived(blk + b)
                        for k in range(KD):
                            r = 32 * (k % 4)
                            ins = mm(o[r:r + 32, 0:BLK], sc3[:, k, :], w[:, k, :], start=k < 4, stop=k >= 4)
                        ins.then_inc(half_used, 1)
                    if b >= 1:
                        pe.wait_ge(*w_.next(S["mod_rows"]))
                        o = J.tile(j - 1)
                        for c in range(4):
                            ins = mm(o[:, BLK + 2 * c:BLK + 2 * c + 2], mrow[(b - 1) % 2][:, c * P:(c + 1) * P],
                                     kc(K_TWO, 2), start=True, stop=True)
                        ins.then_inc(*J.fill(j - 1))

            def gate_rows(j, dg):
                pe.wait_ge(*w_.next(S["diag_ready"]))
                pe.wait_ge(*J.empty(j))
                o = J.tile(j)
                for hf in range(2):
                    ins = mm(o[:, hf * 512:(hf + 1) * 512], ones, dg[:, 4 * hf:4 * hf + 4, :].rearrange("p k n -> p (k n)"),
                             start=True, stop=True)
                ins.then_inc(*J.fill(j))

            def conditioning(l):
                j = JOB[l, "par"]
                pe.wait_ge(*J.empty(j))
                pe.transpose(J.tile(j)[:, 0:P], pack[:, l * P:(l + 1) * P], ident).then_inc(*J.fill(j))
                pe.wait_ge(*w_.next(S["silu_ready"]))
                modulation(l, 0, l * LAYER_BLOCKS)

            for l in range(DEPTH):
                def jb(n):
                    return JOB[l, n]
                wb, q = l * LAYER_BLOCKS, query_tiles(l)
                nq, ns, t0, nsc = len(q), slots_of(l), q[0], len(scatter_parts(l))
                ctx_on = l < DEPTH - 1
                if l == 0:
                    conditioning(0)
                for t in range(NT):
                    pe.wait_ge(*w_.next(S["xn_ready"]))
                    turn_tile(jb("h") + t, lambda k: xn[t % 2][:, k * P:(k + 1) * P])
                pe.wait_ge(*w_.next(S["h_ready"], 2))
                pe.wait_ge(*J.freed(jb("h") + 1))
                pe.wait_ge(*J.freed(jb("h") + 3))

                def last_tiles():
                    pe.wait_ge(*w_.next(S["h_ready"]))
                    pe.wait_ge(*J.freed(jb("h") + 5))


                w = arrived(wb + 4)
                for m in range(4):
                    feature_major(jb("qk") + m, w, m * P, P, t0 if m < 2 else 0, last_tiles if m == 0 else None)
                for m in range(4):
                    j = jb("rot") + m
                    pe.wait_ge(*J.freed(jb("qk") + m))
                    pe.wait_ge(*J.empty(j))
                    o = J.tile(j)
                    mm(o[:, 0:SEQ], kc(K_ROT), QK[:, m, CTX:TOK], start=True, stop=True).then_inc(*J.fill(j))
                w = arrived(wb + 5)
                token_major(jb("v"), w[:, :, 0:256], range(0, 4), 256, 256)
                token_major(jb("v") + 1, w[:, :, 0:256], range(4, 6), 256, 256)
                pe.wait_ge(*w_.next(S["qk_roped"], 4))
                pe.wait_ge(*J.freed(jb("v")))
                pe.wait_ge(*J.freed(jb("v") + 1))

                def diff_score(h, m, t, c0, c1):
                    if t == q[0] and c0 == 0:
                        pe.wait_ge(*w_.next(S["q_split"]))
                    return QS[:, 2 * (h % 2) + m, t * P:(t + 1) * P], QK[:, 2 + h // 2, c0:c1]

                attention(l, DH, jb("datt"), 2, diff_score, PD, PT_d, lambda h, k: V[:, k, h * DV:(h + 1) * DV])

                w = arrived(wb + 6)
                for i in range(3):
                    token_major(jb("mla") + i, w[:, :, 0:MLA_COLS], (2 * i, 2 * i + 1), MLA_COLS, 512)
                modulation(l, 1, wb + 7)
                if l == 0:
                    pe.wait_ge(s_late, 16 * N_LATE)
                pe.wait_ge(*w_.next(S["lat_scaled"]))
                for i in range(3):
                    j = jb("mlaT") + i
                    pe.wait_ge(*J.empty(j))
                    o = J.tile(j)
                    for b in range(2):
                        m_ = MT[:, 2 * i + b, :]
                        for s, (c0, n) in enumerate(((0, P), (P, MQL - P), (MQL, P), (MLA_COLS - MQK, MQK))):
                            c = 512 * b + P * s
                            ins = pe.transpose(o[0:n, c:c + P], m_[:, c0:c0 + n], ident)
                    ins.then_inc(*J.fill(j))
                for i in range(3):
                    pe.wait_ge(*J.freed(jb("mlaT") + i))
                wq = wqu[:, l * 2 * MH * MQK:(l + 1) * 2 * MH * MQK]
                wk = wkv[:, l * 512:(l + 1) * 512]
                for h in range(MH):
                    j = jb("mq") + h
                    pe.wait_ge(*J.empty(j))
                    o = J.tile(j)
                    for c0, c1 in ((t0 * P, 512), (512, TOK)):
                        mm(o[0:MQK, c0:c1], wq[:, h * MQK:(h + 1) * MQK], cq0[:, c0:c1], start=True, stop=False)
                        ins = mm(o[0:MQK, c0:c1], wq[0:MQL - P, (MH + h) * MQK:(MH + h + 1) * MQK], cq1[0:MQL - P, c0:c1],
                                 start=False, stop=True)
                    ins.then_inc(*J.fill(j))
                R = slice(MN, MQK)
                for h in range(MH + 1):
                    j = jb("mrot") + h
                    if h:
                        pe.wait_ge(*J.freed(jb("mq") + h - 1))
                    pe.wait_ge(*J.empty(j))
                    o = J.tile(j)
                    src = KT[R, 0, CTX:TOK] if h == 0 else QT[R, h - 1, CTX:TOK]
                    mm(o[R, 0:SEQ], K[R, K_ROT + MN:K_ROT + MQK], src, start=True, stop=True).then_inc(*J.fill(j))
                for h in range(MH):
                    j = jb("mk") + h
                    pe.wait_ge(*J.empty(j))
                    o = J.tile(j)
                    for c0, c1 in spans(NT):
                        ins = mm(o[0:MN, c0:c1], wk[:, h * P:h * P + MN], ckv[:, c0:c1], start=True, stop=True)
                    ins.then_inc(*J.fill(j))
                for i, tiles in enumerate((range(0, 4), range(4, 6))):
                    j = jb("mv") + i
                    pe.wait_ge(*J.empty(j))
                    o = J.tile(j)
                    for n, t in enumerate(tiles):
                        ins = mm(o[:, n * 256:(n + 1) * 256], ckv[:, t * P:(t + 1) * P],
                                 wk.rearrange("p (h n) -> p h n", h=MH)[:, :, MN:P], start=True, stop=True)
                    ins.then_inc(*J.fill(j))
                pe.wait_ge(*w_.next(S["q_roped"], MH))
                pe.wait_ge(*w_.next(S["kr_all"], MH - 1))
                for h in range(MH):
                    pe.wait_ge(*J.freed(jb("mk") + h))
                for i in range(2):
                    pe.wait_ge(*J.freed(jb("mv") + i))
                attention(l, MH, jb("matt"), 1,
                          lambda h, m, t, c0, c1: (QT[0:MQK, h, t * P:(t + 1) * P], KT[0:MQK, h, c0:c1]),
                          PM, PT_m, lambda h, k: VM[:, k, h * MV:(h + 1) * MV])

                modulation(l, 2, wb + 11)
                w = arrived(wb + 15)
                for m in range(4):
                    feature_major(jb("xbc") + m, w, m * P, P)
                w = arrived(wb + 16)
                for m in range(4, 6):
                    feature_major(jb("xbc") + m, w, (m - 4) * P, P)
                token_major(jb("dt"), w[:, :, 256:272], range(NT), 16, 16)
                w = arrived(wb + 17)
                for i in range(nq // 2):
                    token_major(jb("z") + i, w, q[2 * i:2 * i + 2], 512, 512)
                pe.wait_ge(*w_.next(S["la_ready"]))
                j = jb("cum")
                pe.wait_ge(*J.empty(j))
                o = J.tile(j)
                la3 = LA.rearrange("p (t d n) -> p t d n", t=NT, d=2)
                mm(o[:, 0:48], kc(K_TRU), la3[:, :, 0, :], start=True, stop=True)
                mm(o[:, 48:96], kc(K_TRL), la3[:, :, 1, :], start=True, stop=True)
                mm(o[:, 96:192], ones, LA, start=True, stop=True).then_inc(*J.fill(j))
                pe.wait_ge(*w_.next(S["xbc_ready"], CONV_T))
                for t in range(NT):
                    turn_tile(jb("xT") + t, lambda k: XB[:, k, t * P:(t + 1) * P], 5)
                BT, CTr = XB[:, 4, :], XB[:, 5, :]

                jobs = ssd_jobs(jb("ssd"), nq)

                def chunk_inner(i):
                    t = q[i]
                    j = jobs["cb", i]
                    pe.wait_ge(*J.empty(j))
                    o = J.tile(j)
                    for g in range(SG):
                        r = slice(g * SN, (g + 1) * SN)
                        ins = mm(o[:, g * 512:g * 512 + P], BT[r, t * P:(t + 1) * P], CTr[r, t * P:(t + 1) * P],
                                 start=True, stop=True)
                    ins.then_inc(*J.fill(j))
                    j = jobs["seg", i]
                    pe.wait_ge(*w_.next(S["lf_ready"]))
                    pe.wait_ge(*w_.next(S["lb_ready"]))
                    pe.wait_ge(*J.empty(j))
                    o = J.tile(j)
                    for h in range(SH):
                        mm(o[:, h * P:(h + 1) * P], LM[0][:, h, :], kc(K_TRU), start=True, stop=False)
                        ins = mm(o[:, h * P:(h + 1) * P], LM[1][:, h, :], kc(K_TRL), start=False, stop=True)
                    ins.then_inc(*J.fill(j))

                def chunk_product(i):
                    pe.wait_ge(*w_.next(S["mask_ready"]))
                    pe.wait_ge(*w_.next(S["xdt_ready"], 2))
                    j = jobs["y", i]
                    pe.wait_ge(*J.empty(j))
                    o = J.tile(j)
                    for h in range(SH):
                        hs = slice(h * SP, (h + 1) * SP)
                        mm(o[:, hs], WF[:, h, :], xdt[0][:, hs], start=True, stop=False)
                        ins = mm(o[:, hs], EB[:, h, :], xdt[1][:, hs], start=False, stop=True)
                    ins.then_inc(*J.fill(j))

                def recur(n):
                    d, c, t = chunks()[n]
                    j = jobs["rec", n]
                    pe.wait_ge(*J.empty(j))
                    o = J.tile(j)
                    if c and t in q:
                        pe.wait_ge(*J.freed(jobs["rec", n - 2]))
                        for g in range(SG):
                            r = slice(g * SN, (g + 1) * SN)
                            mm(o[:, g * 512:g * 512 + 256], CTr[r, t * P:(t + 1) * P], HS[d][r, :], start=True, stop=True)
                    pe.wait_ge(*w_.next(S["xw_ready"]))
                    for g in range(SG):
                        ins = mm(o[g * SN:(g + 1) * SN, 768:1024], XT[:, t, SI + g * SN:SI + (g + 1) * SN],
                                 XW[n % 2][:, g * 256:(g + 1) * 256], start=True, stop=True)
                    ins.then_inc(*J.fill(j))

                chunk_inner(0)
                for i in range(NT):
                    if i + 1 < nq:
                        chunk_inner(i + 1)
                    if i < nq:
                        chunk_product(i)
                    recur(2 * i)
                    recur(2 * i + 1)

                for s in range(2):
                    gate_rows(jb("gm") + s, diag[s])
                phase(4 if l == 0 else 7)
                wo = [arrived(wb + 18), arrived(wb + 19)]

                def mixed(i):
                    turn_tile(two_job(jb("out"), nq, i, False),
                              lambda k: Y[:, q[i], k * P:(k + 1) * P] if k < 4 else matt[:, q[i], (k - 4) * P:(k - 3) * P])

                mixed(0)
                for i in range(nq):
                    if i + 1 < nq:
                        mixed(i + 1)
                    pe.wait_ge(*J.freed(two_job(jb("out"), nq, i, False)))
                    j = two_job(jb("out"), nq, i, True)
                    pe.wait_ge(*J.empty(j))
                    o = J.tile(j)
                    for hf in range(2):
                        for k in range(KD):
                            ins = mm(o[:, hf * 512:(hf + 1) * 512], mixT[i % 2][:, k, :], wo[hf][:, k, :], start=k == 0,
                                     stop=k == KD - 1)
                    ins.then_inc(*J.fill(j))

                def latents_turned(i):
                    pe.wait_ge(*w_.next(S["xn_ready"]))
                    turn_tile(router_job(jb("f"), nq, i, False), lambda k: htok[:, q[i], k * P:(k + 1) * P])

                wr = view(wrt[:, l * KD * NE:(l + 1) * KD * NE], k=KD)
                latents_turned(0)
                latents_turned(1)
                for i in range(nq):
                    if i + 2 < nq:
                        latents_turned(i + 2)
                    if i % 2:
                        pe.wait_ge(*J.freed(router_job(jb("f"), nq, i, False)))
                    else:
                        pe.wait_ge(*w_.next(S["h_ready"]))
                    j = router_job(jb("f"), nq, i, True)
                    pe.wait_ge(*J.empty(j))
                    o = J.tile(j)
                    for k in range(KD):
                        ins = mm(o[:, 0:NE], fhT[i % 4][:, k, :], wr[:, k, :], start=k == 0, stop=k == KD - 1)
                    ins.then_inc(*J.fill(j))
                pe.wait_ge(*w_.next(S["aff_ready"]))
                j = jb("aT")
                pe.wait_ge(*J.empty(j))
                o = J.tile(j)
                for t in q:
                    ins = pe.transpose(o[0:NE, t * P:(t + 1) * P], ex[:, t * NE:(t + 1) * NE], ident)
                ins.then_inc(*J.fill(j))
                wd = NE * ns // 2
                for i in range(2):
                    pe.wait_ge(*w_.next(S["bd_ready"]))
                    j = jb("idx") + i
                    pe.wait_ge(*J.empty(j))
                    o = J.tile(j)
                    for c0, c1 in ((0, 512), (512, wd)):
                        if c0 < c1:
                            ins = mm(o[:, c0:c1], K[0:NE, K_ONE:K_ONE + P], bd[0:NE, i * wd + c0:i * wd + c1],
                                     start=True, stop=True)
                    ins.then_inc(*J.fill(j))
                pe.wait_ge(*w_.next(S["topk_ready"]))
                j = jb("idx") + 2
                pe.wait_ge(*J.empty(j))
                o = J.tile(j)
                for i in range(4 if ctx_on else 2):
                    ins = pe.transpose(o[:, i * NE:(i + 1) * NE], slotr[0:NE, i * P:(i + 1) * P], K[0:NE, K_ID:K_ID + NE])
                ins.then_inc(*J.fill(j))

                def take(j, turn, e):
                    pe.wait_ge(S["sel_ready"], e + (l * NE + 1))
                    pe.wait_ge(*J.empty(j, turn))
                    o = J.tile(j)
                    for t in range(CT, NT):
                        for hf in range(2):
                            ins = mm(o[hf * 64:hf * 64 + 64, 0:512], Sel[:, (t - CT) * CAP_L:(t - CT + 1) * CAP_L],
                                     htok[:, t, hf * 512:hf * 512 + 512], start=t == CT, stop=t == NT - 1)
                    if ctx_on:
                        for hf in range(2):
                            for t in range(CT):
                                r = 32 * (2 * hf + t)
                                ins = mm(o[r:r + 32, 512:1024], Sel[:, 256 + t * CAP_C:256 + (t + 1) * CAP_C],
                                         htok[:, t, hf * 512:hf * 512 + 512], start=True, stop=True)
                    ins.then_inc(*J.fill(j))

                def rows_turned(o, col, src, c):
                    for k in range(4):
                        ins = pe.transpose(o[:, col + k * P:col + (k + 1) * P], src[:, c + k * P:c + (k + 1) * P], ident)
                    return ins

                def rows_summed(o, col, src, c):
                    for k in range(4):
                        ins = mm(o[:, col + k * 64:col + (k + 1) * 64], src[:, c + k * P:c + (k + 1) * P], kc(K_SUM, 64),
                                 start=True, stop=True)
                    return ins

                def take_turned(j, turn):
                    pe.wait_ge(*J.freed(j["take"], turn))
                    pe.wait_ge(*J.empty(j["takeT"], turn))
                    o = J.tile(j["takeT"])
                    ins = rows_turned(o, 0, taken, 0)
                    if ctx_on:
                        ins = rows_summed(o, 512, taken, 512)
                    ins.then_inc(*J.fill(j["takeT"]))

                def project(j, turn, blk, b_turn, rows):
                    pe.wait_ge(*J.empty(j, turn))
                    o = J.tile(j)
                    for b in range(2):
                        arrived(blk + b, b_turn)
                        w = ringk(blk + b)
                        for c in range(4):
                            for hf in range(2):
                                at = c * P + b * CAP_L
                                ins = mm(o[hf * 64:hf * 64 + 64, 0:512], rows[:, at:at + CAP_L],
                                         w[:, c, hf * 512:hf * 512 + 512], start=b + c == 0, stop=b * c == 3)
                        for c in range(4 if ctx_on else 0):
                            for hf in range(2):
                                at = 512 + c * 64 + b * CAP_C
                                r = 32 * (2 * hf + c % 2)
                                ins = mm(o[r:r + 32, 512:1024], rows[:, at:at + CAP_C], w[:, c, hf * 512:hf * 512 + 512],
                                         start=b + c // 2 == 0, stop=b * (c // 2) == 1)
                        if b == 0:
                            ins.then_inc(half_used, 1)
                    ins.then_inc(*J.fill(j))

                def hidden_turned(j, turn):
                    pe.wait_ge(*J.freed(j["up"], turn))
                    pe.wait_ge(*J.empty(j["hidT"], turn))
                    o = J.tile(j["hidT"])
                    ins = rows_turned(o, 0, hid, 0)
                    if ctx_on:
                        rows_summed(o, 512, cg, 0)
                        ins = rows_summed(o, 768, cu, 0)
                    ins.then_inc(*J.fill(j["hidT"]))

                def scatter(j, turn, i):
                    pe.wait_ge(S["scat_ready"], i + (l * NE // 2 + 1))
                    for k, (t, c0, c1) in enumerate(scatter_parts(l)):
                        pe.wait_ge(*J.empty(j + k, turn))
                        o = J.tile(j + k)
                        for c in range(c0, c1, 512):
                            ins = mm(o[:, c:c + 512], Sc[:, t * P:(t + 1) * P], yb[:, 1 if t < CT else 0, c:c + 512],
                                     start=True, stop=True)
                        ins.then_inc(*J.fill(j + k))

                def pair(i, last=False):
                    first = isinstance(i, int) and i == 0
                    o, turn, end = pair_jobs(jb("moe"), nsc, i, last)
                    if not first:
                        before, turn_b, _ = pair_jobs(jb("moe"), nsc, i - 1)
                    for p in range(2):
                        e, blk = i * 2 + p, wb + 20 + 6 * p
                        pe.wait_ge(S["xg_ready"], e + (l * NE + 1))
                        project(o[p]["gate"], turn, blk, i * 48, xg)
                        project(o[p]["up"], turn, blk + 2, i * 48, xg)
                        if not (last and p):
                            take(o[p]["take"], turn, e + 1)
                        hidden_turned(o[p], turn)
                        if not (last and p):
                            take_turned(o[p], turn)
                        if not first and p == 0:
                            pe.wait_ge(*J.freed(before[1]["down"], turn_b))
                            scatter(o[p]["scatter"], turn, i - 1)
                        pe.wait_ge(*J.freed(o[p]["hidT"], turn))
                        project(o[p]["down"], turn, blk + 4, i * 48, hidT)
                    return o, end, turn

                take(jb("moe"), 0, 0)
                take_turned({"take": jb("moe"), "takeT": jb("moe") + 1}, 0)
                pair(0)
                pair(1)
                with pe.Fori(2, NE // 2 - 1) as i:
                    pair(i)
                o, end, turn = pair(NE // 2 - 1, last=True)
                pe.wait_ge(*J.freed(o[1]["down"], turn))
                scatter(end, turn, NE // 2 - 1)
                for s in range(2):
                    gate_rows(jb("gf") + s, diagf[s])
                if l + 1 < DEPTH:
                    conditioning(l + 1)


_NAMES = ['x', 'c', 'ctx', 'c_ctx', 'ada_w', 'ada_b', 'norm_mix_pre', 'norm_mix_post', 'norm_ffn_pre',
          'norm_ffn_post', 'w_in', 'ssd_conv_w', 'ssd_conv_b', 'ssd_a_log', 'ssd_dt_bias', 'ssd_d', 'ssd_norm',
          'diff_lam_q1', 'diff_lam_k1', 'diff_lam_q2', 'diff_lam_k2', 'diff_subln', 'mla_q_norm', 'mla_w_q_up',
          'mla_kv_norm', 'mla_w_kv_up', 'w_out', 'router_w', 'router_b', 'w_gate', 'w_up', 'w_down']


def kernel(**inputs):
    import concourse.bacc as bacc
    from concourse.bass_utils import run_bass_kernel_spmd

    nc = bacc.Bacc("TRN2", target_bir_lowering=False, num_devices=1)
    arrays, T = {}, {}
    for name in _NAMES:
        arrays["in_" + name] = np.ascontiguousarray(inputs[name])
    arrays["in_const"] = constants()
    for name in _NAMES + ["const"]:
        T[name] = nc.dram_tensor("in_" + name, arrays["in_" + name].shape, F32, kind="ExternalInput").ap()
    out = nc.dram_tensor("out", (1, SEQ, D), F32, kind="ExternalOutput").ap()
    build(nc, T, out)
    r = run_bass_kernel_spmd(nc, [arrays], core_ids=[0])
    return r.results[0]["out"]
```
